# Optimizing a Trainium2 kernel written in Bass

```python
import jax, jax.numpy as jnp
from jax import lax
import numpy as np

D_MODEL = 1024
BATCH = 1
SEQ = 512
DEPTH = 1

CHUNK = 64
POOL_WIDTH = 1024
POOL_WINDOWS = (2, 4, 8, 16)
POOL_GROUPS = len(POOL_WINDOWS)
POOL_GROUP_WIDTH = POOL_WIDTH // POOL_GROUPS
HGRN_WIDTH = 1024
HGRN_EXPAND = 128
HGRN_HEADS = HGRN_WIDTH // HGRN_EXPAND
HGRN_HEAD_V = HGRN_WIDTH // HGRN_HEADS
MIX_WIDTH = POOL_WIDTH + HGRN_WIDTH
IN_WIDTH = 2 * POOL_WIDTH + 4 * HGRN_WIDTH
EPS = 1e-6


def rms_norm(x, w):
    xf = x.astype(jnp.float32)
    xf = xf * lax.rsqrt(jnp.mean(xf * xf, axis=-1, keepdims=True) + EPS)
    return xf * w.astype(jnp.float32)

def multiscale_pool(u, pool_w, pool_scale):
    B, S, _ = u.shape
    cs = jnp.cumsum(u, axis=1)
    count = jnp.arange(1, S + 1, dtype=jnp.float32)[None, :, None]
    outs = []
    for g, w in enumerate(POOL_WINDOWS):
        lo, hi = g * POOL_GROUP_WIDTH, (g + 1) * POOL_GROUP_WIDTH
        cs_g = cs[..., lo:hi]
        prev = jnp.pad(cs_g, ((0, 0), (w, 0), (0, 0)))[:, :S]
        mean = (cs_g - prev) / jnp.minimum(count, float(w))
        outs.append(mean - u[..., lo:hi])
    d = jnp.stack(outs, axis=2)
    y = jnp.einsum('bsgc,gcd->bsgd', d, pool_w.astype(jnp.float32))
    return y.reshape(B, S, POOL_WIDTH) * pool_scale.astype(jnp.float32)

def _to_chunks(t):
    B, S, H, D = t.shape
    return t.reshape(B, S // CHUNK, CHUNK, H, D).transpose(1, 0, 3, 2, 4)

def hgrn2_chunkwise(q, log_f, k, v):
    B, S, H, dk = q.shape
    dv = v.shape[-1]
    causal = jnp.tril(jnp.ones((CHUNK, CHUNK), dtype=bool))[:, :, None]

    def step(state, xs):
        qc, lfc, kc, vc = xs
        b = jnp.cumsum(lfc, axis=2)
        o_inter = jnp.einsum('bhtk,bhkv->bhtv', qc * jnp.exp(b), state)
        diff = b[:, :, :, None, :] - b[:, :, None, :, :]
        decay = jnp.exp(jnp.where(causal, diff, -jnp.inf))
        attn = jnp.einsum('bhtk,bhsk,bhtsk->bhts', qc, kc, decay)
        o_intra = jnp.einsum('bhts,bhsv->bhtv', attn, vc)
        b_last = b[:, :, -1, :]
        k_dec = kc * jnp.exp(b_last[:, :, None, :] - b)
        new_state = jnp.exp(b_last)[..., None] * state + jnp.einsum('bhsk,bhsv->bhkv', k_dec, vc)
        return new_state, o_inter + o_intra

    state0 = jnp.zeros((B, H, dk, dv), jnp.float32)
    _, o = lax.scan(step, state0, (_to_chunks(q), _to_chunks(log_f), _to_chunks(k), _to_chunks(v)))
    return o.transpose(1, 0, 3, 2, 4).reshape(B, S, H, dv)

def first_inputs(seed: int = 0) -> dict:
    key = jax.random.key(seed)
    ks = jax.random.split(key, 12)
    f32 = jnp.float32
    x = jax.random.normal(ks[0], (BATCH, SEQ, D_MODEL), f32)
    c = jax.random.normal(ks[1], (BATCH, D_MODEL), f32)
    norm_pre_w = 1.0 + 0.05 * jax.random.normal(ks[2], (DEPTH, D_MODEL), f32)
    ada_w = 0.5 * D_MODEL ** -0.5 * jax.random.normal(ks[3], (DEPTH, D_MODEL, 3 * D_MODEL), f32)
    ada_b = 0.01 * jax.random.normal(ks[4], (DEPTH, 3 * D_MODEL), f32)
    w_in = D_MODEL ** -0.5 * jax.random.normal(ks[5], (DEPTH, D_MODEL, IN_WIDTH), f32)
    pool_w = POOL_GROUP_WIDTH ** -0.5 * jax.random.normal(
        ks[6], (DEPTH, POOL_GROUPS, POOL_GROUP_WIDTH, POOL_GROUP_WIDTH), f32)
    pool_scale = 1.0 + 0.05 * jax.random.normal(ks[7], (DEPTH, POOL_WIDTH), f32)
    hgrn_lower_bounds = 0.5 * jax.random.normal(ks[8], (DEPTH, HGRN_WIDTH), f32)
    hgrn_norm_w = 1.0 + 0.05 * jax.random.normal(ks[9], (DEPTH, HGRN_HEAD_V), f32)
    w_out = MIX_WIDTH ** -0.5 * jax.random.normal(ks[10], (DEPTH, MIX_WIDTH, D_MODEL), f32)
    norm_post_w = 1.0 + 0.05 * jax.random.normal(ks[11], (DEPTH, D_MODEL), f32)
    return {"x": x, "c": c, "norm_pre_w": norm_pre_w, "ada_w": ada_w, "ada_b": ada_b,
            "w_in": w_in, "pool_w": pool_w, "pool_scale": pool_scale,
            "hgrn_lower_bounds": hgrn_lower_bounds, "hgrn_norm_w": hgrn_norm_w,
            "w_out": w_out, "norm_post_w": norm_post_w}

def first_block(x, c, norm_pre_w, ada_w, ada_b, w_in, pool_w, pool_scale,
              hgrn_lower_bounds, hgrn_norm_w, w_out, norm_post_w):
    B, S, D = x.shape
    f32 = jnp.float32
    lb_sm = jax.nn.softmax(hgrn_lower_bounds.astype(f32), axis=0)
    lower_bounds = jnp.cumsum(lb_sm, axis=0) - lb_sm[0]
    silu_c = jax.nn.silu(c.astype(f32))
    h_res = x.astype(f32)
    for l in range(DEPTH):
        mod = silu_c @ ada_w[l].astype(f32) + ada_b[l].astype(f32)
        shift, scale, gate = jnp.split(mod[:, None, :], 3, axis=-1)
        h = rms_norm(h_res, norm_pre_w[l]) * (1.0 + scale) + shift
        z = h @ w_in[l].astype(f32)
        u_pool, g_pool, q, f_pre, i_in, g_h = jnp.split(
            z, np.cumsum([POOL_WIDTH, POOL_WIDTH, HGRN_WIDTH, HGRN_WIDTH, HGRN_WIDTH]), axis=-1)
        pool_out = multiscale_pool(u_pool, pool_w[l], pool_scale[l]) * jax.nn.silu(g_pool)
        lb = lower_bounds[l]
        f = lb + (1.0 - lb) * jax.nn.sigmoid(f_pre)
        log_f = jnp.log(f)
        k = 1.0 - f
        heads = lambda t, d: t.reshape(B, S, HGRN_HEADS, d)
        o = hgrn2_chunkwise(heads(q, HGRN_EXPAND), heads(log_f, HGRN_EXPAND),
                            heads(k, HGRN_EXPAND), heads(i_in, HGRN_HEAD_V))
        o = rms_norm(o, hgrn_norm_w[l]) * jax.nn.silu(heads(g_h, HGRN_HEAD_V))
        hgrn_out = o.reshape(B, S, HGRN_WIDTH)
        y = jnp.concatenate([pool_out, hgrn_out], axis=-1) @ w_out[l].astype(f32)
        h_res = h_res + gate * rms_norm(y, norm_post_w[l])
    return h_res.astype(x.dtype)


GRID_W = 64
CTX_LEN = 256
D_MIX = D_MODEL
C_CONV = D_MIX // 2
CONV_K = 31
N_HEADS = 8
QK_NOPE = 64
QK_ROPE = 32
V_DIM = 64
Q_LORA = 384
KV_LORA = 256
D_FF = 2816
FFN_K = 3
Q_BLOCK = 128
ROPE_THETA = 10000.0
LN_EPS = 1e-5
ALPHA = (2 * DEPTH) ** 0.25
BETA = (8 * DEPTH) ** -0.25
D_IN = 2 * C_CONV + Q_LORA + KV_LORA + QK_ROPE
SOFTMAX_SCALE = (QK_NOPE + QK_ROPE) ** -0.5


def layer_norm(x, g=None, b=None):
    xf = x.astype(jnp.float32)
    mu = xf.mean(-1, keepdims=True)
    var = jnp.square(xf - mu).mean(-1, keepdims=True)
    y = (xf - mu) * lax.rsqrt(var + LN_EPS)
    if g is not None:
        y = y * g.astype(jnp.float32) + b.astype(jnp.float32)
    return y.astype(x.dtype)

def rms_norm_2(x, g):
    xf = x.astype(jnp.float32)
    y = xf * lax.rsqrt(jnp.square(xf).mean(-1, keepdims=True) + LN_EPS) * g.astype(jnp.float32)
    return y.astype(x.dtype)

def dwconv(x, w, b):
    k = w.shape[0]
    y = lax.conv_general_dilated(x, w[:, None, :], window_strides=(1,),
                                 padding=[(k // 2, k // 2)],
                                 dimension_numbers=('NWC', 'WIO', 'NWC'),
                                 feature_group_count=x.shape[-1])
    return y + b

def axial_rope_tables(n, dtype):
    rows = n // GRID_W
    row = jnp.repeat(jnp.arange(rows), GRID_W)
    col = jnp.tile(jnp.arange(GRID_W), rows)
    n_freq = QK_ROPE // 4
    inv = ROPE_THETA ** (-jnp.arange(n_freq, dtype=jnp.float32) / n_freq)
    ang = jnp.concatenate([row[:, None] * inv, col[:, None] * inv], axis=-1)
    return jnp.cos(ang).astype(dtype), jnp.sin(ang).astype(dtype)

def apply_rope(x, cos, sin):
    half = x.shape[-1] // 2
    x1, x2 = x[..., :half], x[..., half:]
    return jnp.concatenate([x1 * cos - x2 * sin, x2 * cos + x1 * sin], axis=-1)

def mixer_inputs(h, w_in):
    z = h @ w_in
    return jnp.split(z, [2 * C_CONV, 2 * C_CONV + Q_LORA, 2 * C_CONV + Q_LORA + KV_LORA], axis=-1)

def conformer_conv(u, dw_w, dw_b, ln_g, ln_b):
    a, gte = jnp.split(u, 2, axis=-1)
    v = a * jax.nn.sigmoid(gte)
    v = dwconv(v, dw_w, dw_b)
    return jax.nn.silu(layer_norm(v, ln_g, ln_b))

def mla_queries(cq, q_norm_g, w_uq, cos, sin):
    b, n = cq.shape[:2]
    q = (rms_norm_2(cq, q_norm_g) @ w_uq).reshape(b, n, N_HEADS, QK_NOPE + QK_ROPE)
    q_nope, q_rope = q[..., :QK_NOPE], q[..., QK_NOPE:]
    if cos is not None:
        q_rope = apply_rope(q_rope, cos[:, None, :], sin[:, None, :])
    return q_nope, q_rope

def mla_keys_values(ckv, kr, kv_norm_g, w_ukv, cos, sin):
    b, n = ckv.shape[:2]
    kv = (rms_norm_2(ckv, kv_norm_g) @ w_ukv).reshape(b, n, N_HEADS, QK_NOPE + V_DIM)
    k_nope, v = kv[..., :QK_NOPE], kv[..., QK_NOPE:]
    k_rope = kr if cos is None else apply_rope(kr, cos, sin)
    return k_nope, k_rope, v

def attend(q_nope, q_rope, k_nope, k_rope, v):
    s = (jnp.einsum('bqhd,bkhd->bhqk', q_nope, k_nope)
         + jnp.einsum('bqhr,bkr->bhqk', q_rope, k_rope)).astype(jnp.float32) * SOFTMAX_SCALE
    p = jax.nn.softmax(s, axis=-1).astype(v.dtype)
    return jnp.einsum('bhqk,bkhd->bqhd', p, v)

def attend_blocked(q_nope, q_rope, k_nope, k_rope, v):
    b, n = q_nope.shape[:2]
    nb = n // Q_BLOCK
    qn = q_nope.reshape(b, nb, Q_BLOCK, N_HEADS, QK_NOPE).transpose(1, 0, 2, 3, 4)
    qr = q_rope.reshape(b, nb, Q_BLOCK, N_HEADS, QK_ROPE).transpose(1, 0, 2, 3, 4)
    out = lax.map(lambda qs: attend(qs[0], qs[1], k_nope, k_rope, v), (qn, qr))
    return out.transpose(1, 0, 2, 3, 4).reshape(b, n, N_HEADS, V_DIM)

def merge_groups(conv_out, attn_out, w_o, b_o):
    b, n = conv_out.shape[:2]
    cat = jnp.concatenate([conv_out, attn_out.reshape(b, n, N_HEADS * V_DIM)], axis=-1)
    return cat @ w_o + b_o

def conv_ffn(h, w_up, dw_w, dw_b, w_down, b_down):
    u = dwconv(h @ w_up, dw_w, dw_b)
    g, val = jnp.split(u, 2, axis=-1)
    return (jax.nn.silu(g) * val) @ w_down + b_down

def second_inputs(seed: int = 0) -> dict:
    key = jax.random.key(seed)
    ks = jax.random.split(key, 32)
    L = DEPTH

    def nrm(k, shape, s):
        return s * jax.random.normal(k, shape, jnp.float32)

    return {
        'x': nrm(ks[0], (BATCH, SEQ, D_MODEL), 1.0),
        'c': nrm(ks[1], (BATCH, D_MODEL), 1.0),
        'ctx': nrm(ks[2], (BATCH, CTX_LEN, D_MODEL), 1.0),
        'c_ctx': nrm(ks[3], (D_MODEL,), 1.0),
        'w_ada': nrm(ks[4], (L, D_MODEL, 6 * D_MODEL), D_MODEL ** -0.5),
        'b_ada': nrm(ks[5], (L, 6 * D_MODEL), 0.02),
        'w_in': nrm(ks[6], (L, D_MODEL, D_IN), D_MODEL ** -0.5),
        'conv_dw_w': nrm(ks[7], (L, CONV_K, C_CONV), CONV_K ** -0.5),
        'conv_dw_b': nrm(ks[8], (L, C_CONV), 0.02),
        'conv_ln_g': 1.0 + nrm(ks[9], (L, C_CONV), 0.05),
        'conv_ln_b': nrm(ks[10], (L, C_CONV), 0.02),
        'q_norm_g': 1.0 + nrm(ks[11], (L, Q_LORA), 0.05),
        'w_uq': nrm(ks[12], (L, Q_LORA, N_HEADS * (QK_NOPE + QK_ROPE)), Q_LORA ** -0.5),
        'kv_norm_g': 1.0 + nrm(ks[13], (L, KV_LORA), 0.05),
        'w_ukv': nrm(ks[14], (L, KV_LORA, N_HEADS * (QK_NOPE + V_DIM)), KV_LORA ** -0.5),
        'w_o': nrm(ks[15], (L, D_MIX, D_MODEL), BETA * D_MIX ** -0.5),
        'b_o': nrm(ks[16], (L, D_MODEL), 0.02),
        'ln1_g': 1.0 + nrm(ks[17], (L, D_MODEL), 0.05),
        'ln1_b': nrm(ks[18], (L, D_MODEL), 0.02),
        'w_up': nrm(ks[19], (L, D_MODEL, 2 * D_FF), D_MODEL ** -0.5),
        'ffn_dw_w': nrm(ks[20], (L, FFN_K, 2 * D_FF), FFN_K ** -0.5),
        'ffn_dw_b': nrm(ks[21], (L, 2 * D_FF), 0.02),
        'w_down': nrm(ks[22], (L, D_FF, D_MODEL), BETA * D_FF ** -0.5),
        'b_down': nrm(ks[23], (L, D_MODEL), 0.02),
        'ln2_g': 1.0 + nrm(ks[24], (L, D_MODEL), 0.05),
        'ln2_b': nrm(ks[25], (L, D_MODEL), 0.02),
    }

def second_block(x, c, ctx, c_ctx, w_ada, b_ada, w_in, conv_dw_w, conv_dw_b, conv_ln_g, conv_ln_b,
              q_norm_g, w_uq, kv_norm_g, w_ukv, w_o, b_o, ln1_g, ln1_b,
              w_up, ffn_dw_w, ffn_dw_b, w_down, b_down, ln2_g, ln2_b):
    n = x.shape[1]
    cos, sin = axial_rope_tables(n, x.dtype)
    x = layer_norm(x)
    ctx = layer_norm(ctx)
    for i in range(DEPTH):
        last = i == DEPTH - 1
        mod = jax.nn.silu(c) @ w_ada[i] + b_ada[i]
        sh1, sc1, g1, sh2, sc2, g2 = jnp.split(mod[:, None, :], 6, axis=-1)
        modc = jax.nn.silu(c_ctx) @ w_ada[i] + b_ada[i]
        sh1c, sc1c, g1c, sh2c, sc2c, g2c = jnp.split(modc, 6)

        u_c, cq_c, ckv_c, kr_c = mixer_inputs(ctx * (1 + sc1c) + sh1c, w_in[i])
        k_nope_c, k_rope_c, v_c = mla_keys_values(ckv_c, kr_c, kv_norm_g[i], w_ukv[i], None, None)

        u_l, cq_l, ckv_l, kr_l = mixer_inputs(x * (1 + sc1) + sh1, w_in[i])
        k_nope_l, k_rope_l, v_l = mla_keys_values(ckv_l, kr_l, kv_norm_g[i], w_ukv[i], cos, sin)
        q_nope_l, q_rope_l = mla_queries(cq_l, q_norm_g[i], w_uq[i], cos, sin)
        attn_l = attend_blocked(q_nope_l, q_rope_l,
                                jnp.concatenate([k_nope_c, k_nope_l], axis=1),
                                jnp.concatenate([k_rope_c, k_rope_l], axis=1),
                                jnp.concatenate([v_c, v_l], axis=1))
        conv_l = conformer_conv(u_l, conv_dw_w[i], conv_dw_b[i], conv_ln_g[i], conv_ln_b[i])
        y_l = merge_groups(conv_l, attn_l, w_o[i], b_o[i])
        x_mid = layer_norm(ALPHA * x + g1 * y_l, ln1_g[i], ln1_b[i])

        if not last:
            q_nope_c, q_rope_c = mla_queries(cq_c, q_norm_g[i], w_uq[i], None, None)
            attn_c = attend(q_nope_c, q_rope_c, k_nope_c, k_rope_c, v_c)
            conv_c = conformer_conv(u_c, conv_dw_w[i], conv_dw_b[i], conv_ln_g[i], conv_ln_b[i])
            y_c = merge_groups(conv_c, attn_c, w_o[i], b_o[i])
            ctx = layer_norm(ALPHA * ctx + g1c * y_c, ln1_g[i], ln1_b[i])
            f_c = conv_ffn(ctx * (1 + sc2c) + sh2c, w_up[i], ffn_dw_w[i], ffn_dw_b[i], w_down[i], b_down[i])
            ctx = layer_norm(ALPHA * ctx + g2c * f_c, ln2_g[i], ln2_b[i])

        f_l = conv_ffn(x_mid * (1 + sc2) + sh2, w_up[i], ffn_dw_w[i], ffn_dw_b[i], w_down[i], b_down[i])
        x = layer_norm(ALPHA * x_mid + g2 * f_l, ln2_g[i], ln2_b[i])
    return x


def setup_inputs(seed=0):
    out = dict(first_inputs(seed))
    for name, value in second_inputs(seed + 1).items():
        if name != "x":
            out[name + "_2"] = value
    return out


def reference(
    x, c, norm_pre_w, ada_w, ada_b, w_in, pool_w, pool_scale, hgrn_lower_bounds, hgrn_norm_w,
    w_out, norm_post_w, c_2, ctx_2, c_ctx_2, w_ada_2, b_ada_2, w_in_2, conv_dw_w_2, conv_dw_b_2,
    conv_ln_g_2, conv_ln_b_2, q_norm_g_2, w_uq_2, kv_norm_g_2, w_ukv_2, w_o_2, b_o_2, ln1_g_2,
    ln1_b_2, w_up_2, ffn_dw_w_2, ffn_dw_b_2, w_down_2, b_down_2, ln2_g_2, ln2_b_2,
):
    x = first_block(
        x, c, norm_pre_w, ada_w, ada_b, w_in, pool_w, pool_scale, hgrn_lower_bounds,
        hgrn_norm_w, w_out, norm_post_w,
    )
    return second_block(
        x, c_2, ctx_2, c_ctx_2, w_ada_2, b_ada_2, w_in_2, conv_dw_w_2, conv_dw_b_2, conv_ln_g_2,
        conv_ln_b_2, q_norm_g_2, w_uq_2, kv_norm_g_2, w_ukv_2, w_o_2, b_o_2, ln1_g_2, ln1_b_2,
        w_up_2, ffn_dw_w_2, ffn_dw_b_2, w_down_2, b_down_2, ln2_g_2, ln2_b_2,
    )


_drawn_inputs = setup_inputs


def setup_inputs(seed=0):
    import zlib

    import numpy as np

    out = dict(_drawn_inputs(seed))
    spreads = {}
    factors = {'ada_b': 4.357,
     'pool_scale': 5.366,
     'hgrn_norm_w': 4.186,
     'norm_post_w': 3.524,
     'ctx_2': 7.958,
     'b_ada_2': 3.485,
     'conv_dw_b_2': 8.0,
     'conv_ln_g_2': 7.4,
     'conv_ln_b_2': 40.026,
     'q_norm_g_2': 8.0,
     'kv_norm_g_2': 8.0,
     'b_o_2': 5.389,
     'ln1_b_2': 2.683,
     'ffn_dw_b_2': 8.0,
     'b_down_2': 5.698,
     'ln2_b_2': 2.823}
    for name, (base, spread) in spreads.items():
        noise = np.random.default_rng([zlib.crc32(name.encode()), seed]).standard_normal(out[name].shape)
        drawn = base * np.exp(spread * noise) if base else spread * noise
        out[name] = __import__('jax').numpy.asarray(drawn.astype(out[name].dtype))
    for name, factor in factors.items():
        out[name] = (out[name] * factor).astype(out[name].dtype)
    return out
```

```python
import numpy as np
from contextlib import ExitStack
import concourse.bass as bass
from concourse import mybir

F32 = mybir.dt.float32
F32R = mybir.dt.float32r
U8 = mybir.dt.uint8
ALU = mybir.AluOpType
ACTF = mybir.ActivationFunctionType
AX = mybir.AxisListType
MUL, ADD, SUB = ALU.mult, ALU.add, ALU.subtract

S = 512
D = 1024
EPS1 = 1e-6
EPS2 = 1e-5
ALPHA = 2 ** 0.25
SCALE = 96 ** -0.5
NCTX = 256
NKEY = NCTX + S

PARAMS = [
    [("c", 8), ("norm_pre_w", 8), ("ada_b", 24), ("pool_scale", 8), ("hgrn_lower_bounds", 8),
     ("hgrn_norm_w", 1), ("norm_post_w", 8), ("c_2", 8), ("c_ctx_2", 8), ("conv_dw_b_2", 4),
     ("conv_ln_g_2", 4), ("conv_ln_b_2", 4), ("q_norm_g_2", 3), ("kv_norm_g_2", 2), ("b_o_2", 8),
     ("ln1_g_2", 8), ("ln1_b_2", 8)],
    [("b_ada_2", 48), ("ffn_dw_b_2", 44), ("b_down_2", 8), ("ln2_g_2", 8), ("ln2_b_2", 8)],
    [("conv_dw_w_2", 124)],
    [("ffn_dw_w_2a", 88)],
    [("ffn_dw_w_2b", 44)],
]


class Tok:

    def __init__(self, eng, i):
        self.eng, self.i = eng, i


class DTok:

    def __init__(self, sem, val):
        self.sem, self.val = sem, val


def flat(ws):
    out = []
    for w in ws:
        if w is None:
            continue
        if isinstance(w, (list, tuple)):
            out += flat(w)
        else:
            out.append(w)
    return out


class Prog:

    ENG = ("pe", "act", "dve", "pool", "sp")

    def __init__(self, sems):
        self.sems = sems
        self.q = {e: [] for e in self.ENG}
        self.dcount = {}

    def op(self, eng, fn, *ws):
        self.q[eng].append([flat(ws), fn, False])
        return Tok(eng, len(self.q[eng]) - 1)

    def dma(self, eng, out, in_, sem, *ws):
        n = self.dcount.get(id(sem), 0) + 16
        self.dcount[id(sem)] = n
        self.q[eng].append([flat(ws), lambda e: e.dma_start(out, in_).then_inc(sem, 16), None])
        return DTok(sem, n)

    def number(self):
        for e in self.ENG:
            for ws, _, _ in self.q[e]:
                for w in ws:
                    if isinstance(w, Tok):
                        self.q[w.eng][w.i][2] = True
        self.val = {}
        for e in self.ENG:
            n, vals = 0, []
            for it in self.q[e]:
                n += it[2] is True
                vals.append(n)
            self.val[e] = vals

    def emit(self, name, e):
        seen = {}
        for ws, fn, inc in self.q[name]:
            for w in ws:
                if isinstance(w, Tok):
                    sem, v = self.sems[w.eng], self.val[w.eng][w.i]
                else:
                    sem, v = w.sem, w.val
                if seen.get(id(sem), 0) < v:
                    e.wait_ge(sem, v)
                    seen[id(sem)] = v
            if fn is None:
                continue
            ins = fn(e)
            if inc:
                ins.then_inc(self.sems[name], 1)


class Ring:

    def __init__(self, bufs):
        self.bufs, self.n = bufs, 0
        self.free = [[] for _ in bufs]

    def take(self):
        i = self.n % len(self.bufs)
        self.n += 1
        f, self.free[i] = self.free[i], None
        assert f is not None
        return i, self.bufs[i], f

    def even(self):
        self.n += self.n % 2

    def give(self, i, *toks):
        self.free[i] = flat(toks)


def build(nc, A, out, consts, masks, stop=None):
    ctx = ExitStack()
    with ctx:
        def sb(name, shape, dt=F32, c=ctx):
            return c.enter_context(nc.sbuf_tensor(name, shape, dt))

        sems = {e: ctx.enter_context(nc.semaphore("s_" + e)) for e in Prog.ENG}
        P = Prog(sems)
        s_par = ctx.enter_context(nc.semaphore("s_par"))
        s_con = ctx.enter_context(nc.semaphore("s_con"))
        s_msk = ctx.enter_context(nc.semaphore("s_msk"))
        s_out = ctx.enter_context(nc.semaphore("s_out"))
        NRAW = 3
        s_raw = [ctx.enter_context(nc.semaphore(f"s_raw{i}")) for i in range(NRAW)]

        def T(fn, *w):
            return P.op("pe", fn, *w)

        def C(fn, *w):
            return P.op("act", fn, *w)

        def V(fn, *w):
            return P.op("dve", fn, *w)

        def G(fn, *w):
            return P.op("pool", fn, *w)

        def mm(o, l, r, st, sp, *w, skip=False):
            return T(lambda e: e.matmul(o, l, r, start=st, stop=sp, skip_group_check=skip), *w)

        def tr(o, i, idn, *w):
            return T(lambda e: e.transpose(o, i, idn), *w)

        def act(o, i, f, *w, bias=0.0, scale=1.0, acc=None):
            if acc is not None:
                return C(lambda e: e.activation(o, i, f, bias=bias, scale=scale, accum_out=acc), *w)
            if f == ACTF.Copy:
                return C(lambda e: e.activation(o, i, f), *w)
            return C(lambda e: e.activation(o, i, f, bias=bias, scale=scale), *w)

        def tt(q, o, a, b, op, *w):
            return q(lambda e: e.tensor_tensor(o, a, b, op), *w)

        def ts(q, o, a, s1, s2, o1, o2, *w):
            if s2 is None:
                return q(lambda e: e.tensor_scalar(o, a, s1, None, o1), *w)
            return q(lambda e: e.tensor_scalar(o, a, s1, s2, o1, o2), *w)

        def stt(o, a, s, b, o1, o2, *w):
            return V(lambda e: e.scalar_tensor_tensor(out=o, in0=a, scalar=s, in1=b, op0=o1, op1=o2), *w)

        def cp(q, o, i, *w):
            return q(lambda e: e.tensor_copy(o, i), *w)

        IDN = sb("IDN", [128, 128])
        ONES = sb("ONES", [128, 128])
        NPOW = sb("NPOW", [128, 8])
        PC = sb("PC", [128, 5, 128])
        PX = sb("PX", [128, 208])
        SCT = sb("SCT", [128, 64])
        RAW = [sb(f"RAW{i}", [128, 2048]) for i in range(NRAW)]
        WH = [sb(f"WH{i}", [128, 2048], F32R) for i in range(2)]
        WL = [sb(f"WL{i}", [128, 2048], F32R) for i in range(2)]
        XL = sb("XL", [128, 8, S])
        DG = sb("DG", [128, 512])
        PB = [ctx.enter_context(nc.psum_tensor(f"PB{i}", [128, 1024], F32)) for i in range(4)]
        bank = [PB[i // 2][:, (i % 2) * 512:(i % 2) * 512 + 512] for i in range(8)]

        COL = {}
        for t, rows in enumerate(PARAMS):
            r = 0
            for name, n in rows:
                COL[name] = (t, r)
                r += n
            assert r <= 128

        def col(name, j=0, n=1):
            t, r = COL[name]
            return PC[:, t, r + j:r + j + n]

        npx = [0]

        def newcols(n):
            a = npx[0]
            npx[0] += n
            assert npx[0] <= 208
            return PX[:, a:a + n]

        c_dma = P.dma("act", IDN[:, :], consts[:, 0:128], s_con)
        on_t = G(lambda e: e.memset(ONES[:, :], 1.0))
        np_t = G(lambda e: e.memset(NPOW[:, :], -0.5))

        mainr = Ring(bank[0:4])
        auxr = Ring(bank[4:8])

        items = []

        def wsrc(ap, r0, nk, c0, nc_):
            return ap[r0 * 128:(r0 + nk) * 128, c0:c0 + nc_].rearrange("(k p) n -> p k n", p=128)

        def item_w(loads, pieces=None, n=2048):
            items.append(dict(kind="w", loads=loads, pieces=pieces, n=n))

        def rv(raw, nk, ncol, c0=0):
            return raw[:, 0:nk * ncol].rearrange("p (k n) -> p k n", n=ncol)

        def unit(ap, r0, nk, colsets):
            tot = sum(n for _, n in colsets)
            loads, at = [], 0
            for c0, n in colsets:
                loads.append((lambda raw, at=at, n=n: rv(raw, nk, tot)[:, :, at:at + n], wsrc(ap, r0, nk, c0, n)))
                at += n
            item_w(loads, None, nk * tot)

        class Stream:
            def __init__(s):
                s.nd = s.np = s.nw = s.ready = 0
                s.rfree = [[] for _ in range(NRAW)]
                s.tok = {}
                s.wfree = [[], []]
                s.wready = {}

            def fetch(s):
                while s.nd < len(items) and s.nd < s.np + NRAW:
                    i = s.nd % NRAW
                    for dst, src in items[s.nd]["loads"]:
                        s.tok[s.nd] = P.dma("sp", dst(RAW[i]), src, s_raw[i], s.rfree[i])
                    s.nd += 1

            def process(s):
                s.fetch()
                it = items[s.np]
                i = s.np % NRAW
                raw, tok = RAW[i], s.tok[s.np]
                if it["kind"] == "w":
                    h = s.nw % 2
                    free = s.wfree[h]
                    s.wfree[h] = None
                    assert free is not None
                    pieces = it["pieces"] or [(lambda r, n=it["n"]: r[:, 0:n], lambda w, n=it["n"]: w[:, 0:n])]
                    a_t, v_t = [], []
                    for src, dst in pieces:
                        a_t.append(act(dst(WH[h]), src(raw), ACTF.Copy, tok, free))
                    for (src, dst), a in zip(pieces, a_t):
                        v_t.append(tt(V, dst(WL[h]), src(raw), dst(WH[h]).bitcast(F32), SUB, a, free))
                    s.wready[s.nw] = [a_t[-1], v_t[-1]]
                    s.rfree[i] = [a_t[-1], v_t[-1]]
                    s.nw += 1
                else:
                    s.rfree[i] = flat([it["proc"](raw, tok)])
                s.np += 1
                s.fetch()

            def next(s):
                n = s.ready
                s.ready += 1
                while s.nw < n + 2 and s.np < len(items) and items[s.np]["kind"] in "wa":
                    s.process()
                return n % 2, WH[n % 2], WL[n % 2], s.wready[n]

            def done(s, h, tok):
                s.wfree[h] = [tok]

            def flush_until(s, kind):
                while s.np < len(items) and items[s.np]["kind"] == kind:
                    s.process()

        st = Stream()

        def mm3(o, lh, ll, rh, rl, first, last, *w, skip=False):
            mm(o, lh, rh, first, False, *w, skip=skip)
            mm(o, lh, rl, False, False, skip=skip)
            return mm(o, ll, rh, False, last, skip=skip)

        sct = Ring([SCT[:, 16 * i:16 * i + 16] for i in range(4)])

        def diag_bcast(cols, nt, dgfree, *w):
            ds = []
            for j in range(nt):
                ds.append(ts(V, DG[:, j * 128:(j + 1) * 128], IDN[:, :], cols[:, j:j + 1], None, MUL, None, w, dgfree))
            b, bk, bf = auxr.take()
            t = mm(bk[:, 0:nt * 128], ONES[:, :], DG[:, 0:nt * 128], True, True, ds[-1], bf)
            return b, bk, t

        dgf = [None]

        def stat_cols(accs, nt, *w):
            b, bk, bf = auxr.take()
            t = None
            for a, acc in enumerate(accs):
                for j in range(nt):
                    t = mm(bk[:, a * 4 + j:a * 4 + j + 1], acc[:, j * 128:(j + 1) * 128], ONES[:, 0:1],
                           True, True, w, bf)
            return b, bk, t

        def rms_bcast(acc, nt, n, eps, *w):
            b, bk, t = stat_cols([acc], nt, w)
            si, sc, sf = sct.take()
            v = ts(V, sc[:, 0:nt], bk[:, 0:nt], 1.0 / n, eps, MUL, ADD, t, sf)
            auxr.give(b, v)
            g = G(lambda e: e.tensor_tensor(sc[:, 4:4 + nt], sc[:, 0:nt], NPOW[:, 0:nt], ALU.pow), v, np_t)
            b2, bk2, t2 = diag_bcast(sc[:, 4:4 + nt], nt, dgf[0], g)
            dgf[0] = t2
            sct.give(si, t2)
            return b2, bk2, t2, t

        def ln_bcast(s1, s2, nt, n, eps, *w):
            b, bk, t = stat_cols([s1, s2], nt, w)
            si, sc, sf = sct.take()
            m, v, r, q = (sc[:, 4 * i:4 * i + nt] for i in range(4))
            a1 = ts(V, m, bk[:, 0:nt], 1.0 / n, None, MUL, None, t, sf)
            a2 = ts(V, v, bk[:, 4:4 + nt], 1.0 / n, eps, MUL, ADD, t)
            auxr.give(b, a2)
            a3 = tt(V, q, m, m, MUL, a1)
            a4 = tt(V, v, v, q, SUB, a3, a2)
            g = G(lambda e: e.tensor_tensor(r, v, NPOW[:, 0:nt], ALU.pow), a4, np_t)
            b1, bk1, t1 = diag_bcast(r, nt, dgf[0], g)
            a5 = stt(q, m, -1.0, r, MUL, MUL, g)
            b2, bk2, t2 = diag_bcast(q, nt, t1, a5)
            dgf[0] = t2
            sct.give(si, t2)
            return (b1, bk1, t1), (b2, bk2, t2), t

        def cols_of_acc(dst, acc, n, bias, *w):
            b, bk, bf = auxr.take()
            for j in range(n):
                t = mm(bk[:, j:j + 1], acc[:, j * 128:(j + 1) * 128], ONES[:, 0:1], True, True, w, bf)
            v = tt(V, dst, bk[:, 0:n], bias, ADD, t)
            auxr.give(b, v)
            return t, v

        c1 = ExitStack()
        SM = sb("SM", [128, 512], F32, c1)
        FAC = sb("FAC", [128, 64], F32, c1)
        MK = sb("MK", [128, 7 * 128], U8, c1)
        CC = sb("CC", [128, 24], F32, c1)
        ACC = sb("ACC", [128, 2, 512], F32, c1)
        HH = sb("HH", [128, 8, S], F32R, c1)
        HL = sb("HL", [128, 8, S], F32R, c1)
        MPH = sb("MPH", [128, 8, S], F32R, c1)
        MPL = sb("MPL", [128, 8, S], F32R, c1)
        DH = sb("DH", [128, 2, S], F32R, c1)
        DL = sb("DL", [128, 2, S], F32R, c1)
        HB = sb("HB", [128, 10, S], F32, c1)
        GP = sb("GP", [128, 2, S], F32, c1)
        AT = sb("AT", [128, S], F32, c1)
        KDT = sb("KDT", [128, S], F32, c1)
        E0 = sb("E0", [128, S], F32, c1)
        Q0 = sb("Q0", [128, S], F32, c1)
        SS = sb("SS", [128, 7, 128], F32, c1)
        XR = [sb(f"XR{i}", [128, S], F32, c1) for i in range(4)]
        UPA = sb("UPA", [128, 3 * (16 + S)], F32, c1)
        UP = [UPA[:, i * (16 + S):(i + 1) * (16 + S)] for i in range(3)]
        PR = UPA[:, 0:640].rearrange("p (t n) -> p t n", n=128)
        xr = Ring([x[:, :] for x in XR])
        XT = XL

        P.dma("act", HB[:, 0:2, :].rearrange("p a n -> p (a n)")[:, 0:896], masks[:, :], s_msk)
        P.dma("act", SM[:, :], consts[:, 128:640], s_msk)
        m_dma = P.dma("act", FAC[:, :], consts[:, 640:704], s_msk)
        mk_t = cp(G, MK[:, :], HB[:, 0:2, :].rearrange("p a n -> p (a n)")[:, 0:896], m_dma)

        par = None
        for t, rows in enumerate(PARAMS):
            for name, n in rows:
                r = COL[name][1]
                if name == "conv_dw_w_2":
                    src = A[name][0].rearrange("k (b p) -> (k b) p", p=128)
                elif name == "ffn_dw_w_2a":
                    src = A["ffn_dw_w_2"][0, 0:2, :].rearrange("k (b p) -> (k b) p", p=128)
                elif name == "ffn_dw_w_2b":
                    src = A["ffn_dw_w_2"][0, 2:3, :].rearrange("k (b p) -> (k b) p", p=128)
                elif name == "c_ctx_2":
                    src = A[name].rearrange("(b p) -> b p", p=128)
                else:
                    src = A[name].rearrange("o (b p) -> (o b) p", p=128)
                par = P.dma("act", PR[r:r + n, t, :], src, s_par)

        ss_cols = newcols(8)

        def x_item(j, first):
            def proc(raw, tok):
                o = []
                if first:
                    si, sc, sf = xr.take()
                    a0 = act(DG[:, 0:512], raw[:, 0:512], ACTF.Square, tok, sq_toks[-1:], acc=ss_cols[:, j:j + 1])
                    a1 = act(DG[:, 0:512], raw[:, 512:1024], ACTF.Square, a0, acc=ss_cols[:, 4 + j:5 + j])
                    xr.give(si)
                    o.append(a1)
                    sq_toks.append(a1)
                for hf in range(2):
                    b, bk, bf = mainr.take()
                    for k in range(4):
                        kk = hf * 4 + k
                        t = tr(bk[:, k * 128:(k + 1) * 128], raw[:, kk * 128:(kk + 1) * 128], IDN[:, :], tok, bf, c_dma)
                    dst = (XT if first else XT2)[:, hf * 4:hf * 4 + 4, j * 128:(j + 1) * 128]
                    a = act(dst, bk.rearrange("p (k n) -> p k n", n=128), ACTF.Copy, t, x2_free)
                    mainr.give(b, a)
                    xt_toks.append(a)
                o.append(t)
                return o
            return proc

        sq_toks, xt_toks = [], []
        x2_free = []
        XT2 = HB[:, 0:8, :]
        for j in range(4):
            items.append(dict(kind="x", loads=[(lambda raw: raw[:, 0:1024], A["x"][0, j * 128:(j + 1) * 128, :])],
                              proc=x_item(j, True)))

        M1 = newcols(24)
        M2 = newcols(48)
        MC = newcols(16)
        accf = [[], []]
        cc_t = {}
        mod_t = {}

        def ada_items(name, wap, g, vecs, dsts):
            state = {}

            def proc_for(half):
                def proc(raw, tok):
                    w = raw.rearrange("p (k n) -> p k n", n=512)
                    last = []
                    prev = state.get("prev", [None] * len(vecs))
                    for k in range(4):
                        kk = half * 4 + k
                        for vi, cb in enumerate(vecs):
                            a = ACC[:, vi, :]
                            cs = CC[:, cb + kk:cb + kk + 1]
                            if kk == 0:
                                t = ts(V, a, w[:, k, :], cs, None, MUL, None, tok, cc_t["all"], accf[vi])
                            else:
                                t = stt(a, w[:, k, :], cs, a, MUL, ADD, tok, prev[vi])
                            prev[vi] = t
                            last.append(t)
                    state["prev"] = prev
                    if half == 1:
                        for vi, (dst, bias) in enumerate(dsts):
                            t, v = cols_of_acc(dst, ACC[:, vi, :], 4, bias, prev[vi], on_t)
                            accf[vi] = [t]
                            mod_t[(name, g, vi)] = v
                            mod_t["last"] = v
                    return last[-1]
                return proc

            return [dict(kind="a", loads=[(lambda raw: raw[:, :].rearrange("p (k n) -> p k n", n=512),
                                           wsrc(wap, half * 4, 4, g * 512, 512))], proc=proc_for(half))
                    for half in range(2)]

        def ada1(g):
            return ada_items("a1", A["ada_w"][0], g, [0], [(M1[:, 4 * g:4 * g + 4], col("ada_b", 4 * g, 4))])

        def ada2(g):
            two = g < 4
            return ada_items("a2", A["w_ada_2"][0], g, [8, 16] if two else [8],
                             [(M2[:, 4 * g:4 * g + 4], col("b_ada_2", 4 * g, 4))]
                             + ([(MC[:, 4 * g:4 * g + 4], col("b_ada_2", 4 * g, 4))] if two else []))

        for g in range(4):
            items += ada1(g)
        later = []
        for g in (4, 5):
            later += ada1(g)
        for g in range(12):
            later += ada2(g)

        def also(n=1):
            for _ in range(n):
                if later:
                    items.append(later.pop(0))

        w_in = A["w_in"][0]
        U0, GP0, Q_0, F0, I0, GH0 = (1024 * i for i in range(6))
        for h in range(8):
            unit(w_in, 0, 8, [(I0 + h * 128, 128), (F0 + h * 128, 128)])
            also()
            unit(w_in, 0, 8, [(Q_0 + h * 128, 128), (GH0 + h * 128, 128)])
            also()
        for g in range(4):
            unit(w_in, 0, 8, [(GP0 + g * 256, 256)])
            also()
            unit(w_in, 0, 8, [(U0 + g * 256, 256)])
            unit(A["pool_w"][0, g], 0, 2, [(0, 256)])
            also()
        for cpair in range(4):
            unit(A["w_out"][0], 0, 8, [(cpair * 256, 256)])
            also()
            unit(A["w_out"][0], 8, 8, [(cpair * 256, 256)])
            also()
        also(100)
        for j in range(4):
            items.append(dict(kind="x2", loads=[(lambda raw: raw[:, 0:1024], A["x"][0, j * 128:(j + 1) * 128, :])],
                              proc=x_item(j, False)))

        ctx_items = [dict(kind="c", loads=[(lambda raw: raw[:, 0:1024], A["ctx_2"][0, j * 128:(j + 1) * 128, :])],
                          proc=None) for j in range(2)]
        items += ctx_items
        w2 = A["w_in_2"][0]
        for j in range(4):
            unit(w2, 0, 8, [(j * 128, 128), (512 + j * 128, 128)])
        unit(w2, 0, 8, [(1024, 256)])
        unit(w2, 0, 8, [(1280, 256)])

        def grp(t, a, b, lo, hi, step):
            return t[:, a:a + b].rearrange("p (g n) -> p g n", n=step)[:, :, lo:hi]

        kr_l = [(lambda raw: rv(raw, 8, 160), wsrc(w2, 0, 8, 1536, 160))]
        kr_p = [(lambda r: grp(r, 0, 1280, 0, 128, 160), lambda w: grp(w, 0, 2048, 0, 128, 256))]
        for lo, hi, at in ((128, 160, 128), (128, 160, 160), (128, 160, 192), (144, 160, 224), (128, 144, 240)):
            kr_p.append((lambda r, lo=lo, hi=hi: grp(r, 0, 1280, lo, hi, 160),
                         lambda w, lo=lo, hi=hi, at=at: grp(w, 0, 2048, at, at + hi - lo, 256)))
        item_w(kr_l, kr_p)
        for g in range(2):
            q_l = [(lambda raw: rv(raw, 3, 384), wsrc(A["w_uq_2"][0], 0, 3, g * 384, 384))]
            q_p = [(lambda r, lo=lo, hi=hi: grp(r, 0, 1152, lo, hi, 96),
                    lambda w, lo=lo, hi=hi, at=at: grp(w, 0, 1536, at, at + hi - lo, 128))
                   for lo, hi, at in ((0, 96, 0), (80, 96, 96), (64, 80, 112))]
            item_w(q_l, q_p)
            kv_l = [(lambda raw: rv(raw, 2, 512), wsrc(A["w_ukv_2"][0], 0, 2, g * 512, 512))]
            kv_p = [(lambda r: grp(r, 0, 1024, 0, 64, 128), lambda w: grp(w, 0, 512, 0, 64, 64)),
                    (lambda r: grp(r, 0, 1024, 64, 128, 128), lambda w: grp(w, 512, 512, 0, 64, 64))]
            item_w(kv_l, kv_p)
        for cpair in range(4):
            unit(A["w_o_2"][0], 0, 8, [(cpair * 256, 256)])
        for j in range(22):
            unit(A["w_up_2"][0], 0, 8, [(j * 128, 128), (2816 + j * 128, 128)])
        for cpair in range(4):
            for r0, nk in ((0, 8), (8, 7), (15, 7)):
                unit(A["w_down_2"][0], r0, nk, [(cpair * 256, 256)])

        par_t = None
        for t, rows in enumerate(PARAMS):
            n = sum(r for _, r in rows)
            b, bk, bf = auxr.take()
            x = tr(bk[:, 0:n], PR[0:n, t, :], IDN[0:n, 0:n], par, c_dma, bf)
            par_x = x
            par_t = cp(V, PC[:, t, 0:n], bk[:, 0:n], x)
            auxr.give(b, par_t)
        a1 = act(CC[:, 0:8], col("c", 0, 8), ACTF.Silu, par_t)
        a2 = act(CC[:, 8:24], col("c_2", 0, 16), ACTF.Silu, par_t)
        cc_t["all"] = [a1, a2]
        LB, LT, OML = newcols(8), newcols(8), newcols(8)
        hlb = col("hgrn_lower_bounds", 0, 8)
        v1 = tt(V, LT, hlb, hlb, SUB, par_t)
        v2 = act(LT, LT, ACTF.Exp, v1)
        v3 = V(lambda e: e.reciprocal(OML, LT), v2)
        v4 = tt(V, LT, LT, OML, MUL, v3)
        v5 = tt(V, LB, LT, LT, SUB, v4)
        lb_t = ts(V, OML, LB, -1.0, 1.0, MUL, ADD, v5)
        pad_t = None
        for u in UP:
            pad_t = G(lambda e, u=u: e.memset(u[:, 0:16], 0.0), par_x)

        st.flush_until("x")
        si, sc, sf = sct.take()
        v = tt(V, sc[:, 0:4], ss_cols[:, 0:4], ss_cols[:, 4:8], ADD, sq_toks)
        v = ts(V, sc[:, 0:4], sc[:, 0:4], 1.0 / D, EPS1, MUL, ADD, v)
        g_ = G(lambda e: e.tensor_tensor(sc[:, 4:8], sc[:, 0:4], NPOW[:, 0:4], ALU.pow), v, np_t)
        b, rb, t = diag_bcast(sc[:, 4:8], 4, sq_toks, g_, on_t)
        dgf[0] = t
        sct.give(si, t)
        n_toks = []
        for k in range(8):
            n_toks.append(tt(V, XT[:, k, :], XT[:, k, :], rb, MUL, t, xt_toks))
        auxr.give(b, n_toks[-1])
        st.flush_until("a")
        A1, G1 = newcols(8), newcols(8)
        v = ts(V, A1, M1[:, 8:16], 1.0, None, ADD, None, mod_t["last"])
        a1_t = tt(V, A1, A1, col("norm_pre_w", 0, 8), MUL, v)
        h_toks = []
        for k in range(8):
            v = ts(V, XT[:, k, :], XT[:, k, :], A1[:, k:k + 1], M1[:, k:k + 1], MUL, ADD, a1_t, n_toks[k])
            a = act(HH[:, k, :], XT[:, k, :], ACTF.Copy, v)
            h_toks.append([a, tt(V, HL[:, k, :], XT[:, k, :], HH[:, k, :].bitcast(F32), SUB, a)])
        xt_free = h_toks[-1]

        ticks = []

        def tick():
            for _ in range(1):
                if ticks:
                    try:
                        next(ticks[0])
                    except StopIteration:
                        ticks.pop(0)

        def block(bk, wh, wl, xh, xl, nk, wtoks, xtoks, bf, tk=(), first=True, last=True):
            t = None
            for k in range(nk):
                t = mm3(bk, wh(k), wl(k), xh(k), xl(k), first and k == 0, last and k == nk - 1,
                        wtoks, xtoks[k] if xtoks else None, bf)
                if k in tk:
                    tick()
            return t

        def wk(w, n, c0, m=128):
            v = w[:, :].rearrange("p (k n) -> p k n", n=n)
            return lambda k: v[:, k, c0:c0 + m]

        def wk2(w, nk, c0):
            v = w[:, 0:nk * 256].rearrange("p (k n) -> p k n", n=256)
            return lambda k: v[:, k, c0:c0 + 128]

        hh = lambda k: HH[:, k, :]
        hl = lambda k: HL[:, k, :]

        MKv = MK[:, :].rearrange("p (l n) -> p l n", n=128)
        buf = {"AT": None, "KDT": None, "E0": None, "Q0": None, "SS": None}
        hfree = [dict(v=mk_t, k=mk_t), dict()]
        oh_t = {}

        def zhead(h):
            p = h % 2
            Vb, Kb, Bb, Qb, Gb = (HB[:, 5 * p + i, :] for i in range(5))
            fr = hfree[p]
            r = {}
            TK = (1, 3, 5, 7)
            w, wh, wl, wt = st.next()
            b, bk, bf = mainr.take()
            for j in range(4):
                for k in range(8):
                    js = slice(j * 128, (j + 1) * 128)
                    t = mm3(bk[:, js], HH[:, k, js], HL[:, k, js], wk(wh, 256, 0)(k), wk(wl, 256, 0)(k),
                            k == 0, k == 7, wt, h_toks[k], bf)
                tick()
            r["v"] = act(Vb, bk, ACTF.Copy, t, fr.get("v"))
            mainr.give(b, r["v"])
            b, bk, bf = mainr.take()
            t = block(bk, wk(wh, 256, 128), wk(wl, 256, 128), hh, hl, 8, wt, None, bf, TK)
            st.done(w, t)
            xi, x, xf = xr.take()
            s_ = act(Kb, bk, ACTF.Sigmoid, t, fr.get("k"))
            mainr.give(b, s_)
            f_ = ts(V, Kb, Kb, OML[:, h:h + 1], LB[:, h:h + 1], MUL, ADD, s_, lb_t)
            l_ = act(x, Kb, ACTF.Ln, f_, xf)
            r["k"] = ts(V, Kb, Kb, -1.0, 1.0, MUL, ADD, l_)
            r["b"] = V(lambda e: e.tensor_tensor_scan(Bb, SM[:, :], x, 0.0, MUL, ADD), l_, m_dma, fr.get("b"))
            xr.give(xi, r["b"])
            w, wh, wl, wt = st.next()
            b, bk, bf = mainr.take()
            t = block(bk, wk(wh, 256, 0), wk(wl, 256, 0), hh, hl, 8, wt, None, bf, TK)
            r["q"] = act(Qb, bk, ACTF.Copy, t, fr.get("q"))
            mainr.give(b, r["q"])
            b, bk, bf = mainr.take()
            t = block(bk, wk(wh, 256, 128), wk(wl, 256, 128), hh, hl, 8, wt, None, bf, TK)
            st.done(w, t)
            r["g"] = act(Gb, bk, ACTF.Silu, t, fr.get("g"))
            mainr.give(b, r["g"])
            return r

        def hgrn(h, r):
            p = h % 2
            Vb, Kb, Bb, Qb, Gb = (HB[:, 5 * p + i, :] for i in range(5))
            ats = G(lambda e: e.memset(AT[:, :], 0.0), buf["AT"])
            last_cp = [ats]
            pend = []

            def ew(l):
                half, blk = 1 << (l - 1), 1 << l
                Bv, Kv, Qv = (z.rearrange("p (n b) -> p n b", b=blk) for z in (Bb, Kb, Qb))
                xi, x, xf = xr.take()
                Xv = x.rearrange("p (n b) -> p n b", b=blk)
                ref = Bv[:, :, half - 1:half].broadcast_to([128, 512 // blk, half])
                g1 = tt(G, Xv[:, :, half:blk], Bv[:, :, half:blk], ref, SUB, r["b"], xf)
                g2 = tt(G, Xv[:, :, 0:half], ref, Bv[:, :, 0:half], SUB, r["b"], xf)
                a = act(x, x, ACTF.Exp, g1, g2)
                v1 = tt(V, Xv[:, :, half:blk], Xv[:, :, half:blk], Qv[:, :, half:blk], MUL, a, r["q"])
                v2 = tt(V, Xv[:, :, 0:half], Xv[:, :, 0:half], Kv[:, :, 0:half], MUL, a, r["k"])
                pend.append((l, xi, x, [v1, v2]))

            def sc(l, xi, x, toks):
                b, bk, bf = auxr.take()
                for j in range(4):
                    js = slice(j * 128, (j + 1) * 128)
                    lo = Kb[:, js] if l == 0 else x[:, js]
                    ro = Qb[:, js] if l == 0 else x[:, js]
                    t = mm(bk[:, js], lo, ro, True, True, toks, bf)
                if xi is not None:
                    xr.give(xi, t)
                half, blk = (0, 128) if l == 0 else (1 << (l - 1), 1 << l)
                o, d = (z.rearrange("p (j n b) -> p j n b", n=128 // blk, b=blk)[:, :, :, half:blk]
                        for z in (AT[:, :], bk))
                m = MKv[:, l, :].rearrange("p (j n b) -> p j n b", j=1, b=blk)[:, :, :, half:blk]\
                    .broadcast_to([128, 4, 128 // blk, blk - half])
                last_cp[0] = V(lambda e: e.copy_predicated(o, m, d), t, last_cp[0], mk_t)
                auxr.give(b, last_cp[0])
                return t

            ew(1)
            yield
            sc(0, None, None, [r["k"], r["q"]])
            ew(2)
            yield
            for l in range(3, 7):
                ew(l)
                sc(*pend.pop(0))
                yield
            a = act(E0[:, :], Bb, ACTF.Exp, r["b"], buf["E0"])
            q0 = tt(V, Q0[:, :], E0[:, :], Qb, MUL, a, r["q"], buf["Q0"])
            e0_t = a
            sc(*pend.pop(0))
            xi, x, xf = xr.take()
            Bv = Bb.rearrange("p (n b) -> p n b", b=64)
            Xv = x.rearrange("p (n b) -> p n b", b=64)
            g = tt(G, Xv, Bv[:, :, 63:64].broadcast_to([128, 8, 64]), Bv, SUB, r["b"], xf)
            a = act(x, x, ACTF.Exp, g)
            kd = tt(V, x, x, Kb, MUL, a, r["k"])
            yield
            sc(*pend.pop(0))
            hfree[p]["b"] = [a, e0_t]
            hfree[p]["k"] = kd
            b, bk, bf = auxr.take()
            for j in range(4):
                js = slice(j * 128, (j + 1) * 128)
                t = tr(bk[:, js], x[:, js], IDN[:, :], kd, bf)
            xr.give(xi, t)
            hfree[p]["k"] = [kd, t]
            kt = act(KDT[:, :], bk, ACTF.Copy, t, buf["KDT"])
            auxr.give(b, kt)
            yield
            prev = None
            kb_ = [auxr.take() for _ in range(2)]
            kt_ = [None, None]
            for c in range(7):
                rs = slice((c % 2) * 64, (c % 2) * 64 + 64)
                js = slice((c // 2) * 128, (c // 2) * 128 + 128)
                kt_[c % 2] = mm(kb_[c % 2][1][:, js], KDT[rs, js], Vb[rs, js], True, True, kt, r["v"], kb_[c % 2][2])
            yield
            for c in range(7):
                kv = kb_[c % 2][1][:, (c // 2) * 128:(c // 2) * 128 + 128]
                if c == 0:
                    prev = cp(V, SS[:, 0, :], kv, kt_, buf["SS"])
                else:
                    prev = stt(SS[:, c, :], SS[:, c - 1, :], E0[:, 64 * c + 63:64 * c + 64], kv, MUL, ADD,
                               prev, e0_t)
            auxr.give(kb_[0][0], prev)
            auxr.give(kb_[1][0], prev)
            t = kt_
            yield
            buf["KDT"] = t
            buf["E0"] = [prev, q0]
            b, bk, bf = auxr.take()
            for j in range(4):
                js = slice(j * 128, (j + 1) * 128)
                mm(bk[:, js], Vb[:, js], AT[:, js], j == 0, False, last_cp[0], bf, skip=True)
            yield
            for c in range(1, 8):
                t = mm(bk[:, c * 64:c * 64 + 64], SS[:, c - 1, :], Q0[:, c * 64:c * 64 + 64], False, c == 7,
                       prev, q0, skip=True)
            buf["AT"] = buf["SS"] = buf["Q0"] = t
            hfree[p]["v"] = t
            hfree[p]["q"] = t
            xi, x, xf = xr.take()
            o = act(XT[:, h, :], bk, ACTF.Copy, t, xt_free)
            sq = act(x, bk, ACTF.Square, t, xf)
            auxr.give(b, sq)
            yield
            rb_, rbk, rt, stt_ = rms_bcast(x, 4, 128, EPS1, sq)
            xr.give(xi, stt_)
            yield
            v = stt(XT[:, h, :], XT[:, h, :], col("hgrn_norm_w"), rbk, MUL, MUL, rt, o)
            auxr.give(rb_, v)
            oh_t[h] = tt(G, XT[:, h, :], XT[:, h, :], Gb, MUL, v, r["g"])
            hfree[p]["g"] = oh_t[h]

        for h in range(8):
            r = zhead(h)
            while ticks:
                tick()
            ticks.append(hgrn(h, r))

        mix_t = {}
        gp_free, d_free = [None], [None]
        upf = [[], [], []]
        for g in range(4):
            w, wh, wl, wt = st.next()
            gp_t = []
            for m in range(2):
                b, bk, bf = mainr.take()
                t = block(bk, wk(wh, 256, m * 128), wk(wl, 256, m * 128), hh, hl, 8, wt, None, bf, (1, 3, 5, 7))
                a = act(GP[:, m, :], bk, ACTF.Silu, t, gp_free[0])
                mainr.give(b, a)
                gp_t.append(a)
            st.done(w, t)
            w, wh, wl, wt = st.next()
            dt_ = []
            for m in range(2):
                b, bk, bf = mainr.take()
                t = block(bk, wk(wh, 256, m * 128), wk(wl, 256, m * 128), hh, hl, 8, wt, None, bf, (1, 3, 5, 7))
                u, s0, s1 = UP[0], UP[1], UP[2]
                a = act(u[:, 16:], bk, ACTF.Copy, t, upf[0])
                mainr.give(b, a)
                src, prev = u, a
                for i in range(g + 1):
                    d = 1 << i
                    dst = (s0, s1)[i % 2]
                    prev = tt(G, dst[:, 16:], src[:, 16:], src[:, 16 - d:528 - d], ADD, prev, pad_t, upf[1 + i % 2])
                    src = dst
                wd = 2 << g
                prev = tt(V, src[:, 16:16 + wd], src[:, 16:16 + wd], FAC[:, 16 * g:16 * g + wd], MUL, prev, m_dma)
                prev = stt(src[:, 16:], src[:, 16:], 1.0 / wd, u[:, 16:], MUL, SUB, prev)
                a = act(DH[:, m, :], src[:, 16:], ACTF.Copy, prev, d_free[0])
                v = tt(V, DL[:, m, :], src[:, 16:], DH[:, m, :].bitcast(F32), SUB, a)
                upf = [[prev], [v], [v]]
                dt_.append([a, v])
            st.done(w, t)
            last_z = t
            w, wh, wl, wt = st.next()
            for m in range(2):
                b, bk, bf = mainr.take()
                t = block(bk, wk(wh, 256, m * 128), wk(wl, 256, m * 128), lambda k: DH[:, k, :],
                          lambda k: DL[:, k, :], 2, wt, dt_, bf)
                kk = 2 * g + m
                v = stt(GP[:, m, :], bk, col("pool_scale", kk), GP[:, m, :], MUL, MUL, t, gp_t[m])
                mainr.give(b, v)
                a = act(MPH[:, kk, :], GP[:, m, :], ACTF.Copy, v)
                v = tt(V, MPL[:, kk, :], GP[:, m, :], MPH[:, kk, :].bitcast(F32), SUB, a)
                gp_free[0] = v
                mix_t[kk] = [a, v]
            d_free[0] = t
            st.done(w, t)
        while ticks:
            tick()
        for h in range(8):
            a = act(HH[:, h, :], XT[:, h, :], ACTF.Copy, oh_t[h], last_z)
            v = tt(V, HL[:, h, :], XT[:, h, :], HH[:, h, :].bitcast(F32), SUB, a, last_z)
            mix_t[8 + h] = [a, v]
        xt_free = [mix_t[15]]

        def acc_stats(src, m, s1, s2, sq, stt_, toks):
            a = act(sq[1], src, ACTF.Square, toks, sq[2])
            if m == 0:
                t2 = cp(G, s2, sq[1], a, stt_.get("free"))
                t1 = cp(G, s1, src, toks, stt_.get("free")) if s1 is not None else None
            else:
                t2 = tt(G, s2, s2, sq[1], ADD, a, stt_["s2"])
                t1 = tt(G, s1, s1, src, ADD, toks, stt_["s1"]) if s1 is not None else None
            stt_["s1"], stt_["s2"] = t1, t2
            return [a, t2]

        y_t = []
        chain = {}
        S1, S2 = AT[:, :], Q0[:, :]
        for cpair in range(4):
            bs = [mainr.take() for _ in range(2)]
            for half in range(2):
                w, wh, wl, wt = st.next()
                for m in range(2):
                    b, bk, bf = bs[m]
                    if half == 0:
                        xh_, xl_, xt_ = (lambda k: MPH[:, k, :]), (lambda k: MPL[:, k, :]), [mix_t[k] for k in range(8)]
                    else:
                        xh_, xl_, xt_ = hh, hl, [mix_t[8 + k] for k in range(8)]
                    t = block(bk, wk(wh, 256, m * 128), wk(wl, 256, m * 128), xh_, xl_, 8, wt, xt_, bf,
                              first=half == 0, last=half == 1)
                    if half == 1:
                        kk = 2 * cpair + m
                        a = act(XT[:, kk, :], bk, ACTF.Copy, t, xt_free)
                        mainr.give(b, a)
                        y_t.append(a)
                        xi, x, xf = xr.take()
                        u = acc_stats(XT[:, kk, :], kk, None, S2, (xi, x, xf), chain, [a, buf["Q0"]])
                        xr.give(xi, u)
                st.done(w, t)
        st.flush_until("a")
        x2_free += [oh_t[7], oh_t[6]]
        xt_toks = []
        st.flush_until("x2")
        b, rb, t, _ = rms_bcast(S2, 4, D, EPS1, chain["s2"])
        g1_t = tt(V, G1, M1[:, 16:24], col("norm_post_w", 0, 8), MUL, mod_t["last"])
        x1_t = []
        chain = {"free": [t, buf["AT"]]}
        for k in range(8):
            v = stt(XT[:, k, :], XT[:, k, :], G1[:, k:k + 1], rb, MUL, MUL, t, g1_t, y_t[k])
            v = tt(V, XT[:, k, :], XT[:, k, :], XT2[:, k, :], ADD, v, xt_toks)
            x1_t.append(v)
            xi, x, xf = xr.take()
            u = acc_stats(XT[:, k, :], k, S1, S2, (xi, x, xf), chain, v)
            xr.give(xi, u)
        auxr.give(b, v)
        (b1, rb, t1), (b2, mb, t2), st_t = ln_bcast(S1, S2, 4, D, EPS2, chain["s1"], chain["s2"])
        xl_t = []
        for k in range(8):
            v = tt(V, XL[:, k, :], XL[:, k, :], rb, MUL, t1, x1_t[k], chain["s1"], chain["s2"])
            v = tt(V, XL[:, k, :], XL[:, k, :], mb, ADD, v, t2)
            xl_t.append(v)
        auxr.give(b1, v)
        auxr.give(b2, v)
        end1 = [v, t2]
        c1.close()
        assert not ticks
        if stop == 1:
            return finish(nc, ctx, P, A, out, XL, xl_t, IDN, mainr, s_out, ACTF, act, tr)

        cM = ExitStack()
        MH = sb("MH", [128, 8, S], F32R, cM)
        ML = sb("ML", [128, 8, S], F32R, cM)
        c2 = ExitStack()
        CH = sb("CH", [128, 6, 512], F32R, c2)
        CL = sb("CL", [128, 6, 512], F32R, c2)
        QG = sb("QG", [128, 4, S], F32, c2)
        KG = sb("KG", [128, 4, NKEY], F32, c2)
        VG = sb("VG", [128, 6, 256], F32, c2)
        KR = sb("KR", [128, NKEY], F32, c2)
        VP = sb("VP", [128, 4, S + 30], F32, c2)
        CV = sb("CV", [128, 4, S], F32, c2)
        OTm = sb("OTm", [128, 4, 512], F32, c2)
        PM = [sb(f"PM{i}", [128, NKEY], F32, c2) for i in range(2)]
        PT = [sb(f"PT{i}", [128, NKEY], F32, c2) for i in range(2)]
        CS = sb("CS", [128, NKEY], F32, c2)
        XC = KG[:, :, :].rearrange("p a n -> p (a n)")[:, 0:2048].rearrange("p (k n) -> p k n", n=NCTX)
        HCH = CH[:, 0:4, :].rearrange("p a n -> p (a n)").rearrange("p (k n) -> p k n", n=NCTX)
        HCL = CL[:, 0:4, :].rearrange("p a n -> p (a n)").rearrange("p (k n) -> p k n", n=NCTX)
        CQ = QG[:, 0:3, :]
        CKV = KG[:, 0:2, :]
        CKH, CKL = (z[:, 3:6, :].rearrange("p a n -> p (a n)").rearrange("p (k n) -> p k n", n=NKEY)
                    for z in (CH, CL))
        cs_t = P.dma("act", CS[:, :], consts[:, 704:704 + NKEY], s_msk, end1, st_t, *[xl_t])
        vp_t = [G(lambda e, a=a: e.memset(VP[:, :, a:a + 15], 0.0), end1, oh_t[7], chain["s2"]) for a in (0, S + 15)]

        xc_t = []
        stc = newcols(16)
        for j in range(2):
            def proc(raw, tok, j=j):
                o = []
                si, x, sf = pmr.take()
                a1 = act(x, raw[:, 0:512], ACTF.Square, tok, sf, end1, acc=stc[:, j:j + 1])
                a2 = act(x, raw[:, 512:1024], ACTF.Square, a1, acc=stc[:, 2 + j:3 + j])
                a3 = act(x, raw[:, 0:512], ACTF.Identity, a2, acc=stc[:, 4 + j:5 + j])
                a4 = act(x, raw[:, 512:1024], ACTF.Identity, a3, acc=stc[:, 6 + j:7 + j])
                pmr.give(si, a4)
                for hf in range(2):
                    b, bk, bf = mainr.take()
                    for k in range(4):
                        kk = hf * 4 + k
                        t = tr(bk[:, k * 128:(k + 1) * 128], raw[:, kk * 128:(kk + 1) * 128], IDN[:, :], tok, bf)
                    a = act(XC[:, hf * 4:hf * 4 + 4, j * 128:(j + 1) * 128], bk.rearrange("p (k n) -> p k n", n=128),
                            ACTF.Copy, t, end1)
                    mainr.give(b, a)
                    xc_t.append(a)
                return [a4, t]
            ctx_items[j]["proc"] = proc
            if j == 0:
                pmr = Ring([x[:, 0:512] for x in PM])
            st.process()
        v1 = tt(V, stc[:, 8:10], stc[:, 4:6], stc[:, 6:8], ADD, xc_t)
        v2 = tt(V, stc[:, 10:12], stc[:, 0:2], stc[:, 2:4], ADD, xc_t)
        v1 = ts(V, stc[:, 8:10], stc[:, 8:10], 1.0 / D, None, MUL, None, v1)
        v2 = ts(V, stc[:, 10:12], stc[:, 10:12], 1.0 / D, EPS2, MUL, ADD, v2)
        v3 = tt(V, stc[:, 12:14], stc[:, 8:10], stc[:, 8:10], MUL, v1)
        v4 = tt(V, stc[:, 10:12], stc[:, 10:12], stc[:, 12:14], SUB, v2, v3)
        g = G(lambda e: e.tensor_tensor(stc[:, 12:14], stc[:, 10:12], NPOW[:, 0:2], ALU.pow), v4)
        v5 = stt(stc[:, 14:16], stc[:, 8:10], -1.0, stc[:, 12:14], MUL, MUL, g)
        b1, rb, t1 = diag_bcast(stc[:, 12:14], 2, dgf[0], g)
        b2, mb, t2 = diag_bcast(stc[:, 14:16], 2, t1, v5)
        dgf[0] = t2
        SC1, SC2, SC1C = newcols(8), newcols(8), newcols(8)
        e1 = ts(V, SC1, M2[:, 8:16], 1.0, None, ADD, None, mod_t["last"])
        e2 = ts(V, SC2, M2[:, 32:40], 1.0, None, ADD, None, mod_t["last"])
        e3 = ts(V, SC1C, MC[:, 8:16], 1.0, None, ADD, None, mod_t["last"])

        def split(dh, dl, src, *w):
            a = act(dh, src, ACTF.Copy, w)
            return [a, tt(V, dl, src, dh.bitcast(F32), SUB, a, w)]

        hc_t = []
        for k in range(8):
            x = XC[:, k, :]
            v = tt(V, x, x, rb[:, 0:NCTX], MUL, t1, xc_t)
            v = tt(V, x, x, mb[:, 0:NCTX], ADD, v, t2)
            vl = v
            v = ts(V, x, x, SC1C[:, k:k + 1], MC[:, k:k + 1], MUL, ADD, v, e3)
            hc_t.append(split(HCH[:, k, :], HCL[:, k, :], x, v, end1))
        auxr.give(b1, vl)
        auxr.give(b2, vl)

        xw = Ring([x[:, 0:512] for x in PT])
        h2_t = []
        for k in range(8):
            si, x, sf = xw.take()
            v = ts(V, x, XL[:, k, :], SC1[:, k:k + 1], M2[:, k:k + 1], MUL, ADD, xl_t[k], e1, sf, end1)
            h2_t.append(split(MH[:, k, :], ML[:, k, :], x, v, end1))
            xw.give(si, h2_t[-1])
        mh = lambda k: MH[:, k, :]
        ml = lambda k: ML[:, k, :]

        va_t, conv_t = [], []

        def conv(j):
            v = ts(V, CV[:, j, :], VP[:, j, 0:S], col("conv_dw_w_2", j), col("conv_dw_b_2", j), MUL, ADD, va_t[j], vp_t)
            for k in range(1, 31):
                v = stt(CV[:, j, :], VP[:, j, k:k + S], col("conv_dw_w_2", 4 * k + j), CV[:, j, :], MUL, ADD, v)
                if k % 2 == 0:
                    yield
            conv_t.append(v)

        TK8 = (0, 1, 2, 3, 4, 5, 6, 7)
        for j in range(4):
            w, wh, wl, wt = st.next()
            b, bk, bf = mainr.take()
            t = block(bk, wk(wh, 256, 0), wk(wl, 256, 0), mh, ml, 8, wt, h2_t, bf, TK8)
            b2, bk2, bf2 = mainr.take()
            t2 = block(bk2, wk(wh, 256, 128), wk(wl, 256, 128), mh, ml, 8, wt, h2_t, bf2, TK8)
            st.done(w, t2)
            a = act(VP[:, j, 15:15 + S], bk2, ACTF.Sigmoid, t2, end1)
            mainr.give(b2, a)
            v = tt(V, VP[:, j, 15:15 + S], VP[:, j, 15:15 + S], bk, MUL, a, t)
            mainr.give(b, v)
            va_t.append(v)
            ticks.append(conv(j))

        s2q, s2k = newcols(1), None
        qc, kc = {}, {}
        SQ = PM[0][:, 0:512]
        SA = PM[1][:, 0:512]

        def lat(m, dst, wh_, wl_, wt, tk=()):
            b, bk, bf = mainr.take()
            t = block(bk, wh_, wl_, mh, ml, 8, wt, h2_t, bf, tk)
            return b, bk, t

        def ctxb(wh_, wl_, wt):
            b, bk, bf = mainr.take()
            t = block(bk[:, 0:NCTX], wh_, wl_, lambda k: HCH[:, k, :], lambda k: HCL[:, k, :], 8, wt, hc_t, bf)
            return b, bk[:, 0:NCTX], t

        x_free = [hc_t[-1]]
        cq_t, ckv_t = [], []
        w, wh, wl, wt = st.next()
        for m in range(2):
            b, bk, t = lat(m, None, wk(wh, 256, m * 128), wk(wl, 256, m * 128), wt, TK8)
            a = act(CQ[:, m, :], bk, ACTF.Copy, t, end1)
            mainr.give(b, a)
            cq_t.append(a)
        st.done(w, t)
        w, wh, wl, wt = st.next()
        b, bk, t = lat(2, None, wk(wh, 256, 0), wk(wl, 256, 0), wt, TK8)
        a = act(CQ[:, 2, :], bk, ACTF.Copy, t, end1)
        mainr.give(b, a)
        cq_t.append(a)
        for m in range(2):
            c0 = 128
            if m == 1:
                w, wh, wl, wt = st.next()
                c0 = 0
            b, bk, t = lat(m, None, wk(wh, 256, c0), wk(wl, 256, c0), wt, TK8)
            a = act(CKV[:, m, NCTX:NKEY], bk, ACTF.Copy, t, x_free)
            mainr.give(b, a)
            b, bk, t = ctxb(wk(wh, 256, c0), wk(wl, 256, c0), wt)
            a2 = act(CKV[:, m, 0:NCTX], bk, ACTF.Copy, t, x_free)
            mainr.give(b, a2)
            ckv_t.append([a, a2])
            if m == 0:
                st.done(w, t)
        kr_t = []
        for which in range(2):
            if which == 0:
                b, bk, t = lat(0, None, wk(wh, 256, 128), wk(wl, 256, 128), wt, TK8)
                cs = slice(NCTX, NKEY)
            else:
                b, bk, t = ctxb(wk(wh, 256, 128), wk(wl, 256, 128), wt)
                cs = slice(0, NCTX)
            si, x, sf = xw.take()
            n = cs.stop - cs.start
            v1 = tt(V, x[64:96, 0:n], bk[96:128, 0:n], CS[96:128, cs], MUL, t, cs_t, sf)
            v2 = tt(V, KR[64:96, cs], bk[64:96, 0:n], CS[64:96, cs], MUL, t, cs_t)
            mainr.give(b, v2)
            v = tt(V, KR[64:96, cs], KR[64:96, cs], x[64:96, 0:n], ADD, v1, v2)
            xw.give(si, v)
            kr_t.append(v)
        st.done(w, t)
        h2_free = t

        def rms_small(src, nb, cols, n, toks, name, dh, dl):
            nt = cols // 128
            chn = None
            sc_ = None
            SAv, SQv = PM[1][:, 0:cols], PM[0][:, 0:cols]
            for m in range(nb):
                if m == 0:
                    chn = act(SAv, src[:, m, :], ACTF.Square, toks[m], sfree[0])
                else:
                    a = act(SQv, src[:, m, :], ACTF.Square, toks[m], sfree[0], chn if m > 1 else None)
                    chn = tt(V, SAv, SAv, SQv, ADD, a, chn)
            res, at = [], 0
            while at < nt:
                k = min(4, nt - at)
                b, bk, t, stt_ = rms_bcast(SAv[:, at * 128:(at + k) * 128], k, n, EPS2, chn)
                for m in range(nb):
                    cs = slice(at * 128, (at + k) * 128)
                    v = stt(src[:, m, cs], src[:, m, cs], col(name, m), bk[:, 0:k * 128], MUL, MUL, t)
                    res.append(split(dh[:, m, cs], dl[:, m, cs], src[:, m, cs], v, h2_free))
                auxr.give(b, v)
                at += k
            sfree[0] = [stt_, chn]
            return res

        sfree = [hc_t[-1]]
        pm_free0 = pmr.free
        sfree = [[*flat(pmr.free[0]), *flat(pmr.free[1])]]
        cqn = rms_small(CQ, 3, S, 384, cq_t, "q_norm_g_2", CH[:, 0:3, :], CL[:, 0:3, :])
        ckn = rms_small(CKV, 2, NKEY, 256, ckv_t, "kv_norm_g_2", CKH, CKL)

        pmr = Ring([x[:, :] for x in PM])
        ptr = Ring([x[:, :] for x in PT])
        pmr.free = [list(sfree[0]), list(sfree[0])]
        ptr.free = [list(flat(xw.free[0])), list(flat(xw.free[1]))]
        NM = newcols(6)
        nmr = Ring([NM[:, 0:3], NM[:, 3:6]])
        qg_free, kg_free, vg_free = [cqn, None], [ckn, None], [None]
        o_t = []
        for g in range(2):
            w, wh, wl, wt = st.next()
            wq = (z[:, 0:1536].rearrange("p (k h n) -> p k h n", k=3, h=4) for z in (wh, wl))
            wqh, wql = wq
            q_t = []
            for h in range(4):
                b, bk, bf = mainr.take()
                t = block(bk, lambda k: wqh[:, k, h, :], lambda k: wql[:, k, h, :], lambda k: CH[:, k, :],
                          lambda k: CL[:, k, :], 3, [wt, cqn], None, bf, (0, 1, 2))
                a = act(QG[0:64, h, :], bk[0:64, :], ACTF.Copy, t, qg_free)
                si, x, sf = ptr.take()
                v1 = tt(V, x[64:96, 0:S], bk[96:128, :], CS[96:128, NCTX:NKEY], MUL, t, sf)
                v2 = tt(V, QG[64:96, h, :], bk[64:96, :], CS[64:96, NCTX:NKEY], MUL, t, qg_free)
                mainr.give(b, a, v2)
                v = tt(V, QG[64:96, h, :], QG[64:96, h, :], x[64:96, 0:S], ADD, v1, v2)
                ptr.give(si, v)
                q_t.append([a, v])
            st.done(w, t)
            w, wh, wl, wt = st.next()
            wkh, wkl = (z[:, 0:512].rearrange("p (k n) -> p k n", k=2) for z in (wh, wl))
            wvh, wvl = (z[:, 512:1024].rearrange("p (k n) -> p k n", k=2) for z in (wh, wl))
            k_t = [[] for _ in range(4)]
            for h in range(4):
                k_t[h].append(cp(G, KG[64:96, h, :], KR[64:96, :], kr_t, kg_free))
            for pr in range(2):
                for cs in (slice(NCTX, NKEY), slice(0, NCTX)):
                    n = cs.stop - cs.start
                    b, bk, bf = mainr.take()
                    t = block(bk[:, 0:n], lambda k: wkh[:, k, pr * 128:pr * 128 + 128],
                              lambda k: wkl[:, k, pr * 128:pr * 128 + 128], lambda k: CKH[:, k, cs],
                              lambda k: CKL[:, k, cs], 2, [wt, ckn], None, bf, (0, 1))
                    for i in range(2):
                        a = act(KG[0:64, 2 * pr + i, cs], bk[64 * i:64 * i + 64, 0:n], ACTF.Copy, t, kg_free)
                        k_t[2 * pr + i].append(a)
                    mainr.give(b, a)
            v_t = []
            for t6 in range(6):
                b, bk, bf = mainr.take()
                ks = slice(t6 * 128, t6 * 128 + 128)
                t = block(bk[:, 0:256], lambda k: CKH[:, k, ks], lambda k: CKL[:, k, ks],
                          lambda k: wvh[:, k, :], lambda k: wvl[:, k, :], 2, [wt, ckn], None, bf, (0,))
                a = act(VG[:, t6, :], bk[:, 0:256], ACTF.Copy, t, vg_free)
                mainr.give(b, a)
                v_t.append(a)
            st.done(w, t)
            c_free = t

            seq = [(h, j) for h in range(4) for j in range(4)]
            stage = {}

            def scores(i):
                h, j = seq[i]
                i0, _, f0 = auxr.take()
                i1, _, f1 = auxr.take()
                bp = PB[2 + i0 // 2]
                assert i0 % 2 == 0
                js = slice(j * 128, (j + 1) * 128)
                mm(bp[:, 0:512], QG[0:96, h, js], KG[0:96, h, 0:512], True, True, q_t[h], k_t[h], f0, f1)
                t = mm(bp[:, 512:768], QG[0:96, h, js], KG[0:96, h, 512:768], True, True)
                ni, nm, nf = nmr.take()
                v = V(lambda e: e.tensor_reduce(nm[:, 0:1], bp[:, 0:NKEY], AX.X, ALU.max, negate=True), t, nf)
                v = ts(V, nm[:, 0:1], nm[:, 0:1], SCALE, None, MUL, None, v)
                pi, pm, pf = pmr.take()
                a = act(pm, bp[:, 0:NKEY], ACTF.Exp, v, pf, bias=nm[:, 0:1], scale=SCALE, acc=nm[:, 1:2])
                auxr.give(i0, a)
                auxr.give(i1, a)
                v = V(lambda e: e.reciprocal(nm[:, 2:3], nm[:, 1:2]), a)
                stage[i] = [t, pi, pm, a, ni, nm, v]

            def turn(i):
                t, pi, pm, a, ni, nm, v = stage[i]
                m0, _, f0 = mainr.take()
                m1, _, f1 = mainr.take()
                assert m0 % 2 == 0
                mp = PB[m0 // 2]
                for k in range(6):
                    t = tr(mp[:, k * 128:(k + 1) * 128], pm[:, k * 128:(k + 1) * 128], IDN[:, :], a, f0, f1)
                pmr.give(pi, t)
                qi, pt, qf = ptr.take()
                c = act(pt[:, 0:512], mp[:, 0:512], ACTF.Copy, t, qf)
                c2_ = cp(V, pt[:, 512:768], mp[:, 512:768], t, qf)
                mainr.give(m0, c)
                mainr.give(m1, c2_)
                stage[i] += [qi, pt, [c, c2_]]

            def values(i):
                h, j = seq[i]
                ni, nm, v, qi, pt, ct = stage[i][4:]
                m0, _, f0 = mainr.take()
                m1, _, f1 = mainr.take()
                bk = PB[m0 // 2][:, 0:64]
                for k in range(6):
                    t = mm(bk, pt[:, k * 128:(k + 1) * 128], VG[:, k, h * 64:h * 64 + 64], k == 0, k == 5, ct, v_t, f0, f1)
                ptr.give(qi, t)
                hg = 4 * g + h
                v = ts(V, OTm[:, j, hg * 64:hg * 64 + 64], bk, nm[:, 2:3], None, MUL, None, t, v)
                mainr.give(m0, v)
                mainr.give(m1, f1)
                nmr.give(ni, v)
                o_t.append(v)
                return t

            auxr.even()
            mainr.even()
            scores(0)
            for i in range(16):
                if i + 1 < 16:
                    scores(i + 1)
                turn(i)
                tick()
                t = values(i)
            qg_free, kg_free, vg_free = [t], [t], [t]

        while ticks:
            tick()

        S1_, S2_ = PT[0][:, 0:512], PT[1][:, 0:512]
        SQ_ = [PM[0][:, 0:512], PM[1][:, 0:512]]
        fr_ = [flat(ptr.free), flat(pmr.free)]
        c1_ = c2_ = None
        sqf = [None, None]
        for j in range(4):
            a = act(SQ_[j % 2], CV[:, j, :], ACTF.Square, conv_t[j], fr_, sqf[j % 2])
            if j == 0:
                c1_ = cp(G, S1_, CV[:, j, :], conv_t[j], fr_)
                c2_ = cp(G, S2_, SQ_[0], a, fr_)
            else:
                c1_ = tt(G, S1_, S1_, CV[:, j, :], ADD, conv_t[j], c1_)
                c2_ = tt(G, S2_, S2_, SQ_[j % 2], ADD, a, c2_)
            sqf[j % 2] = c2_
        (b1, rb, t1), (b2, mb, t2), _ = ln_bcast(S1_, S2_, 4, 512, EPS2, c1_, c2_)
        m_t = []
        for j in range(4):
            x = CV[:, j, :]
            v = tt(V, x, x, rb, MUL, t1, c1_, a)
            v = tt(V, x, x, mb, ADD, v, t2)
            vv = v
            a = act(x, x, ACTF.Silu, v, bias=col("conv_ln_b_2", j), scale=col("conv_ln_g_2", j))
            m_t.append(split(MH[:, j, :], ML[:, j, :], x, a, h2_free))
        auxr.give(b1, vv)
        auxr.give(b2, vv)
        for f in range(4):
            b, bk, bf = mainr.take()
            for j in range(4):
                t = tr(bk[:, j * 128:(j + 1) * 128], OTm[:, j, f * 128:(f + 1) * 128], IDN[:, :], o_t[-1], o_t, bf)
            a = act(MH[:, 4 + f, :], bk, ACTF.Copy, t, h2_free)
            v = tt(V, ML[:, 4 + f, :], bk, MH[:, 4 + f, :].bitcast(F32), SUB, a)
            mainr.give(b, v)
            m_t.append([a, v])
        ot_free = t

        def residual(bk, k, bias, gate, t, *w):
            si, x, sf = wr.take()
            v = ts(V, x, bk, bias, gate, ADD, MUL, t, sf)
            v2 = stt(XL[:, k, :], XL[:, k, :], ALPHA, x, MUL, ADD, v, w)
            wr.give(si, v2)
            return v, v2

        def stats_of(k, toks, s1, s2, chain):
            si, x, sf = wr.take()
            u = acc_stats(XL[:, k, :], k, s1, s2, (si, x, sf), chain, toks)
            wr.give(si, u)

        wr = Ring([OTm[:, i, :] for i in range(4)])
        wr.free = [[ot_free] for _ in range(4)]
        S1, S2 = CV[:, 0, :], CV[:, 1, :]
        chain = {"free": [m_t[0], m_t[1]]}
        r_t = []
        for cpair in range(4):
            w, wh, wl, wt = st.next()
            for m in range(2):
                kk = 2 * cpair + m
                b, bk, bf = mainr.take()
                t = block(bk, wk(wh, 256, m * 128), wk(wl, 256, m * 128), mh, ml, 8, wt, m_t, bf)
                v, v2 = residual(bk, kk, col("b_o_2", kk), M2[:, 16 + kk:17 + kk], t, h2_t[kk])
                mainr.give(b, v)
                r_t.append(v2)
                stats_of(kk, v2, S1, S2, chain)
            st.done(w, t)
        mo_free = t
        (b1, rb, t1), (b2, mb, t2), st1 = ln_bcast(S1, S2, 4, D, EPS2, chain["s1"], chain["s2"])
        A2, B2 = newcols(8), newcols(8)
        v = tt(V, A2, SC2, col("ln1_g_2", 0, 8), MUL, e2)
        v_ = tt(V, B2, SC2, col("ln1_b_2", 0, 8), MUL, e2)
        v_ = tt(V, B2, B2, M2[:, 24:32], ADD, v_)
        h3_t, xm_t = [], []
        for k in range(8):
            x = XL[:, k, :]
            v1 = tt(V, x, x, rb, MUL, t1, chain["s1"], chain["s2"], r_t[k])
            v1 = tt(V, x, x, mb, ADD, v1, t2)
            si, y, sf = wr.take()
            v2 = ts(V, y, x, A2[:, k:k + 1], B2[:, k:k + 1], MUL, ADD, v1, v, v_, sf)
            h3_t.append(split(MH[:, k, :], ML[:, k, :], y, v2, mo_free))
            wr.give(si, h3_t[-1])
            xm_t.append(ts(G, x, x, col("ln1_g_2", k), col("ln1_b_2", k), MUL, ADD, v1, v2))
        auxr.give(b1, v1)
        auxr.give(b2, v1)
        end2 = [h3_t[-1], st1, t2]
        c2.close()

        c3 = ExitStack()
        AH = sb("AH", [128, 22, S], F32R, c3)
        AL = sb("AL", [128, 22, S], F32R, c3)
        YG = [sb(f"YG{i}", [128, S], F32, c3) for i in range(4)]
        ygr = Ring([y[:, :] for y in YG])

        def tap(i, blk_):
            return col("ffn_dw_w_2a", 44 * i + blk_) if i < 2 else col("ffn_dw_w_2b", blk_)

        a_t = []
        for j in range(22):
            w, wh, wl, wt = st.next()
            ys = []
            for m in range(2):
                b, bk, bf = mainr.take()
                t = block(bk, wk(wh, 256, m * 128), wk(wl, 256, m * 128), mh, ml, 8, wt, h3_t, bf)
                blk_ = 22 * m + j
                yi, y, yf = ygr.take()
                a = act(y, bk, ACTF.Identity, t, yf, end2, bias=col("ffn_dw_b_2", blk_), scale=tap(1, blk_))
                v = stt(y[:, 1:S], bk[:, 0:S - 1], tap(0, blk_), y[:, 1:S], MUL, ADD, a)
                v = stt(y[:, 0:S - 1], bk[:, 1:S], tap(2, blk_), y[:, 0:S - 1], MUL, ADD, v)
                mainr.give(b, v)
                ys.append((yi, y, v))
            st.done(w, t)
            (gi, yg, gt), (vi, yv, vt) = ys
            a = act(yg, yg, ACTF.Silu, gt)
            v = tt(V, yg, yg, yv, MUL, a, vt)
            s_ = split(AH[:, j, :], AL[:, j, :], yg, v, end2)
            ygr.give(gi, s_)
            ygr.give(vi, v)
            a_t.append(s_)
        up_end = t
        c3y = YG
        wr = Ring([y[:, :] for y in YG])
        wr.free = [[s_, v] for _ in range(4)]
        cM2 = ExitStack()
        cM2.close()
        S1, S2 = YG[2][:, :], YG[3][:, :]
        wr = Ring([YG[0][:, :], YG[1][:, :]])
        wr.free = [[s_, v], [s_, v]]
        chain = {"free": [s_, v]}
        r_t = []
        for cpair in range(4):
            bs = [mainr.take() for _ in range(2)]
            for q, (r0, nk) in enumerate(((0, 8), (8, 7), (15, 7))):
                w, wh, wl, wt = st.next()
                for m in range(2):
                    b, bk, bf = bs[m]
                    t = block(bk, wk2(wh, nk, m * 128), wk2(wl, nk, m * 128), lambda k: AH[:, r0 + k, :],
                              lambda k: AL[:, r0 + k, :], nk, wt, [a_t[r0 + k] for k in range(nk)], bf,
                              first=q == 0, last=q == 2)
                    if q == 2:
                        kk = 2 * cpair + m
                        v, v2 = residual(bk, kk, col("b_down_2", kk), M2[:, 40 + kk:41 + kk], t, xm_t[kk])
                        mainr.give(b, v)
                        r_t.append(v2)
                        stats_of(kk, v2, S1, S2, chain)
                st.done(w, t)
        (b1, rb, t1), (b2, mb, t2), _ = ln_bcast(S1, S2, 4, D, EPS2, chain["s1"], chain["s2"])
        f_t = []
        for k in range(8):
            x = XL[:, k, :]
            v1 = tt(V, x, x, rb, MUL, t1, chain["s1"], chain["s2"], r_t[k])
            v1 = tt(V, x, x, mb, ADD, v1, t2)
            f_t.append(act(x, x, ACTF.Identity, v1, bias=col("ln2_b_2", k), scale=col("ln2_g_2", k)))
        auxr.give(b1, v1)
        auxr.give(b2, v1)
        c3.close()
        cM.close()
        OUTB = sb("OUTB", [128, 4, 1024])
        od = []
        for j in range(4):
            for hf in range(2):
                b, bk, bf = mainr.take()
                for k in range(4):
                    kk = hf * 4 + k
                    t_ = tr(bk[:, k * 128:(k + 1) * 128], XL[:, kk, j * 128:(j + 1) * 128], IDN[:, :], f_t[kk], bf)
                o = cp(V, OUTB[:, j, hf * 512:(hf + 1) * 512], bk, t_, t, f_t[-1])
                mainr.give(b, o)
            od.append(P.dma("sp", out[0, j * 128:(j + 1) * 128, :], OUTB[:, j, :], s_out, o))
        P.q["sp"].append([[od[-1]], None, None])
        run_blocks(nc, ctx, P)


def finish(nc, ctx, P, A, out, XL, toks, IDN, mainr, s_out, ACTF, act, tr):
    ot = ctx.enter_context(nc.sbuf_tensor("OT_", [128, 4, 1024], F32))
    for j in range(4):
        for hf in range(2):
            b, bk, bf = mainr.take()
            for k in range(4):
                kk = hf * 4 + k
                t = tr(bk[:, k * 128:(k + 1) * 128], XL[:, kk, j * 128:(j + 1) * 128], IDN[:, :], toks[kk], toks[-1], bf)
            a = act(ot[:, j, hf * 512:(hf + 1) * 512], bk, ACTF.Copy, t)
            mainr.give(b, a)
        d = P.dma("sp", out[0, j * 128:(j + 1) * 128, :], ot[:, j, :], s_out, a)
    P.q["sp"].append([[d], None, None])
    run_blocks(nc, ctx, P)


def run_blocks(nc, ctx, P):
    P.number()
    blk = ctx.enter_context(nc.Block())

    @blk.sync
    def _(e):
        P.emit("sp", e)

    @blk.gpsimd
    def _(e):
        P.emit("pool", e)

    @blk.scalar
    def _(e):
        P.emit("act", e)

    @blk.tensor
    def _(e):
        P.emit("pe", e)

    @blk.vector
    def _(e):
        P.emit("dve", e)


_INS = ["x", "c", "norm_pre_w", "ada_w", "ada_b", "w_in", "pool_w", "pool_scale", "hgrn_lower_bounds",
        "hgrn_norm_w", "w_out", "norm_post_w", "c_2", "ctx_2", "c_ctx_2", "w_ada_2", "b_ada_2", "w_in_2",
        "conv_dw_w_2", "conv_dw_b_2", "conv_ln_g_2", "conv_ln_b_2", "q_norm_g_2", "w_uq_2", "kv_norm_g_2",
        "w_ukv_2", "w_o_2", "b_o_2", "ln1_g_2", "ln1_b_2", "w_up_2", "ffn_dw_w_2", "ffn_dw_b_2", "w_down_2",
        "b_down_2", "ln2_g_2", "ln2_b_2"]


def shape_constants():
    f = np.float32
    con = np.zeros((128, 704 + 768), f)
    con[:, 0:128] = np.eye(128, dtype=f)
    con[:, 128:640] = (np.arange(512) % 64 != 0).astype(f)
    for g in range(4):
        w = 2 << g
        con[:, 640 + 16 * g:640 + 16 * g + w] = f(w) / np.arange(1, w + 1, dtype=f)
    tok = np.arange(S)
    inv = (f(10000.0) ** (-np.arange(8, dtype=f) / f(8))).astype(f)
    ang = np.concatenate([(tok // 64).astype(f)[:, None] * inv, (tok % 64).astype(f)[:, None] * inv], -1).astype(f)
    co, si = np.cos(ang).T.astype(f), np.sin(ang).T.astype(f)
    con[64:96, 704:960] = 1.0
    con[64:96, 960:1472] = np.concatenate([co, co])
    con[96:128, 960:1472] = np.concatenate([-si, si])
    s_, t_ = np.arange(128)[:, None], np.arange(128)[None, :]
    mk = np.zeros((128, 7, 128), f)
    mk[:, 0] = s_ == t_
    for lv in range(1, 7):
        h, b = 1 << (lv - 1), 1 << lv
        mk[:, lv] = ((s_ // b == t_ // b) & (s_ % b < h) & (t_ % b >= h))
    return con, mk.reshape(128, 7 * 128)


def kernel(_stop=None, **inputs):
    import numpy as _np
    import concourse.bacc as _bacc
    from concourse import mybir as _mybir
    from concourse.bass_utils import run_bass_kernel_spmd as _run

    nc = _bacc.Bacc("TRN2", target_bir_lowering=False, num_devices=1)
    arrays, args = {}, {}
    con, mk = shape_constants()
    for name, a in [(n, inputs[n]) for n in _INS] + [("consts", con), ("masks", mk)]:
        a = _np.ascontiguousarray(a)
        arrays[f"in_{name}"] = a
        args[name] = nc.dram_tensor(f"in_{name}", a.shape, _mybir.dt.from_np(a.dtype), kind="ExternalInput").ap()
    out = nc.dram_tensor("out_0", (1, S, D), _mybir.dt.float32, kind="ExternalOutput").ap()
    build(nc, args, out, args.pop("consts"), args.pop("masks"), _stop)
    r = _run(nc, [arrays], core_ids=[0])
    return r.results[0]["out_0"]
```

```python
import numpy as np
from contextlib import ExitStack
import concourse.bass as bass
from concourse import mybir

F32 = mybir.dt.float32
F32R = mybir.dt.float32r
U8 = mybir.dt.uint8
ALU = mybir.AluOpType
ACTF = mybir.ActivationFunctionType
AX = mybir.AxisListType
MUL, ADD, SUB = ALU.mult, ALU.add, ALU.subtract

S = 512
D = 1024
EPS1 = 1e-6
EPS2 = 1e-5
ALPHA = 2 ** 0.25
SCALE = 96 ** -0.5
NCTX = 256
NKEY = NCTX + S

PARAMS = [("c", 8), ("norm_pre_w", 8), ("ada_b", 24), ("pool_scale", 8), ("hgrn_lower_bounds", 8),
          ("hgrn_norm_w", 1), ("norm_post_w", 8), ("c_2", 8), ("c_ctx_2", 8), ("conv_dw_b_2", 4),
          ("conv_ln_g_2", 4), ("conv_ln_b_2", 4), ("q_norm_g_2", 3), ("kv_norm_g_2", 2), ("b_o_2", 8),
          ("ln1_g_2", 8), ("ln1_b_2", 8), ("b_ada_2", 48), ("ffn_dw_b_2", 44), ("b_down_2", 8),
          ("ln2_g_2", 8), ("ln2_b_2", 8), ("conv_dw_w_2", 124), ("ffn_dw_w_2", 132)]
NPAR = sum(n for _, n in PARAMS)


def stream_layout():
    items = []

    def w(*blocks):
        items.append(("w", list(blocks)))

    later = [("a", ("ada_w", 0, 4 * half, 4, [(512 * g, 512)]), g, half) for g in (4, 5) for half in range(2)]
    later += [("a", ("w_ada_2", 0, 4 * half, 4, [(512 * g, 512)]), g, half) for g in range(12) for half in range(2)]

    def also():
        if later:
            items.append(later.pop(0))

    for g in range(4):
        for half in range(2):
            items.append(("a", ("ada_w", 0, 4 * half, 4, [(512 * g, 512)]), g, half))
    U0, GP0, Q_0, F0, I0, GH0 = (1024 * i for i in range(6))
    for h in range(8):
        w(("w_in", 0, 0, 8, [(I0 + h * 128, 128)]), ("w_in", 0, 0, 8, [(F0 + h * 128, 128)]))
        also()
        w(("w_in", 0, 0, 8, [(Q_0 + h * 128, 128)]), ("w_in", 0, 0, 8, [(GH0 + h * 128, 128)]))
        also()
    for g in range(4):
        w(*[("w_in", 0, 0, 8, [(GP0 + (2 * g + m) * 128, 128)]) for m in range(2)])
        also()
        w(*[("w_in", 0, 0, 8, [(U0 + (2 * g + m) * 128, 128)]) for m in range(2)])
        w(*[("pool_w", (0, g), 0, 2, [(m * 128, 128)]) for m in range(2)])
        also()
    for m in range(8):
        w(*[("w_out", 0, 8 * half, 8, [(m * 128, 128)]) for half in range(2)])
        also()
    while later:
        also()
    for j in range(4):
        w(("w_in_2", 0, 0, 8, [(j * 128, 128)]), ("w_in_2", 0, 0, 8, [(512 + j * 128, 128)]))
    w(*[("w_in_2", 0, 0, 8, [(1024 + 128 * m, 128)]) for m in range(2)])
    w(*[("w_in_2", 0, 0, 8, [(1280 + 128 * m, 128)]) for m in range(2)])
    w(("w_in_2", 0, 0, 8, [(1536, 128)]),
      ("w_in_2", 0, 0, 8, [(1664, 32), (1664, 32), (1664, 32), (1680, 16), (1664, 16)]))
    for g in range(2):
        w(*[("w_uq_2", 0, 0, 3, [(h * 96, 96), (h * 96 + 80, 16), (h * 96 + 64, 16)])
            for h in range(4 * g, 4 * g + 4)])
        w(*[("w_ukv_2", 0, 0, 2, [(h * 128, 64), (h * 128 + 128, 64)]) for h in (4 * g, 4 * g + 2)],
          ("w_ukv_2", 0, 0, 2, [(h * 128 + 64, 64) for h in range(4 * g, 4 * g + 4)]))
    for c in range(4):
        w(*[("w_o_2", 0, 0, 8, [((2 * c + m) * 128, 128)]) for m in range(2)])
    for j in range(22):
        w(*[("w_up_2", 0, 0, 8, [(2816 * m + j * 128, 128)]) for m in range(2)])
    for c in range(4):
        for r0, nk in ((0, 8), (8, 7), (15, 7)):
            w(*[("w_down_2", 0, r0, nk, [((2 * c + m) * 128, 128)]) for m in range(2)])
    return items


def block_size(b):
    return b[3] * sum(n for _, n in b[4])


class Tok:

    def __init__(self, eng, i):
        self.eng, self.i = eng, i


class DTok:

    def __init__(self, sem, val):
        self.sem, self.val = sem, val


def flat(ws):
    out = []
    for w in ws:
        if w is None:
            continue
        if isinstance(w, (list, tuple)):
            out += flat(w)
        else:
            out.append(w)
    return out


class Prog:

    ENG = ("pe", "act", "dve", "pool", "sp")

    def __init__(self, sems):
        self.sems = sems
        self.q = {e: [] for e in self.ENG}
        self.dcount = {}

    def op(self, eng, fn, *ws):
        self.q[eng].append([flat(ws), fn, False])
        return Tok(eng, len(self.q[eng]) - 1)

    def dma(self, eng, out, in_, sem, *ws):
        n = self.dcount.get(id(sem), 0) + 16
        self.dcount[id(sem)] = n
        self.q[eng].append([flat(ws), lambda e: e.dma_start(out, in_).then_inc(sem, 16), None])
        return DTok(sem, n)

    def number(self):
        for e in self.ENG:
            for ws, _, _ in self.q[e]:
                for w in ws:
                    if isinstance(w, Tok):
                        self.q[w.eng][w.i][2] = True
        self.val = {}
        for e in self.ENG:
            n, vals = 0, []
            for it in self.q[e]:
                n += it[2] is True
                vals.append(n)
            self.val[e] = vals

    def emit(self, name, e):
        seen = {}
        for ws, fn, inc in self.q[name]:
            for w in ws:
                if isinstance(w, Tok):
                    sem, v = self.sems[w.eng], self.val[w.eng][w.i]
                else:
                    sem, v = w.sem, w.val
                if seen.get(id(sem), 0) < v:
                    e.wait_ge(sem, v)
                    seen[id(sem)] = v
            if fn is None:
                continue
            ins = fn(e)
            if inc:
                ins.then_inc(self.sems[name], 1)


class Ring:

    def __init__(self, bufs):
        self.bufs, self.n = bufs, 0
        self.free = [[] for _ in bufs]

    def take(self):
        i = self.n % len(self.bufs)
        self.n += 1
        f, self.free[i] = self.free[i], None
        assert f is not None
        return i, self.bufs[i], f

    def skip(self, i):
        self.n = i

    def even(self):
        self.n += self.n % 2

    def give(self, i, *toks):
        self.free[i] = flat(toks)


def build(nc, A, out, consts, masks, stop=None):
    LAY = stream_layout()

    ctx = ExitStack()
    with ctx:
        def sb(name, shape, dt=F32, c=ctx):
            return c.enter_context(nc.sbuf_tensor(name, shape, dt))

        sems = {e: ctx.enter_context(nc.semaphore("s_" + e)) for e in Prog.ENG}
        P = Prog(sems)
        s_par = ctx.enter_context(nc.semaphore("s_par"))
        s_con = ctx.enter_context(nc.semaphore("s_con"))
        s_msk = ctx.enter_context(nc.semaphore("s_msk"))
        s_out = ctx.enter_context(nc.semaphore("s_out"))
        s_c = ctx.enter_context(nc.semaphore("s_c"))
        s_x = [ctx.enter_context(nc.semaphore(f"s_x{i}")) for i in range(4)]
        NRAW = 3
        s_raw = [ctx.enter_context(nc.semaphore(f"s_raw{i}")) for i in range(NRAW)]

        def T(fn, *w):
            return P.op("pe", fn, *w)

        def C(fn, *w):
            return P.op("act", fn, *w)

        def V(fn, *w):
            return P.op("dve", fn, *w)

        def G(fn, *w):
            return P.op("pool", fn, *w)

        def mm(o, l, r, st, sp, *w, skip=False):
            return T(lambda e: e.matmul(o, l, r, start=st, stop=sp, skip_group_check=skip), *w)

        def tr(o, i, idn, *w):
            return T(lambda e: e.transpose(o, i, idn), *w)

        def act(o, i, f, *w, bias=0.0, scale=1.0, acc=None):
            if acc is not None:
                return C(lambda e: e.activation(o, i, f, bias=bias, scale=scale, accum_out=acc), *w)
            if f == ACTF.Copy:
                return C(lambda e: e.activation(o, i, f), *w)
            return C(lambda e: e.activation(o, i, f, bias=bias, scale=scale), *w)

        def tt(q, o, a, b, op, *w):
            return q(lambda e: e.tensor_tensor(o, a, b, op), *w)

        def ts(q, o, a, s1, s2, o1, o2, *w):
            if s2 is None:
                return q(lambda e: e.tensor_scalar(o, a, s1, None, o1), *w)
            return q(lambda e: e.tensor_scalar(o, a, s1, s2, o1, o2), *w)

        def stt(o, a, s, b, o1, o2, *w):
            return V(lambda e: e.scalar_tensor_tensor(out=o, in0=a, scalar=s, in1=b, op0=o1, op1=o2), *w)

        def cp(q, o, i, *w):
            return q(lambda e: e.tensor_copy(o, i), *w)

        IDN = sb("IDN", [128, 128])
        ONES = sb("ONES", [128, 128])
        NPOW = sb("NPOW", [128, 8])
        PC = sb("PC", [128, NPAR])
        PX = sb("PX", [128, 208])
        SCT = sb("SCT", [128, 64])
        RAW = [sb(f"RAW{i}", [128, 2048]) for i in range(NRAW)]
        WH = [sb(f"WH{i}", [128, 1024], F32R) for i in range(4)]
        WL = [sb(f"WL{i}", [128, 1024], F32R) for i in range(4)]
        XL = sb("XL", [128, 8, S])
        DG = sb("DG", [128, 512])
        PB = [ctx.enter_context(nc.psum_tensor(f"PB{i}", [128, 1024], F32)) for i in range(4)]
        bank = [PB[i // 2][:, (i % 2) * 512:(i % 2) * 512 + 512] for i in range(8)]

        COL, r = {}, 0
        for name, n in PARAMS:
            COL[name] = r
            r += n

        def col(name, j=0, n=1):
            return PC[:, COL[name] + j:COL[name] + j + n]

        npx = [0]

        def newcols(n):
            a = npx[0]
            npx[0] += n
            assert npx[0] <= 208
            return PX[:, a:a + n]

        par_t = P.dma("act", PC[:, :], A["params"][:, :], s_par)
        c_dma = P.dma("act", IDN[:, :], consts[:, 0:128], s_con)
        on_t = G(lambda e: e.memset(ONES[:, :], 1.0))
        np_t = G(lambda e: e.memset(NPOW[:, :], -0.5))

        mainr = Ring(bank[0:4])
        auxr = Ring(bank[4:8])

        offs, at = [], 0
        for it in LAY:
            n = block_size(it[1]) if it[0] == "a" else sum(block_size(b) for b in it[1])
            offs.append((at, n))
            at += 128 * n

        class Stream:

            def __init__(s):
                s.nd = s.np = s.nb = s.nw = s.ready = s.at = 0
                s.rfree = [[] for _ in range(NRAW)]
                s.tok, s.part = {}, []
                s.wfree = [[], [], [], []]
                s.wready = {}
                s.limit = 0

            def fetch(s):
                while s.nd < len(LAY) and s.nd < s.np + NRAW:
                    i = s.nd % NRAW
                    o, n = offs[s.nd]
                    src = A["wstream"][o:o + 128 * n].rearrange("(p n) -> p n", p=128)
                    s.tok[s.nd] = P.dma("sp", RAW[i][:, 0:n], src, s_raw[i], s.rfree[i])
                    s.nd += 1

            def pump(s):
                s.fetch()
                while s.np < len(LAY):
                    it = LAY[s.np]
                    i = s.np % NRAW
                    raw, tok = RAW[i], s.tok[s.np]
                    if it[0] == "w":
                        h = s.nw % 4
                        free = s.wfree[h]
                        if free is None:
                            return
                        n = block_size(it[1][s.nb])
                        src = raw[:, s.at:s.at + n]
                        s.wfree[h] = None
                        a = act(WH[h][:, 0:n], src, ACTF.Copy, tok, free)
                        v = tt(V, WL[h][:, 0:n], src, WH[h][:, 0:n].bitcast(F32), SUB, a, free)
                        s.wready[s.nw] = [a, v]
                        s.part += [a, v]
                        s.nw += 1
                        s.nb += 1
                        s.at += n
                        if s.nb < len(it[1]):
                            continue
                        s.rfree[i], s.part, s.nb, s.at = s.part, [], 0, 0
                    else:
                        s.rfree[i] = flat([ada_item(it, raw, tok)])
                    s.np += 1
                    s.fetch()

            def next(s):
                n = s.ready
                s.ready += 1
                return n % 4, WH[n % 4], WL[n % 4], s.wready[n]

            def done(s, h, tok):
                s.wfree[h] = [tok]
                s.pump()

        st = Stream()

        def mm3(o, lh, ll, rh, rl, first, last, *w, skip=False):
            mm(o, lh, rh, first, False, *w, skip=skip)
            mm(o, lh, rl, False, False, skip=skip)
            return mm(o, ll, rh, False, last, skip=skip)

        sct = Ring([SCT[:, 16 * i:16 * i + 16] for i in range(4)])

        def diag_bcast(cols, nt, dgfree, *w):
            ds = []
            for j in range(nt):
                ds.append(ts(V, DG[:, j * 128:(j + 1) * 128], IDN[:, :], cols[:, j:j + 1], None, MUL, None, w, dgfree))
            b, bk, bf = auxr.take()
            t = mm(bk[:, 0:nt * 128], ONES[:, :], DG[:, 0:nt * 128], True, True, ds[-1], bf)
            return b, bk, t

        dgf = [None]

        def stat_cols(accs, nt, *w):
            b, bk, bf = auxr.take()
            t = None
            for a, acc in enumerate(accs):
                for j in range(nt):
                    t = mm(bk[:, a * 4 + j:a * 4 + j + 1], acc[:, j * 128:(j + 1) * 128], ONES[:, 0:1],
                           True, True, w, bf)
            return b, bk, t

        def rms_bcast(acc, nt, n, eps, *w):
            b, bk, t = stat_cols([acc], nt, w)
            si, sc, sf = sct.take()
            v = ts(V, sc[:, 0:nt], bk[:, 0:nt], 1.0 / n, eps, MUL, ADD, t, sf)
            auxr.give(b, v)
            g = G(lambda e: e.tensor_tensor(sc[:, 4:4 + nt], sc[:, 0:nt], NPOW[:, 0:nt], ALU.pow), v, np_t)
            b2, bk2, t2 = diag_bcast(sc[:, 4:4 + nt], nt, dgf[0], g)
            dgf[0] = t2
            sct.give(si, t2)
            return b2, bk2, t2, t

        def ln_bcast(s1, s2, nt, n, eps, *w):
            b, bk, t = stat_cols([s1, s2], nt, w)
            si, sc, sf = sct.take()
            m, v, r, q = (sc[:, 4 * i:4 * i + nt] for i in range(4))
            a1 = ts(V, m, bk[:, 0:nt], 1.0 / n, None, MUL, None, t, sf)
            a2 = ts(V, v, bk[:, 4:4 + nt], 1.0 / n, eps, MUL, ADD, t)
            auxr.give(b, a2)
            a3 = tt(V, q, m, m, MUL, a1)
            a4 = tt(V, v, v, q, SUB, a3, a2)
            g = G(lambda e: e.tensor_tensor(r, v, NPOW[:, 0:nt], ALU.pow), a4, np_t)
            b1, bk1, t1 = diag_bcast(r, nt, dgf[0], g)
            a5 = stt(q, m, -1.0, r, MUL, MUL, g)
            b2, bk2, t2 = diag_bcast(q, nt, t1, a5)
            dgf[0] = t2
            sct.give(si, t2)
            return (b1, bk1, t1), (b2, bk2, t2), t

        def cols_of_acc(dst, acc, n, bias, *w):
            b, bk, bf = auxr.take()
            for j in range(n):
                t = mm(bk[:, j:j + 1], acc[:, j * 128:(j + 1) * 128], ONES[:, 0:1], True, True, w, bf)
            v = tt(V, dst, bk[:, 0:n], bias, ADD, t)
            auxr.give(b, v)
            return t, v

        c1 = ExitStack()
        SM = sb("SM", [128, 512], F32, c1)
        FAC = sb("FAC", [128, 64], F32, c1)
        MK = sb("MK", [128, 7 * 128], U8, c1)
        CC = sb("CC", [128, 24], F32, c1)
        ACC = sb("ACC", [128, 2, 512], F32, c1)
        HH = sb("HH", [128, 8, S], F32R, c1)
        HL = sb("HL", [128, 8, S], F32R, c1)
        MPH = sb("MPH", [128, 8, S], F32R, c1)
        MPL = sb("MPL", [128, 8, S], F32R, c1)
        DH = sb("DH", [128, 2, S], F32R, c1)
        DL = sb("DL", [128, 2, S], F32R, c1)
        HB = sb("HB", [128, 10, S], F32, c1)
        GP = sb("GP", [128, 2, S], F32, c1)
        AT = sb("AT", [128, S], F32, c1)
        KDT = sb("KDT", [128, S], F32, c1)
        E0 = sb("E0", [128, S], F32, c1)
        Q0 = sb("Q0", [128, S], F32, c1)
        SS = sb("SS", [128, 7, 128], F32, c1)
        XR = [sb(f"XR{i}", [128, S], F32, c1) for i in range(4)]
        UPA = sb("UPA", [128, 3 * (16 + S)], F32, c1)
        UP = [UPA[:, i * (16 + S):(i + 1) * (16 + S)] for i in range(3)]
        xr = Ring([x[:, :] for x in XR])
        XT = XL

        P.dma("act", HB[:, 0:2, :].rearrange("p a n -> p (a n)")[:, 0:896], masks[:, :], s_msk)
        P.dma("act", SM[:, :], consts[:, 128:640], s_msk)
        m_dma = P.dma("act", FAC[:, :], consts[:, 640:704], s_msk)
        mk_t = cp(G, MK[:, :], HB[:, 0:2, :].rearrange("p a n -> p (a n)")[:, 0:896], m_dma)

        xsrc = A["xT"].rearrange("(k p) t -> p k t", p=128)
        x_t = [P.dma("sp", XT[:, 4 * i:4 * i + 4, :], xsrc[:, 4 * i:4 * i + 4, :], s_x[i]) for i in range(2)]
        M1 = newcols(24)
        M2 = newcols(48)
        MC = newcols(16)
        accf = [[], []]
        mod_t = {}
        acc_prev = [None, None]
        deferred = []

        def defer(n, fn):
            deferred.append([n, fn])

        def run_deferred(every=False):
            for d in deferred:
                d[0] -= 1
            while deferred and (every or deferred[0][0] <= 0):
                deferred.pop(0)[1]()

        cc_t = [act(CC[:, 0:8], col("c", 0, 8), ACTF.Silu, par_t),
                act(CC[:, 8:24], col("c_2", 0, 16), ACTF.Silu, par_t)]
        def ada_item(it, raw, tok):
            _, (name, *_), g, half = it
            w = raw[:, :].rearrange("p (k n) -> p k n", n=512)
            vecs = [0] if name == "ada_w" else [8, 16] if g < 4 else [8]
            if half == 0:
                run_deferred(True)
            last = None
            for k in range(4):
                kk = 4 * half + k
                for vi, cb in enumerate(vecs):
                    a, cs = ACC[:, vi, :], CC[:, cb + kk:cb + kk + 1]
                    if kk == 0:
                        last = ts(V, a, w[:, k, :], cs, None, MUL, None, tok, cc_t, accf[vi])
                    else:
                        last = stt(a, w[:, k, :], cs, a, MUL, ADD, tok, acc_prev[vi])
                    acc_prev[vi] = last
            if half == 1:
                def sums():
                    for vi in range(len(vecs)):
                        if name == "ada_w":
                            dst, bias = M1, "ada_b"
                        else:
                            dst, bias = (M2, MC)[vi], "b_ada_2"
                        t, v = cols_of_acc(dst[:, 4 * g:4 * g + 4], ACC[:, vi, :], 4, col(bias, 4 * g, 4),
                                           acc_prev[vi], on_t)
                        accf[vi] = [t]
                        key = "1s" if name == "ada_w" and g < 4 else "1g" if name == "ada_w" else "2"
                        mod_t[key] = [mod_t.get(key), v]
                if name == "ada_w" and g < 4:
                    sums()
                else:
                    defer(4, sums)
            return last

        LB, LT, OML = newcols(8), newcols(8), newcols(8)
        hlb = col("hgrn_lower_bounds", 0, 8)
        v1 = tt(V, LT, hlb, hlb, SUB, par_t)
        v2 = act(LT, LT, ACTF.Exp, v1)
        v3 = V(lambda e: e.reciprocal(OML, LT), v2)
        v4 = tt(V, LT, LT, OML, MUL, v3)
        v5 = tt(V, LB, LT, LT, SUB, v4)
        lb_t = ts(V, OML, LB, -1.0, 1.0, MUL, ADD, v5)
        pad_t = None
        for u in UP:
            pad_t = G(lambda e, u=u: e.memset(u[:, 0:16], 0.0))

        xb, xbk, xbf = auxr.take()
        pa = None
        for k in range(8):
            xi, x, xf = xr.take() if k else (None, Q0[:, :], None)
            a = act(x, XT[:, k, :], ACTF.Square, x_t[k // 4], xf)
            if k:
                pa = tt(V, Q0[:, :], Q0[:, :], x, ADD, a, pa or a0)
                xr.give(xi, pa)
            else:
                a0 = a
        for j in range(4):
            t = mm(xbk[:, j:j + 1], Q0[:, j * 128:(j + 1) * 128], ONES[:, 0:1], True, True, pa, on_t, xbf)
        si, sc, sf = sct.take()
        v = ts(V, sc[:, 0:4], xbk[:, 0:4], 1.0 / D, EPS1, MUL, ADD, t)
        auxr.give(xb, v)
        g_ = G(lambda e: e.tensor_tensor(sc[:, 4:8], sc[:, 0:4], NPOW[:, 0:4], ALU.pow), v, np_t)
        b, rb, t = diag_bcast(sc[:, 4:8], 4, None, g_, on_t, c_dma)
        dgf[0] = t
        sct.give(si, t)
        n_toks = [tt(V, XT[:, k, :], XT[:, k, :], rb, MUL, t, a) for k in range(8)]
        auxr.give(b, n_toks[-1])
        st.pump()
        A1, G1 = newcols(8), newcols(8)
        v = ts(V, A1, M1[:, 8:16], 1.0, None, ADD, None, mod_t["1s"])
        a1_t = tt(V, A1, A1, col("norm_pre_w", 0, 8), MUL, v)

        def split_later(dh, dl, src, q, *w):
            a = act(dh, src, ACTF.Copy, w)
            r = [a]
            q.append(lambda: r.append(tt(V, dl, src, dh.bitcast(F32), SUB, a, w)))
            if len(q) > 1:
                q.pop(0)()
            return r

        def flush(q):
            while q:
                q.pop(0)()

        h_toks, lq = [], []
        for k in range(8):
            v = ts(V, XT[:, k, :], XT[:, k, :], A1[:, k:k + 1], M1[:, k:k + 1], MUL, ADD, a1_t, n_toks[k])
            h_toks.append(split_later(HH[:, k, :], HL[:, k, :], XT[:, k, :], lq, v))
        flush(lq)
        xt_free = h_toks[-1]

        ticks = []

        def tick():
            run_deferred()
            if ticks:
                try:
                    next(ticks[0])
                except StopIteration:
                    ticks.pop(0)

        def block(bk, wh, wl, xh, xl, nk, wtoks, xtoks, bf, tk=(), first=True, last=True):
            t = None
            for k in range(nk):
                t = mm3(bk, wh(k), wl(k), xh(k), xl(k), first and k == 0, last and k == nk - 1,
                        wtoks, xtoks[k] if xtoks else None, bf)
                if k in tk:
                    tick()
            return t

        def wk(w, m=128, c0=0):
            return lambda k: w[:, c0 + k * m:c0 + k * m + m]

        def block1(xh_, xl_, nk, xtoks, tk=(), n=S, first=True, last=True, bnk=None):
            w, wh, wl, wt = st.next()
            b, bk, bf = bnk or mainr.take()
            t = block(bk[:, 0:n], wk(wh), wk(wl), xh_, xl_, nk, wt, xtoks, bf, tk, first, last)
            st.done(w, t)
            return b, bk, t

        def blocks3(xh_, xl_, xtoks):
            ws = [st.next() for _ in range(3)]
            bs = [mainr.take() for _ in range(3)]
            t = [None] * 3
            for k in range(8):
                for i in range(3):
                    (_, wh, wl, wt), (_, bk, bf) = ws[i], bs[i]
                    t[i] = mm3(bk, wk(wh)(k), wk(wl)(k), xh_(k), xl_(k), k == 0, k == 7, wt, xtoks[k], bf)
            for i in range(3):
                st.done(ws[i][0], t[i])
            return [(bs[i][0], bs[i][1], t[i]) for i in range(3)]

        hh = lambda k: HH[:, k, :]
        hl = lambda k: HL[:, k, :]

        MKv = MK[:, :].rearrange("p (l n) -> p l n", n=128)
        buf = {"AT": None, "KDT": None, "E0": None, "Q0": None, "SS": None}
        hfree = [dict(v=mk_t, k=mk_t), dict()]
        oh_t = {}

        def zhead(h):
            p = h % 2
            Vb, Kb, Bb, Qb, Gb = (HB[:, 5 * p + i, :] for i in range(5))
            fr = hfree[p]
            r = {}
            TK = (1, 3, 5, 7)
            three = blocks3(hh, hl, h_toks) if h == 0 else None
            b, bk, t = three.pop(0) if h == 0 else block1(hh, hl, 8, None, TK)
            r["v"] = act(Vb, bk, ACTF.Copy, t, fr.get("v"))
            mainr.give(b, r["v"])
            b, bk, t = three.pop(0) if h == 0 else block1(hh, hl, 8, None, TK)
            xi, x, xf = xr.take()
            s_ = act(Kb, bk, ACTF.Sigmoid, t, fr.get("k"))
            mainr.give(b, s_)
            f_ = ts(V, Kb, Kb, OML[:, h:h + 1], LB[:, h:h + 1], MUL, ADD, s_, lb_t)
            l_ = act(x, Kb, ACTF.Ln, f_, xf)
            r["k"] = ts(V, Kb, Kb, -1.0, 1.0, MUL, ADD, l_)
            r["b"] = V(lambda e: e.tensor_tensor_scan(Bb, SM[:, :], x, 0.0, MUL, ADD), l_, m_dma, fr.get("b"))
            xr.give(xi, r["b"])
            b, bk, t = three.pop(0) if h == 0 else block1(hh, hl, 8, None, TK)
            r["q"] = act(Qb, bk, ACTF.Copy, t, fr.get("q"))
            mainr.give(b, r["q"])
            b, bk, t = block1(hh, hl, 8, None, TK)
            r["g"] = act(Gb, bk, ACTF.Silu, t, fr.get("g"))
            mainr.give(b, r["g"])
            return r

        def hgrn(h, r):
            p = h % 2
            Vb, Kb, Bb, Qb, Gb = (HB[:, 5 * p + i, :] for i in range(5))
            ats = G(lambda e: e.memset(AT[:, :], 0.0), buf["AT"])
            last_cp = [ats]
            pend = []

            def ew(l):
                half, blk = 1 << (l - 1), 1 << l
                Bv, Kv, Qv = (z.rearrange("p (n b) -> p n b", b=blk) for z in (Bb, Kb, Qb))
                xi, x, xf = xr.take()
                Xv = x.rearrange("p (n b) -> p n b", b=blk)
                ref = Bv[:, :, half - 1:half].broadcast_to([128, 512 // blk, half])
                g1 = tt(G, Xv[:, :, half:blk], Bv[:, :, half:blk], ref, SUB, r["b"], xf)
                g2 = tt(G, Xv[:, :, 0:half], ref, Bv[:, :, 0:half], SUB, r["b"], xf)
                a = act(x, x, ACTF.Exp, g1, g2)
                v1 = tt(V, Xv[:, :, half:blk], Xv[:, :, half:blk], Qv[:, :, half:blk], MUL, a, r["q"])
                v2 = tt(V, Xv[:, :, 0:half], Xv[:, :, 0:half], Kv[:, :, 0:half], MUL, a, r["k"])
                pend.append((l, xi, x, [v1, v2]))

            def sc(l, xi, x, toks):
                b, bk, bf = auxr.take()
                for j in range(4):
                    js = slice(j * 128, (j + 1) * 128)
                    lo = Kb[:, js] if l == 0 else x[:, js]
                    ro = Qb[:, js] if l == 0 else x[:, js]
                    t = mm(bk[:, js], lo, ro, True, True, toks, bf)
                if xi is not None:
                    xr.give(xi, t)
                half, blk = (0, 128) if l == 0 else (1 << (l - 1), 1 << l)
                o, d = (z.rearrange("p (j n b) -> p j n b", n=128 // blk, b=blk)[:, :, :, half:blk]
                        for z in (AT[:, :], bk))
                m = MKv[:, l, :].rearrange("p (j n b) -> p j n b", j=1, b=blk)[:, :, :, half:blk]\
                    .broadcast_to([128, 4, 128 // blk, blk - half])
                last_cp[0] = V(lambda e: e.copy_predicated(o, m, d), t, last_cp[0], mk_t)
                auxr.give(b, last_cp[0])
                return t

            ew(1)
            b, bk, bf = auxr.take()
            for j in range(4):
                js = slice(j * 128, (j + 1) * 128)
                t = tr(bk[:, js], Vb[:, js], IDN[:, :], r["v"], bf)
            v_t = act(Vb, bk, ACTF.Copy, t)
            auxr.give(b, v_t)
            yield
            ew(2)
            sc(0, None, None, [r["k"], r["q"]])
            yield
            for l in range(3, 7):
                ew(l)
                sc(*pend.pop(0))
                yield
            a = act(E0[:, :], Bb, ACTF.Exp, r["b"], buf["E0"])
            q0 = tt(V, Q0[:, :], E0[:, :], Qb, MUL, a, r["q"], buf["Q0"])
            e0_t = a
            sc(*pend.pop(0))
            xi, x, xf = xr.take()
            Bv = Bb.rearrange("p (n b) -> p n b", b=64)
            Xv = x.rearrange("p (n b) -> p n b", b=64)
            g = tt(G, Xv, Bv[:, :, 63:64].broadcast_to([128, 8, 64]), Bv, SUB, r["b"], xf)
            a = act(x, x, ACTF.Exp, g)
            kd = tt(V, x, x, Kb, MUL, a, r["k"])
            yield
            sc(*pend.pop(0))
            hfree[p]["b"] = [a, e0_t]
            hfree[p]["k"] = kd
            b, bk, bf = auxr.take()
            for j in range(4):
                js = slice(j * 128, (j + 1) * 128)
                t = tr(bk[:, js], x[:, js], IDN[:, :], kd, bf)
            xr.give(xi, t)
            hfree[p]["k"] = [kd, t]
            kt = act(KDT[:, :], bk, ACTF.Copy, t, buf["KDT"])
            auxr.give(b, kt)
            yield
            ob, obk, obf = auxr.take()
            for j in range(4):
                js = slice(j * 128, (j + 1) * 128)
                mm(obk[:, js], Vb[:, js], AT[:, js], j == 0, False, last_cp[0], v_t, obf, skip=True)
            yield
            prev = None
            kb_ = [auxr.take() for _ in range(2)]
            kt_ = [None, None]
            for c in range(7):
                rs = slice((c % 2) * 64, (c % 2) * 64 + 64)
                js = slice((c // 2) * 128, (c // 2) * 128 + 128)
                kt_[c % 2] = mm(kb_[c % 2][1][:, js], KDT[rs, js], Vb[rs, js], True, True, kt, v_t, kb_[c % 2][2])
            yield
            for c in range(7):
                kv = kb_[c % 2][1][:, (c // 2) * 128:(c // 2) * 128 + 128]
                if c == 0:
                    prev = cp(V, SS[:, 0, :], kv, kt_, buf["SS"])
                else:
                    prev = stt(SS[:, c, :], SS[:, c - 1, :], E0[:, 64 * c + 63:64 * c + 64], kv, MUL, ADD,
                               prev, e0_t)
            auxr.give(kb_[0][0], prev)
            auxr.give(kb_[1][0], prev)
            t = kt_
            yield
            buf["KDT"] = t
            buf["E0"] = [prev, q0]
            b, bk = ob, obk
            for c in range(1, 8):
                t = mm(bk[:, c * 64:c * 64 + 64], SS[:, c - 1, :], Q0[:, c * 64:c * 64 + 64], False, c == 7,
                       prev, q0, skip=True)
            buf["AT"] = buf["SS"] = buf["Q0"] = t
            hfree[p]["v"] = t
            hfree[p]["q"] = t
            xi, x, xf = xr.take()
            o = act(XT[:, h, :], bk, ACTF.Copy, t, xt_free)
            sq = act(x, bk, ACTF.Square, t, xf)
            auxr.give(b, sq)
            yield
            b, bk, t = stat_cols([x], 4, sq)
            xr.give(xi, t)
            si, sc_, sf = sct.take()
            v = ts(V, sc_[:, 0:4], bk[:, 0:4], 1.0 / 128, EPS1, MUL, ADD, t, sf)
            auxr.give(b, v)
            g = G(lambda e: e.tensor_tensor(sc_[:, 4:8], sc_[:, 0:4], NPOW[:, 0:4], ALU.pow), v, np_t)
            yield
            rb_, rbk, rt = diag_bcast(sc_[:, 4:8], 4, dgf[0], g)
            dgf[0] = rt
            sct.give(si, rt)
            yield
            v = stt(XT[:, h, :], XT[:, h, :], col("hgrn_norm_w"), rbk, MUL, MUL, rt, o)
            auxr.give(rb_, v)
            oh_t[h] = tt(G, XT[:, h, :], XT[:, h, :], Gb, MUL, v, r["g"])
            hfree[p]["g"] = oh_t[h]

        for h in range(8):
            r = zhead(h)
            while ticks:
                tick()
            ticks.append(hgrn(h, r))

        mix_t = {}
        gp_free, d_free = [None], [None]
        upf = [[], [], []]
        for g in range(4):
            gp_t = []
            for m in range(2):
                b, bk, t = block1(hh, hl, 8, None, (1, 3, 5, 7))
                a = act(GP[:, m, :], bk, ACTF.Silu, t, gp_free[0])
                mainr.give(b, a)
                gp_t.append(a)
            dt_ = []
            for m in range(2):
                b, bk, t = block1(hh, hl, 8, None, (1, 3, 5, 7))
                last_z = t
                u, s0, s1 = UP[0], UP[1], UP[2]
                a = act(u[:, 16:], bk, ACTF.Copy, t, upf[0])
                mainr.give(b, a)
                src, prev = u, a
                for i in range(g + 1):
                    d = 1 << i
                    dst = (s0, s1)[i % 2]
                    prev = tt(G, dst[:, 16:], src[:, 16:], src[:, 16 - d:528 - d], ADD, prev, pad_t, upf[1 + i % 2])
                    src = dst
                wd = 2 << g
                prev = tt(V, src[:, 16:16 + wd], src[:, 16:16 + wd], FAC[:, 16 * g:16 * g + wd], MUL, prev, m_dma)
                prev = stt(src[:, 16:], src[:, 16:], 1.0 / wd, u[:, 16:], MUL, SUB, prev)
                a = act(DH[:, m, :], src[:, 16:], ACTF.Copy, prev, d_free[0])
                v = tt(V, DL[:, m, :], src[:, 16:], DH[:, m, :].bitcast(F32), SUB, a)
                upf = [[prev], [v], [v]]
                dt_.append([a, v])
            for m in range(2):
                b, bk, t = block1(lambda k: DH[:, k, :], lambda k: DL[:, k, :], 2, dt_)
                kk = 2 * g + m
                v = stt(GP[:, m, :], bk, col("pool_scale", kk), GP[:, m, :], MUL, MUL, t, gp_t[m])
                mainr.give(b, v)
                a = act(MPH[:, kk, :], GP[:, m, :], ACTF.Copy, v)
                v = tt(V, MPL[:, kk, :], GP[:, m, :], MPH[:, kk, :].bitcast(F32), SUB, a)
                gp_free[0] = v
                mix_t[kk] = [a, v]
            d_free[0] = t
        while ticks:
            tick()
        run_deferred(True)
        for h in range(8):
            mix_t[8 + h] = split_later(HH[:, h, :], HL[:, h, :], XT[:, h, :], lq, oh_t[h], last_z)
        flush(lq)
        XT2 = HB[:, 0:8, :]
        x2_t = [P.dma("sp", XT2[:, 4 * i:4 * i + 4, :], xsrc[:, 4 * i:4 * i + 4, :], s_x[2 + i], oh_t[6], oh_t[7],
                      list(hfree[0].values()), list(hfree[1].values())) for i in range(2)]
        xt_free = [mix_t[15]]

        def acc_stats(src, m, s1, s2, sq, stt_, toks):
            a = act(sq[1], src, ACTF.Square, toks, sq[2])
            if m == 0:
                t2 = cp(G, s2, sq[1], a, stt_.get("free"))
                t1 = cp(G, s1, src, toks, stt_.get("free")) if s1 is not None else None
            else:
                t2 = tt(G, s2, s2, sq[1], ADD, a, stt_["s2"])
                t1 = tt(G, s1, s1, src, ADD, toks, stt_["s1"]) if s1 is not None else None
            stt_["s1"], stt_["s2"] = t1, t2
            return [a, t2]

        y_t = []
        chain = {}
        S1, S2 = AT[:, :], Q0[:, :]
        for kk in range(8):
            bnk = mainr.take()
            block1(lambda k: MPH[:, k, :], lambda k: MPL[:, k, :], 8, [mix_t[k] for k in range(8)], (3, 7), last=False,
                   bnk=bnk)
            b, bk, t = block1(hh, hl, 8, [mix_t[8 + k] for k in range(8)], (3, 7), first=False, bnk=bnk)
            a = act(XT[:, kk, :], bk, ACTF.Copy, t, xt_free)
            mainr.give(b, a)
            y_t.append(a)
            xi, x, xf = xr.take()
            u = acc_stats(XT[:, kk, :], kk, None, S2, (xi, x, xf), chain, [a, buf["Q0"]])
            xr.give(xi, u)
        run_deferred(True)
        b, rb, t, _ = rms_bcast(S2, 4, D, EPS1, chain["s2"])
        g1_t = tt(V, G1, M1[:, 16:24], col("norm_post_w", 0, 8), MUL, mod_t["1g"])
        x1_t = []
        chain = {"free": [t, buf["AT"]]}
        for k in range(8):
            v = stt(XT[:, k, :], XT[:, k, :], G1[:, k:k + 1], rb, MUL, MUL, t, g1_t, y_t[k])
            v = tt(V, XT[:, k, :], XT[:, k, :], XT2[:, k, :], ADD, v, x2_t)
            x1_t.append(v)
            xi, x, xf = xr.take()
            u = acc_stats(XT[:, k, :], k, S1, S2, (xi, x, xf), chain, v)
            xr.give(xi, u)
        auxr.give(b, v)
        (b1, rb, t1), (b2, mb, t2), st_t = ln_bcast(S1, S2, 4, D, EPS2, chain["s1"], chain["s2"])
        xl_t = []
        for k in range(8):
            v = tt(V, XL[:, k, :], XL[:, k, :], rb, MUL, t1, x1_t[k], chain["s1"], chain["s2"])
            v = tt(V, XL[:, k, :], XL[:, k, :], mb, ADD, v, t2)
            xl_t.append(v)
        auxr.give(b1, v)
        auxr.give(b2, v)
        end1 = [v, t2]
        c1.close()
        assert not ticks
        if stop == 1:
            return finish(nc, ctx, P, A, out, XL, xl_t, IDN, mainr, s_out, ACTF, act, tr)

        cM = ExitStack()
        MH = sb("MH", [128, 8, S], F32R, cM)
        ML = sb("ML", [128, 8, S], F32R, cM)
        c2 = ExitStack()
        CH = sb("CH", [128, 6, 512], F32R, c2)
        CL = sb("CL", [128, 6, 512], F32R, c2)
        QG = sb("QG", [128, 4, S], F32, c2)
        KG = sb("KG", [128, 4, NKEY], F32, c2)
        VG = sb("VG", [128, 6, 256], F32, c2)
        KR = sb("KR", [128, NKEY], F32, c2)
        VP = sb("VP", [128, 4, S + 30], F32, c2)
        CV = sb("CV", [128, 4, S], F32, c2)
        OTm = sb("OTm", [128, 4, 512], F32, c2)
        PM = [sb(f"PM{i}", [128, NKEY], F32, c2) for i in range(2)]
        PT = [sb(f"PT{i}", [128, NKEY], F32, c2) for i in range(2)]
        CS = sb("CS", [128, NKEY], F32, c2)
        XC = KG[:, :, :].rearrange("p a n -> p (a n)")[:, 0:2048].rearrange("p (k n) -> p k n", n=NCTX)
        HCH = CH[:, 0:4, :].rearrange("p a n -> p (a n)").rearrange("p (k n) -> p k n", n=NCTX)
        HCL = CL[:, 0:4, :].rearrange("p a n -> p (a n)").rearrange("p (k n) -> p k n", n=NCTX)
        CQ = QG[:, 0:3, :]
        CKV = KG[:, 0:2, :]
        CKH, CKL = (z[:, 3:6, :].rearrange("p a n -> p (a n)").rearrange("p (k n) -> p k n", n=NKEY)
                    for z in (CH, CL))
        cs_t = P.dma("act", CS[:, :], consts[:, 704:704 + NKEY], s_msk, end1, st_t, *[xl_t])
        vp_t = [G(lambda e, a=a: e.memset(VP[:, :, a:a + 15], 0.0), end1, oh_t[7], chain["s2"]) for a in (0, S + 15)]

        SC1, SC2, SC1C = newcols(8), newcols(8), newcols(8)
        e1 = ts(V, SC1, M2[:, 8:16], 1.0, None, ADD, None, mod_t["2"])
        e2 = ts(V, SC2, M2[:, 32:40], 1.0, None, ADD, None, mod_t["2"])
        e3 = ts(V, SC1C, MC[:, 8:16], 1.0, None, ADD, None, mod_t["2"])
        csrc = A["ctxT"].rearrange("(k p) t -> p k t", p=128)
        xc_t = P.dma("sp", XC, csrc, s_c, end1)

        def split(dh, dl, src, *w):
            a = act(dh, src, ACTF.Copy, w)
            return [a, tt(V, dl, src, dh.bitcast(F32), SUB, a, w)]

        hc_t = []

        def ctx_norm():
            CS1, CS2, CSQ = PM[0][:, 0:NCTX], PM[1][:, 0:NCTX], PM[0][:, NCTX:2 * NCTX]
            a = act(CS2, XC[:, 0, :], ACTF.Square, xc_t, end1)
            c2_ = a
            c1_ = cp(G, CS1, XC[:, 0, :], xc_t, end1)
            for k in range(1, 8):
                a = act(CSQ, XC[:, k, :], ACTF.Square, c2_)
                c2_ = tt(G, CS2, CS2, CSQ, ADD, a)
                c1_ = tt(G, CS1, CS1, XC[:, k, :], ADD, c1_)
                yield
            b, bk, t = stat_cols([CS1, CS2], 2, c1_, c2_)
            stc = newcols(8)
            v1 = ts(V, stc[:, 0:2], bk[:, 0:2], 1.0 / D, None, MUL, None, t)
            v2 = ts(V, stc[:, 2:4], bk[:, 4:6], 1.0 / D, EPS2, MUL, ADD, t)
            auxr.give(b, v2)
            v3 = tt(V, stc[:, 4:6], stc[:, 0:2], stc[:, 0:2], MUL, v1)
            v4 = tt(V, stc[:, 2:4], stc[:, 2:4], stc[:, 4:6], SUB, v2, v3)
            g = G(lambda e: e.tensor_tensor(stc[:, 4:6], stc[:, 2:4], NPOW[:, 0:2], ALU.pow), v4)
            v5 = stt(stc[:, 6:8], stc[:, 0:2], -1.0, stc[:, 4:6], MUL, MUL, g)
            yield
            b1, rb, t1 = diag_bcast(stc[:, 4:6], 2, dgf[0], g)
            yield
            b2, mb, t2 = diag_bcast(stc[:, 6:8], 2, t1, v5)
            dgf[0] = t2
            for k in range(8):
                x = XC[:, k, :]
                v = tt(V, x, x, rb[:, 0:NCTX], MUL, t1, xc_t, c1_, a)
                v = tt(V, x, x, mb[:, 0:NCTX], ADD, v, t2)
                vl = v
                v = ts(V, x, x, SC1C[:, k:k + 1], MC[:, k:k + 1], MUL, ADD, v, e3)
                hc_t.append(split(HCH[:, k, :], HCL[:, k, :], x, v, end1))
                yield
            auxr.give(b1, vl)
            auxr.give(b2, vl)

        xw = Ring([x[:, 0:512] for x in PT])
        h2_t = []
        for k in range(8):
            si, x, sf = xw.take()
            v = ts(V, x, XL[:, k, :], SC1[:, k:k + 1], M2[:, k:k + 1], MUL, ADD, xl_t[k], e1, sf, end1)
            h2_t.append(split_later(MH[:, k, :], ML[:, k, :], x, lq, v, end1))
            xw.give(si)
            xw.free[si] = h2_t[-1]
        flush(lq)
        ticks.append(ctx_norm())
        mh = lambda k: MH[:, k, :]
        ml = lambda k: ML[:, k, :]

        def drain(n=10 ** 6):
            while ticks and n:
                tick()
                n -= 1

        va_t, conv_t = [], []

        def conv(j):
            v = ts(V, CV[:, j, :], VP[:, j, 0:S], col("conv_dw_w_2", j), col("conv_dw_b_2", j), MUL, ADD, va_t[j], vp_t)
            for k in range(1, 31):
                v = stt(CV[:, j, :], VP[:, j, k:k + S], col("conv_dw_w_2", 4 * k + j), CV[:, j, :], MUL, ADD, v)
                yield
            conv_t.append(v)

        TK8 = (0, 1, 2, 3, 4, 5, 6, 7)
        three = blocks3(mh, ml, h2_t)
        for j in range(4):
            b, bk, t = three.pop(0) if three else block1(mh, ml, 8, h2_t, TK8)
            b2, bk2, t2 = three.pop(0) if three else block1(mh, ml, 8, h2_t, TK8)
            a = act(VP[:, j, 15:15 + S], bk2, ACTF.Sigmoid, t2, end1)
            mainr.give(b2, a)
            v = tt(V, VP[:, j, 15:15 + S], VP[:, j, 15:15 + S], bk, MUL, a, t)
            mainr.give(b, v)
            va_t.append(v)
            ticks.append(conv(j))

        for _ in range(40):
            if len(hc_t) < 8:
                tick()
        x_free = [hc_t[-1]]
        cq_t, ckv_t = [], []
        hch, hcl = (lambda k: HCH[:, k, :]), (lambda k: HCL[:, k, :])

        def ctxb(w):
            b, bk, bf = mainr.take()
            t = block(bk[:, 0:NCTX], wk(w[1]), wk(w[2]), hch, hcl, 8, w[3], hc_t, bf)
            return b, bk[:, 0:NCTX], t

        def both(w):
            b, bk, bf = mainr.take()
            t = block(bk, wk(w[1]), wk(w[2]), mh, ml, 8, w[3], h2_t, bf)
            yield b, bk, t
            yield ctxb(w)

        for m in range(3):
            b, bk, t = block1(mh, ml, 8, h2_t, ())
            a = act(CQ[:, m, :], bk, ACTF.Copy, t, end1)
            mainr.give(b, a)
            cq_t.append(a)
        for m in range(2):
            w = st.next()
            ts_ = []
            for (b, bk, t), cs in zip(both(w), (slice(NCTX, NKEY), slice(0, NCTX))):
                a = act(CKV[:, m, cs], bk, ACTF.Copy, t, x_free)
                mainr.give(b, a)
                ts_.append(a)
            st.done(w[0], t)
            ckv_t.append(ts_)
        kr_t = []
        w = st.next()
        for (b, bk, t), cs in zip(both(w), (slice(NCTX, NKEY), slice(0, NCTX))):
            si, x, sf = xw.take()
            n = cs.stop - cs.start
            v1 = tt(V, x[64:96, 0:n], bk[96:128, 0:n], CS[96:128, cs], MUL, t, cs_t, sf)
            v2 = tt(V, KR[64:96, cs], bk[64:96, 0:n], CS[64:96, cs], MUL, t, cs_t)
            mainr.give(b, v2)
            v = tt(V, KR[64:96, cs], KR[64:96, cs], x[64:96, 0:n], ADD, v1, v2)
            xw.give(si, v)
            kr_t.append(v)
        st.done(w[0], t)
        h2_free = t

        def rms_small(src, nb, cols, n, toks, name, dh, dl):
            nt = cols // 128
            chn = None
            sc_ = None
            SAv, SQv = PM[1][:, 0:cols], PM[0][:, 0:cols]
            for m in range(nb):
                if m == 0:
                    chn = act(SAv, src[:, m, :], ACTF.Square, toks[m], sfree[0])
                else:
                    a = act(SQv, src[:, m, :], ACTF.Square, toks[m], sfree[0], chn if m > 1 else None)
                    chn = tt(V, SAv, SAv, SQv, ADD, a, chn)
            res, at = [], 0
            while at < nt:
                k = min(4, nt - at)
                b, bk, t, stt_ = rms_bcast(SAv[:, at * 128:(at + k) * 128], k, n, EPS2, chn)
                for m in range(nb):
                    cs = slice(at * 128, (at + k) * 128)
                    v = stt(src[:, m, cs], src[:, m, cs], col(name, m), bk[:, 0:k * 128], MUL, MUL, t)
                    res.append(split(dh[:, m, cs], dl[:, m, cs], src[:, m, cs], v, h2_free))
                auxr.give(b, v)
                at += k
            sfree[0] = [stt_, chn]
            return res

        sfree = [[hc_t[-1], dgf[0]]]
        cqn = rms_small(CQ, 3, S, 384, cq_t, "q_norm_g_2", CH[:, 0:3, :], CL[:, 0:3, :])
        ckn = rms_small(CKV, 2, NKEY, 256, ckv_t, "kv_norm_g_2", CKH, CKL)

        cqn_k = [cqn] * 3
        pmr = Ring([x[:, :] for x in PM])
        ptr = Ring([x[:, :] for x in PT])
        pmr.free = [list(sfree[0]), list(sfree[0])]
        ptr.free = [list(flat(xw.free[0])), list(flat(xw.free[1]))]
        NM = newcols(12)
        nmr = Ring([NM[:, 3 * i:3 * i + 3] for i in range(4)])
        qg_free, kg_free, vg_free = [cqn, None], [ckn, None], [None]
        o_t = []
        CT = 3
        for g in range(2):
            q_t = []
            for h in range(4):
                b, bk, t = block1(lambda k: CH[:, k, :], lambda k: CL[:, k, :], 3, cqn_k, (0,))
                a = act(QG[0:64, h, :], bk[0:64, :], ACTF.Copy, t, qg_free)
                si, x, sf = ptr.take()
                v1 = tt(V, x[64:96, 0:S], bk[96:128, :], CS[96:128, NCTX:NKEY], MUL, t, sf)
                v2 = tt(V, QG[64:96, h, :], bk[64:96, :], CS[64:96, NCTX:NKEY], MUL, t, qg_free)
                mainr.give(b, a, v2)
                v = tt(V, QG[64:96, h, :], QG[64:96, h, :], x[64:96, 0:S], ADD, v1, v2)
                ptr.give(si, v)
                q_t.append([a, v])
            k_t = [[] for _ in range(4)]
            for h in range(4):
                k_t[h].append(cp(G, KG[64:96, h, :], KR[64:96, :], kr_t, kg_free))
            for pr in range(2):
                w, wh, wl, wt = st.next()
                for cs in (slice(NCTX, NKEY), slice(0, NCTX)):
                    n = cs.stop - cs.start
                    b, bk, bf = mainr.take()
                    t = block(bk[:, 0:n], wk(wh), wk(wl), lambda k: CKH[:, k, cs], lambda k: CKL[:, k, cs], 2,
                              [wt, ckn], None, bf, (0,))
                    for i in range(2):
                        a = act(KG[0:64, 2 * pr + i, cs], bk[64 * i:64 * i + 64, 0:n], ACTF.Copy, t, kg_free)
                        k_t[2 * pr + i].append(a)
                    mainr.give(b, a)
                st.done(w, t)
            v_t = []
            w, wh, wl, wt = st.next()
            for t6 in range(6):
                b, bk, bf = mainr.take()
                ks = slice(t6 * 128, t6 * 128 + 128)
                t = block(bk[:, 0:256], lambda k: CKH[:, k, ks], lambda k: CKL[:, k, ks],
                          wk(wh, 256), wk(wl, 256), 2, [wt, ckn], None, bf)
                a = act(VG[:, t6, :], bk[:, 0:256], ACTF.Copy, t, vg_free)
                mainr.give(b, a)
                v_t.append(a)
            st.done(w, t)
            c_free = t

            seq = [(h, j) for h in range(4) for j in range(4)]
            stage = {}

            def scores(i):
                h, j = seq[i]
                i0, _, f0 = auxr.take()
                i1, _, f1 = auxr.take()
                bp = PB[2 + i0 // 2]
                assert i0 % 2 == 0
                js = slice(j * 128, (j + 1) * 128)
                mm(bp[:, 0:512], QG[0:96, h, js], KG[0:96, h, 0:512], True, True, q_t[h], k_t[h], f0, f1)
                t = mm(bp[:, 512:768], QG[0:96, h, js], KG[0:96, h, 512:768], True, True)
                ni, nm, nf = nmr.take()
                v = V(lambda e: e.tensor_reduce(nm[:, 0:1], bp[:, 0:NKEY], AX.X, ALU.max, negate=True), t, nf)
                v = ts(V, nm[:, 0:1], nm[:, 0:1], SCALE, None, MUL, None, v)
                pi, pm, pf = pmr.take()
                a = act(pm, bp[:, 0:NKEY], ACTF.Exp, v, pf, bias=nm[:, 0:1], scale=SCALE, acc=nm[:, 1:2])
                auxr.give(i0, a)
                auxr.give(i1, a)
                v = V(lambda e: e.reciprocal(nm[:, 2:3], nm[:, 1:2]), a)
                stage[i] = [t, pi, pm, a, ni, nm, v]

            def turn(i):
                t, pi, pm, a, ni, nm, v = stage[i]
                f0, f1 = tfree[0]
                mp = PB[0]
                for k in range(6):
                    t = tr(mp[:, k * 128:(k + 1) * 128], pm[:, k * 128:(k + 1) * 128], IDN[:, :], a, f0, f1)
                pmr.give(pi, t)
                qi, pt, qf = ptr.take()
                c = act(pt[:, 0:512], mp[:, 0:512], ACTF.Copy, t, qf)
                c2_ = cp(V, pt[:, 512:768], mp[:, 512:768], t, qf)
                tfree[0] = [c, c2_]
                stage[i] += [qi, pt, [c, c2_]]

            def values(i):
                h, j = seq[i]
                ni, nm, v, qi, pt, ct = stage[i][4:]
                bk = bank[2 + i % 2][:, 0:64]
                f0, f1 = ofree[i % 2], None
                for k in range(6):
                    t = mm(bk, pt[:, k * 128:(k + 1) * 128], VG[:, k, h * 64:h * 64 + 64], k == 0, k == 5, ct, v_t, f0, f1)
                ptr.give(qi, t)
                hg = 4 * g + h
                v = ts(V, OTm[:, j, hg * 64:hg * 64 + 64], bk, nm[:, 2:3], None, MUL, None, t, v)
                ofree[i % 2] = v
                nmr.give(ni, v)
                o_t.append(v)
                return t

            auxr.even()
            mainr.even()
            mb_ = [mainr.take() for _ in range(4)]
            mb_.sort(key=lambda z: z[0])
            tfree, ofree = [[mb_[0][2], mb_[1][2]]], [mb_[2][2], mb_[3][2]]
            scores(0)
            for i in range(17):
                if i + 1 < 16:
                    scores(i + 1)
                for _ in range(CT):
                    tick()
                if i < 16:
                    turn(i)
                if i:
                    t = values(i - 1)
            for i, f in enumerate((tfree[0][0], tfree[0][1], ofree[0], ofree[1])):
                mainr.give(i, f)
            qg_free, kg_free, vg_free = [t], [t], [t]

        while ticks:
            tick()

        S1_, S2_ = PT[0][:, 0:512], PT[1][:, 0:512]
        SQ_ = [PM[0][:, 0:512], PM[1][:, 0:512]]
        fr_ = [flat(ptr.free), flat(pmr.free)]
        c1_ = c2_ = None
        sqf = [None, None]
        for j in range(4):
            a = act(SQ_[j % 2], CV[:, j, :], ACTF.Square, conv_t[j], fr_, sqf[j % 2])
            if j == 0:
                c1_ = cp(G, S1_, CV[:, j, :], conv_t[j], fr_)
                c2_ = cp(G, S2_, SQ_[0], a, fr_)
            else:
                c1_ = tt(G, S1_, S1_, CV[:, j, :], ADD, conv_t[j], c1_)
                c2_ = tt(G, S2_, S2_, SQ_[j % 2], ADD, a, c2_)
            sqf[j % 2] = c2_
        (b1, rb, t1), (b2, mb, t2), _ = ln_bcast(S1_, S2_, 4, 512, EPS2, c1_, c2_)
        m_t = []
        for j in range(4):
            x = CV[:, j, :]
            v = tt(V, x, x, rb, MUL, t1, c1_, a)
            v = tt(V, x, x, mb, ADD, v, t2)
            vv = v
            a = act(x, x, ACTF.Silu, v, bias=col("conv_ln_b_2", j), scale=col("conv_ln_g_2", j))
            m_t.append(split(MH[:, j, :], ML[:, j, :], x, a, h2_free))
        auxr.give(b1, vv)
        auxr.give(b2, vv)
        for f in range(4):
            b, bk, bf = mainr.take()
            for j in range(4):
                t = tr(bk[:, j * 128:(j + 1) * 128], OTm[:, j, f * 128:(f + 1) * 128], IDN[:, :], o_t[-1], o_t, bf)
            a = act(MH[:, 4 + f, :], bk, ACTF.Copy, t, h2_free)
            v = tt(V, ML[:, 4 + f, :], bk, MH[:, 4 + f, :].bitcast(F32), SUB, a)
            mainr.give(b, v)
            m_t.append([a, v])
        ot_free = t

        def residual(bk, k, bias, gate, t, *w):
            si, x, sf = wr.take()
            v = ts(V, x, bk, bias, gate, ADD, MUL, t, sf)
            v2 = stt(XL[:, k, :], XL[:, k, :], ALPHA, x, MUL, ADD, v, w)
            wr.give(si, v2)
            return v, v2

        def stats_of(k, toks, s1, s2, chain):
            si, x, sf = wr.take()
            u = acc_stats(XL[:, k, :], k, s1, s2, (si, x, sf), chain, toks)
            wr.give(si, u)

        wr = Ring([OTm[:, i, :] for i in range(4)])
        wr.free = [[ot_free] for _ in range(4)]
        S1, S2 = CV[:, 0, :], CV[:, 1, :]
        chain = {"free": [m_t[0], m_t[1]]}
        r_t = []
        three = blocks3(mh, ml, m_t)
        for kk in range(8):
            b, bk, t = three.pop(0) if three else block1(mh, ml, 8, m_t)
            v, v2 = residual(bk, kk, col("b_o_2", kk), M2[:, 16 + kk:17 + kk], t, h2_t[kk])
            mainr.give(b, v)
            r_t.append(v2)
            stats_of(kk, v2, S1, S2, chain)
        mo_free = t
        (b1, rb, t1), (b2, mb, t2), st1 = ln_bcast(S1, S2, 4, D, EPS2, chain["s1"], chain["s2"])
        A2, B2 = newcols(8), newcols(8)
        v = tt(V, A2, SC2, col("ln1_g_2", 0, 8), MUL, e2)
        v_ = tt(V, B2, SC2, col("ln1_b_2", 0, 8), MUL, e2)
        v_ = tt(V, B2, B2, M2[:, 24:32], ADD, v_)
        h3_t, xm_t = [], []
        for k in range(8):
            x = XL[:, k, :]
            v1 = tt(V, x, x, rb, MUL, t1, chain["s1"], chain["s2"], r_t[k])
            v1 = tt(V, x, x, mb, ADD, v1, t2)
            si, y, sf = wr.take()
            v2 = ts(V, y, x, A2[:, k:k + 1], B2[:, k:k + 1], MUL, ADD, v1, v, v_, sf)
            h3_t.append(split(MH[:, k, :], ML[:, k, :], y, v2, mo_free))
            wr.give(si, h3_t[-1])
            xm_t.append(ts(G, x, x, col("ln1_g_2", k), col("ln1_b_2", k), MUL, ADD, v1, v2))
        auxr.give(b1, v1)
        auxr.give(b2, v1)
        end2 = [h3_t[-1], st1, t2]
        c2.close()

        c3 = ExitStack()
        AH = sb("AH", [128, 22, S], F32R, c3)
        AL = sb("AL", [128, 22, S], F32R, c3)
        YG = [sb(f"YG{i}", [128, S], F32, c3) for i in range(4)]
        ygr = Ring([y[:, :] for y in YG])

        def tap(i, blk_):
            return col("ffn_dw_w_2", 44 * i + blk_)

        a_t = []
        three = blocks3(mh, ml, h3_t)
        for j in range(22):
            ys = []
            for m in range(2):
                b, bk, t = three.pop(0) if three else block1(mh, ml, 8, h3_t)
                blk_ = 22 * m + j
                yi, y, yf = ygr.take()
                a = act(y, bk, ACTF.Identity, t, yf, end2, bias=col("ffn_dw_b_2", blk_), scale=tap(1, blk_))
                v = stt(y[:, 1:S], bk[:, 0:S - 1], tap(0, blk_), y[:, 1:S], MUL, ADD, a)
                v = stt(y[:, 0:S - 1], bk[:, 1:S], tap(2, blk_), y[:, 0:S - 1], MUL, ADD, v)
                mainr.give(b, v)
                ys.append((yi, y, v))
            (gi, yg, gt), (vi, yv, vt) = ys
            a = act(yg, yg, ACTF.Silu, gt)
            v = tt(V, yg, yg, yv, MUL, a, vt)
            s_ = split(AH[:, j, :], AL[:, j, :], yg, v, end2)
            ygr.give(gi, s_)
            ygr.give(vi, v)
            a_t.append(s_)
        up_end = t
        c3y = YG
        wr = Ring([y[:, :] for y in YG])
        wr.free = [[s_, v] for _ in range(4)]
        cM2 = ExitStack()
        cM2.close()
        S1, S2 = YG[2][:, :], YG[3][:, :]
        wr = Ring([YG[0][:, :], YG[1][:, :]])
        wr.free = [[s_, v], [s_, v]]
        chain = {"free": [s_, v]}
        r_t = []
        for cpair in range(4):
            bs = [mainr.take() for _ in range(2)]
            for q, (r0, nk) in enumerate(((0, 8), (8, 7), (15, 7))):
                for m in range(2):
                    kk = 2 * cpair + m
                    b, bk, t = block1(lambda k: AH[:, r0 + k, :], lambda k: AL[:, r0 + k, :], nk,
                                      [a_t[r0 + k] for k in range(nk)], first=q == 0, last=q == 2, bnk=bs[m])
                    if q == 2:
                        v, v2 = residual(bk, kk, col("b_down_2", kk), M2[:, 40 + kk:41 + kk], t, xm_t[kk])
                        mainr.give(b, v)
                        r_t.append(v2)
                        stats_of(kk, v2, S1, S2, chain)
        (b1, rb, t1), (b2, mb, t2), _ = ln_bcast(S1, S2, 4, D, EPS2, chain["s1"], chain["s2"])
        f_t = []
        for k in range(8):
            x = XL[:, k, :]
            v1 = tt(V, x, x, rb, MUL, t1, chain["s1"], chain["s2"], r_t[k])
            v1 = tt(V, x, x, mb, ADD, v1, t2)
            f = act(x, x, ACTF.Identity, v1, bias=col("ln2_b_2", k), scale=col("ln2_g_2", k))
            f_t.append(P.dma("sp", out[k * 128:(k + 1) * 128, :], x, s_out, f))
        P.q["sp"].append([[f_t[-1]], None, None])
        c3.close()
        cM.close()
        run_blocks(nc, ctx, P)


def finish(nc, ctx, P, A, out, XL, toks, IDN, mainr, s_out, ACTF, act, tr):
    ot = ctx.enter_context(nc.sbuf_tensor("OT_", [128, 4, 1024], F32))
    for j in range(4):
        for hf in range(2):
            b, bk, bf = mainr.take()
            for k in range(4):
                kk = hf * 4 + k
                t = tr(bk[:, k * 128:(k + 1) * 128], XL[:, kk, j * 128:(j + 1) * 128], IDN[:, :], toks[kk], toks[-1], bf)
            a = act(ot[:, j, hf * 512:(hf + 1) * 512], bk, ACTF.Copy, t)
            mainr.give(b, a)
        d = P.dma("sp", out[0, j * 128:(j + 1) * 128, :], ot[:, j, :], s_out, a)
    P.q["sp"].append([[d], None, None])
    run_blocks(nc, ctx, P)


def run_blocks(nc, ctx, P):
    P.number()
    blk = ctx.enter_context(nc.Block())

    @blk.sync
    def _(e):
        P.emit("sp", e)

    @blk.gpsimd
    def _(e):
        P.emit("pool", e)

    @blk.scalar
    def _(e):
        P.emit("act", e)

    @blk.tensor
    def _(e):
        P.emit("pe", e)

    @blk.vector
    def _(e):
        P.emit("dve", e)


def shape_constants():
    f = np.float32
    con = np.zeros((128, 704 + 768), f)
    con[:, 0:128] = np.eye(128, dtype=f)
    con[:, 128:640] = (np.arange(512) % 64 != 0).astype(f)
    for g in range(4):
        w = 2 << g
        con[:, 640 + 16 * g:640 + 16 * g + w] = f(w) / np.arange(1, w + 1, dtype=f)
    tok = np.arange(S)
    inv = (f(10000.0) ** (-np.arange(8, dtype=f) / f(8))).astype(f)
    ang = np.concatenate([(tok // 64).astype(f)[:, None] * inv, (tok % 64).astype(f)[:, None] * inv], -1).astype(f)
    co, si = np.cos(ang).T.astype(f), np.sin(ang).T.astype(f)
    con[64:96, 704:960] = 1.0
    con[64:96, 960:1472] = np.concatenate([co, co])
    con[96:128, 960:1472] = np.concatenate([-si, si])
    s_, t_ = np.arange(128)[:, None], np.arange(128)[None, :]
    mk = np.zeros((128, 7, 128), f)
    mk[:, 0] = s_ == t_
    for lv in range(1, 7):
        h, b = 1 << (lv - 1), 1 << lv
        mk[:, lv] = ((s_ // b == t_ // b) & (s_ % b < h) & (t_ % b >= h))
    return con, mk.reshape(128, 7 * 128)


def host_layout(np, inputs):
    cols = []
    for name, n in PARAMS:
        a = np.ascontiguousarray(inputs[name]).reshape(n, 128)
        cols.append(a.T)
    parts = []
    for it in stream_layout():
        blocks = it[1] if it[0] == "w" else [it[1]]
        views = []
        for name, at, r0, nk, sets in blocks:
            a = np.asarray(inputs[name])
            a = a[at[0]][at[1]] if isinstance(at, tuple) else a[at]
            rows = a[r0 * 128:(r0 + nk) * 128]
            b = np.concatenate([rows[:, c:c + n] for c, n in sets], axis=1)
            views.append(b.reshape(nk, 128, -1).transpose(1, 0, 2).reshape(128, -1))
        parts.append(np.concatenate(views, axis=1).reshape(-1))
    return {
        "params": np.concatenate(cols, axis=1),
        "xT": np.asarray(inputs["x"])[0].T,
        "ctxT": np.asarray(inputs["ctx_2"])[0].T,
        "wstream": np.concatenate(parts),
    }


def kernel(_stop=None, **inputs):
    import numpy as _np
    import concourse.bacc as _bacc
    from concourse import mybir as _mybir
    from concourse.bass_utils import run_bass_kernel_spmd as _run

    nc = _bacc.Bacc("TRN2", target_bir_lowering=False, num_devices=1)
    arrays, args = {}, {}
    con, mk = shape_constants()
    packed = host_layout(_np, inputs)
    for name, a in list(packed.items()) + [("consts", con), ("masks", mk)]:
        a = _np.ascontiguousarray(a)
        arrays[f"in_{name}"] = a
        args[name] = nc.dram_tensor(f"in_{name}", a.shape, _mybir.dt.from_np(a.dtype), kind="ExternalInput").ap()
    out = nc.dram_tensor("out_0", (D, S) if _stop is None else (1, S, D), _mybir.dt.float32, kind="ExternalOutput").ap()
    build(nc, args, out, args.pop("consts"), args.pop("masks"), _stop)
    r = _run(nc, [arrays], core_ids=[0])
    if _stop:
        return r.results[0]["out_0"]
    return _np.ascontiguousarray(r.results[0]["out_0"].T).reshape(1, S, D)
```

```python
import numpy as np
from contextlib import ExitStack
import concourse.bass as bass
from concourse import mybir

F32 = mybir.dt.float32
F32R = mybir.dt.float32r
U8 = mybir.dt.uint8
ALU = mybir.AluOpType
ACTF = mybir.ActivationFunctionType
AX = mybir.AxisListType
MUL, ADD, SUB = ALU.mult, ALU.add, ALU.subtract

S = 512
D = 1024
EPS1 = 1e-6
EPS2 = 1e-5
ALPHA = 2 ** 0.25
SCALE = 96 ** -0.5
NCTX = 256
NKEY = NCTX + S

PARAMS = [("c", 8), ("norm_pre_w", 8), ("ada_b", 24), ("pool_scale", 8), ("hgrn_lower_bounds", 8),
          ("hgrn_norm_w", 1), ("norm_post_w", 8), ("c_2", 8), ("c_ctx_2", 8), ("conv_dw_b_2", 4),
          ("conv_ln_g_2", 4), ("conv_ln_b_2", 4), ("q_norm_g_2", 3), ("kv_norm_g_2", 2), ("b_o_2", 8),
          ("ln1_g_2", 8), ("ln1_b_2", 8), ("b_ada_2", 48), ("ffn_dw_b_2", 44), ("b_down_2", 8),
          ("ln2_g_2", 8), ("ln2_b_2", 8), ("conv_dw_w_2", 124), ("ffn_dw_w_2", 132)]
NPAR = sum(n for _, n in PARAMS)


def stream_layout():
    items = []

    def w(*blocks):
        items.append(("w", list(blocks)))

    later = [("a", ("ada_w", 0, 4 * half, 4, [(512 * g, 512)]), g, half) for g in (4, 5) for half in range(2)]
    later += [("a", ("w_ada_2", 0, 4 * half, 4, [(512 * g, 512)]), g, half) for g in range(12) for half in range(2)]

    def also():
        if later:
            items.append(later.pop(0))

    U0, GP0, Q_0, F0, I0, GH0 = (1024 * i for i in range(6))
    ada1 = [("a", ("ada_w", 0, 4 * half, 4, [(512 * g, 512)]), g, half) for g in range(4) for half in range(2)]
    for h in range(8):
        if h == 0:
            items += ada1[0:2] + ada1[4:5]
        w(("w_in", 0, 0, 8, [(I0 + h * 128, 128)]), ("w_in", 0, 0, 8, [(F0 + h * 128, 128)]))
        if h:
            also()
        else:
            items += ada1[5:6]
        w(("w_in", 0, 0, 8, [(Q_0 + h * 128, 128)]), ("w_in", 0, 0, 8, [(GH0 + h * 128, 128)]))
        if h:
            also()
        else:
            items += ada1[2:4] + ada1[6:8]
    def pw(g):
        w(*[("pool_w", (0, g), 0, 2, [(m * 128, 128)]) for m in range(2)])

    for g in (3, 2, 1, 0):
        w(*[("w_in", 0, 0, 8, [(GP0 + (2 * g + m) * 128, 128)]) for m in range(2)])
        also()
        if g < 3:
            pw(g + 1)
        w(*[("w_in", 0, 0, 8, [(U0 + (2 * g + m) * 128, 128)]) for m in range(2)])
        also()
    for m in range(8):
        if m == 0:
            w(("w_out", 0, 2, 8, [(0, 128)]))
            pw(0)
            w(("w_out", 0, 10, 8, [(0, 128)]))
        else:
            w(*[("w_out", 0, r0, 8, [(m * 128, 128)]) for r0 in (2, 10)])
        also()
    while later:
        also()
    for j in range(4):
        w(("w_in_2", 0, 0, 8, [(j * 128, 128)]), ("w_in_2", 0, 0, 8, [(512 + j * 128, 128)]))
    w(*[("w_in_2", 0, 0, 8, [(1024 + 128 * m, 128)]) for m in range(2)])
    w(*[("w_in_2", 0, 0, 8, [(1280 + 128 * m, 128)]) for m in range(2)])
    w(("w_in_2", 0, 0, 8, [(1536, 128)]),
      ("w_in_2", 0, 0, 8, [(1664, 32), (1664, 32), (1664, 32), (1680, 16), (1664, 16)]))
    for g in range(2):
        w(*[("w_uq_2", 0, 0, 3, [(h * 96, 96), (h * 96 + 80, 16), (h * 96 + 64, 16)])
            for h in range(4 * g, 4 * g + 4)])
        w(*[("w_ukv_2", 0, 0, 2, [(h * 128, 64), (h * 128 + 128, 64)]) for h in (4 * g, 4 * g + 2)],
          ("w_ukv_2", 0, 0, 2, [(h * 128 + 64, 64) for h in range(4 * g, 4 * g + 4)]))
    for c in range(4):
        w(*[("w_o_2", 0, 0, 8, [((2 * c + m) * 128, 128)]) for m in range(2)])
    for j in range(22):
        w(*[("w_up_2", 0, 0, 8, [(2816 * m + j * 128, 128)]) for m in range(2)])
    for c in range(4):
        for r0, nk in ((0, 8), (8, 7), (15, 7)):
            w(*[("w_down_2", 0, r0, nk, [((2 * c + m) * 128, 128)]) for m in range(2)])
    return items


def block_size(b):
    return b[3] * sum(n for _, n in b[4])


class Tok:

    def __init__(self, eng, i):
        self.eng, self.i = eng, i


class DTok:

    def __init__(self, sem, val):
        self.sem, self.val = sem, val


def flat(ws):
    out = []
    for w in ws:
        if w is None:
            continue
        if isinstance(w, (list, tuple)):
            out += flat(w)
        else:
            out.append(w)
    return out


class Prog:

    ENG = ("pe", "act", "dve", "pool", "sp")

    def __init__(self, sems):
        self.sems = sems
        self.q = {e: [] for e in self.ENG}
        self.dcount = {}

    def op(self, eng, fn, *ws):
        self.q[eng].append([flat(ws), fn, False])
        return Tok(eng, len(self.q[eng]) - 1)

    def dma(self, eng, out, in_, sem, *ws):
        n = self.dcount.get(id(sem), 0) + 16
        self.dcount[id(sem)] = n
        self.q[eng].append([flat(ws), lambda e: e.dma_start(out, in_).then_inc(sem, 16), None])
        return DTok(sem, n)

    def number(self):
        for e in self.ENG:
            for ws, _, _ in self.q[e]:
                for w in ws:
                    if isinstance(w, Tok):
                        self.q[w.eng][w.i][2] = True
        self.val = {}
        for e in self.ENG:
            n, vals = 0, []
            for it in self.q[e]:
                n += it[2] is True
                vals.append(n)
            self.val[e] = vals

    def emit(self, name, e):
        seen = {}
        for ws, fn, inc in self.q[name]:
            for w in ws:
                if isinstance(w, Tok):
                    sem, v = self.sems[w.eng], self.val[w.eng][w.i]
                else:
                    sem, v = w.sem, w.val
                if seen.get(id(sem), 0) < v:
                    e.wait_ge(sem, v)
                    seen[id(sem)] = v
            if fn is None:
                continue
            ins = fn(e)
            if inc:
                ins.then_inc(self.sems[name], 1)


class Ring:

    def __init__(self, bufs):
        self.bufs, self.n = bufs, 0
        self.free = [[] for _ in bufs]

    def take(self):
        i = self.n % len(self.bufs)
        self.n += 1
        f, self.free[i] = self.free[i], None
        assert f is not None
        return i, self.bufs[i], f

    def skip(self, i):
        self.n = i

    def even(self):
        self.n += self.n % 2

    def give(self, i, *toks):
        self.free[i] = flat(toks)


def build(nc, A, out, consts, masks):
    LAY = stream_layout()

    ctx = ExitStack()
    with ctx:
        def sb(name, shape, dt=F32, c=ctx):
            return c.enter_context(nc.sbuf_tensor(name, shape, dt))

        sems = {e: ctx.enter_context(nc.semaphore("s_" + e)) for e in Prog.ENG}
        P = Prog(sems)
        s_par = ctx.enter_context(nc.semaphore("s_par"))
        s_con = ctx.enter_context(nc.semaphore("s_con"))
        s_msk = ctx.enter_context(nc.semaphore("s_msk"))
        s_out = ctx.enter_context(nc.semaphore("s_out"))
        s_c = ctx.enter_context(nc.semaphore("s_c"))
        s_x = [ctx.enter_context(nc.semaphore(f"s_x{i}")) for i in range(4)]
        NRAW = 3
        s_raw = [ctx.enter_context(nc.semaphore(f"s_raw{i}")) for i in range(NRAW)]

        def T(fn, *w):
            return P.op("pe", fn, *w)

        def C(fn, *w):
            return P.op("act", fn, *w)

        def V(fn, *w):
            return P.op("dve", fn, *w)

        def G(fn, *w):
            return P.op("pool", fn, *w)

        def mm(o, l, r, st, sp, *w, skip=False):
            return T(lambda e: e.matmul(o, l, r, start=st, stop=sp, skip_group_check=skip), *w)

        def tr(o, i, idn, *w):
            return T(lambda e: e.transpose(o, i, idn), *w)

        def act(o, i, f, *w, bias=0.0, scale=1.0, acc=None):
            if acc is not None:
                return C(lambda e: e.activation(o, i, f, bias=bias, scale=scale, accum_out=acc), *w)
            if f == ACTF.Copy:
                return C(lambda e: e.activation(o, i, f), *w)
            return C(lambda e: e.activation(o, i, f, bias=bias, scale=scale), *w)

        def tt(q, o, a, b, op, *w):
            return q(lambda e: e.tensor_tensor(o, a, b, op), *w)

        def ts(q, o, a, s1, s2, o1, o2, *w):
            if s2 is None:
                return q(lambda e: e.tensor_scalar(o, a, s1, None, o1), *w)
            return q(lambda e: e.tensor_scalar(o, a, s1, s2, o1, o2), *w)

        def stt(o, a, s, b, o1, o2, *w):
            return V(lambda e: e.scalar_tensor_tensor(out=o, in0=a, scalar=s, in1=b, op0=o1, op1=o2), *w)

        def cp(q, o, i, *w):
            return q(lambda e: e.tensor_copy(o, i), *w)

        IDN = sb("IDN", [128, 128])
        ONES = sb("ONES", [128, 128])
        NPOW = sb("NPOW", [128, 8])
        PC = sb("PC", [128, NPAR])
        PX = sb("PX", [128, 256])
        SCT = sb("SCT", [128, 64])
        RAW = [sb(f"RAW{i}", [128, 2048]) for i in range(NRAW)]
        WH = [sb(f"WH{i}", [128, 1024], F32R) for i in range(4)]
        WL = [sb(f"WL{i}", [128, 1024], F32R) for i in range(4)]
        XL = sb("XL", [128, 8, S])
        DG = sb("DG", [128, 512])
        PTA = sb("PTA", [128, 1536])
        HH = sb("HH", [128, 8, S], F32R)
        HL = sb("HL", [128, 8, S], F32R)
        PB = [ctx.enter_context(nc.psum_tensor(f"PB{i}", [128, 1024], F32)) for i in range(4)]
        bank = [PB[i // 2][:, (i % 2) * 512:(i % 2) * 512 + 512] for i in range(8)]

        COL, r = {}, 0
        for name, n in PARAMS:
            COL[name] = r
            r += n

        def col(name, j=0, n=1):
            return PC[:, COL[name] + j:COL[name] + j + n]

        npx = [0]

        def newcols(n):
            a = npx[0]
            npx[0] += n
            assert npx[0] <= 256
            return PX[:, a:a + n]

        par_t = P.dma("act", PC[:, :], A["params"][:, :], s_par)
        c_dma = P.dma("act", IDN[:, :], consts[:, 0:128], s_con)
        on_t = G(lambda e: e.memset(ONES[:, :], 1.0))
        np_t = G(lambda e: e.memset(NPOW[:, :], -0.5))

        mainr = Ring(bank[0:4])
        auxr = Ring(bank[4:8])

        offs, at = [], 0
        for it in LAY:
            n = block_size(it[1]) if it[0] == "a" else sum(block_size(b) for b in it[1])
            offs.append((at, n))
            at += 128 * n

        class Stream:

            def __init__(s):
                s.nd = s.np = s.nb = s.nw = s.ready = s.at = 0
                s.rfree = [[] for _ in range(NRAW)]
                s.tok, s.part = {}, []
                s.wfree = [[], [], [], []]
                s.wready = {}
                s.over = set()
                s.chunks = []

            def fetch(s):
                while s.nd < len(LAY) and (s.nd < NRAW or s.nd - NRAW in s.over):
                    i = s.nd % NRAW
                    o, n = offs[s.nd]
                    src = A["wstream"][o:o + 128 * n].rearrange("(p n) -> p n", p=128)
                    s.tok[s.nd] = P.dma("sp", RAW[i][:, 0:n], src, s_raw[i], s.rfree[i])
                    s.nd += 1

            def pump(s, limit=len(LAY)):
                s.fetch()
                while s.np < limit:
                    it = LAY[s.np]
                    i = s.np % NRAW
                    while s.np not in s.tok:
                        s.chunk()
                    raw, tok = RAW[i], s.tok[s.np]
                    if it[0] == "w":
                        h = s.nw % 4
                        free = s.wfree[h]
                        if free is None:
                            return
                        n = block_size(it[1][s.nb])
                        src = raw[:, s.at:s.at + n]
                        s.wfree[h] = None
                        a = act(WH[h][:, 0:n], src, ACTF.Copy, tok, free)
                        v = tt(V, WL[h][:, 0:n], src, WH[h][:, 0:n].bitcast(F32), SUB, a, free)
                        s.wready[s.nw] = [a, v]
                        s.part += [a, v]
                        s.nw += 1
                        s.nb += 1
                        s.at += n
                        if s.nb < len(it[1]):
                            continue
                        s.rfree[i], s.part, s.nb, s.at = s.part, [], 0, 0
                        s.over.add(s.np)
                    elif it[1][0] == "ada_w" and it[2] < 4:
                        s.rfree[i] = flat([ada_item(it, raw, tok)])
                        s.over.add(s.np)
                    else:
                        for k in range(4):
                            s.chunks.append((s.np, k, it, raw, tok))
                    s.np += 1
                    s.fetch()

            def chunk(s):
                n, k, it, raw, tok = s.chunks.pop(0)
                r = ada_item(it, raw, tok, (k,))
                if k == 3:
                    s.rfree[n % NRAW] = flat([r])
                    s.over.add(n)
                    s.fetch()

            def next(s):
                n = s.ready
                s.ready += 1
                return n % 4, WH[n % 4], WL[n % 4], s.wready[n]

            def done(s, h, tok):
                s.wfree[h] = [tok]
                s.pump()

        st = Stream()

        def mm3(o, lh, ll, rh, rl, first, last, *w, skip=False):
            mm(o, lh, rh, first, False, *w, skip=skip)
            mm(o, lh, rl, False, False, skip=skip)
            return mm(o, ll, rh, False, last, skip=skip)

        sct = Ring([SCT[:, 16 * i:16 * i + 16] for i in range(4)])

        def diag_bcast(cols, nt, dgfree, *w, dg=None):
            ds = []
            dg = DG[:, :] if dg is None else dg
            for j in range(nt):
                ds.append(ts(V, dg[:, j * 128:(j + 1) * 128], IDN[:, :], cols[:, j:j + 1], None, MUL, None, w, dgfree))
            b, bk, bf = auxr.take()
            t = mm(bk[:, 0:nt * 128], ONES[:, :], dg[:, 0:nt * 128], True, True, ds[-1], bf)
            return b, bk, t

        dgf = [None]

        def stat_cols(accs, nt, *w):
            b, bk, bf = auxr.take()
            t = None
            for a, acc in enumerate(accs):
                for j in range(nt):
                    t = mm(bk[:, a * 4 + j:a * 4 + j + 1], acc[:, j * 128:(j + 1) * 128], ONES[:, 0:1],
                           True, True, w, bf)
            return b, bk, t

        def rms_bcast(acc, nt, n, eps, *w):
            b, bk, t = stat_cols([acc], nt, w)
            si, sc, sf = sct.take()
            v = ts(V, sc[:, 0:nt], bk[:, 0:nt], 1.0 / n, eps, MUL, ADD, t, sf)
            auxr.give(b, v)
            g = G(lambda e: e.tensor_tensor(sc[:, 4:4 + nt], sc[:, 0:nt], NPOW[:, 0:nt], ALU.pow), v, np_t)
            b2, bk2, t2 = diag_bcast(sc[:, 4:4 + nt], nt, dgf[0], g)
            dgf[0] = t2
            sct.give(si, t2)
            return b2, bk2, t2, t

        def ln_bcast(s1, s2, nt, n, eps, *w, last=None, dg=None, dgf2=None):
            b, bk, bf = auxr.take()
            src = [(0, s1, w), (1, s2, w)]
            if last:
                src += [(0, last[0], last[2]), (1, last[1], last[2])]
            for i, (a, acc, ws) in enumerate(src):
                for j in range(nt):
                    t = mm(bk[:, a * 4 + j:a * 4 + j + 1], acc[:, j * 128:(j + 1) * 128], ONES[:, 0:1],
                           i == 0 and j == 0, i == len(src) - 1, ws, bf, skip=True)
            si, sc, sf = sct.take()
            m, v, r, q = (sc[:, 4 * i:4 * i + nt] for i in range(4))
            a1 = ts(V, m, bk[:, 0:nt], 1.0 / n, None, MUL, None, t, sf)
            a2 = ts(V, v, bk[:, 4:4 + nt], 1.0 / n, eps, MUL, ADD, t)
            auxr.give(b, a2)
            a3 = tt(V, q, m, m, MUL, a1)
            a4 = tt(V, v, v, q, SUB, a3, a2)
            g = G(lambda e: e.tensor_tensor(r, v, NPOW[:, 0:nt], ALU.pow), a4, np_t)
            b1, bk1, t1 = diag_bcast(r, nt, dgf[0], g)
            a5 = stt(q, m, -1.0, r, MUL, MUL, g)
            b2, bk2, t2 = diag_bcast(q, nt, t1 if dg is None else dgf2, a5, dg=dg)
            dgf[0] = t2 if dg is None else t1
            sct.give(si, t2)
            return (b1, bk1, t1), (b2, bk2, t2), t

        def cols_of_acc(dst, acc, n, bias, *w):
            b, bk, bf = auxr.take()
            for j in range(n):
                t = mm(bk[:, j:j + 1], acc[:, j * 128:(j + 1) * 128], ONES[:, 0:1], True, True, w, bf)
            v = tt(V, dst, bk[:, 0:n], bias, ADD, t)
            auxr.give(b, v)
            return t, v

        c1 = ExitStack()
        SM = sb("SM", [128, 512], F32, c1)
        FAC = sb("FAC", [128, 64], F32, c1)
        MK = sb("MK", [128, 7 * 128], U8, c1)
        CC = sb("CC", [128, 24], F32, c1)
        ACC = sb("ACC", [128, 2, 512], F32, c1)
        MPH = sb("MPH", [128, 8, S], F32R, c1)
        MPL = sb("MPL", [128, 8, S], F32R, c1)
        DH = sb("DH", [128, 2, S], F32R, c1)
        DL = sb("DL", [128, 2, S], F32R, c1)
        HB = sb("HB", [128, 10, S], F32, c1)
        GP = sb("GP", [128, 2, S], F32, c1)
        AT = sb("AT", [128, S], F32, c1)
        KDT = sb("KDT", [128, S], F32, c1)
        E0 = sb("E0", [128, S], F32, c1)
        Q0 = sb("Q0", [128, S], F32, c1)
        SS = sb("SS", [128, 7, 128], F32, c1)
        XR = [PTA[:, 512 * i:512 * i + 512] for i in range(3)] + [sb("XR3", [128, S], F32, c1)[:, :]]
        UPA = sb("UPA", [128, 3 * (16 + S)], F32, c1)
        UP = [UPA[:, i * (16 + S):(i + 1) * (16 + S)] for i in range(3)]
        xr = Ring(XR)
        XT = XL

        P.dma("act", HB[:, 0:2, :].rearrange("p a n -> p (a n)")[:, 0:896], masks[:, :], s_msk)
        P.dma("act", SM[:, :], consts[:, 128:640], s_msk)
        m_dma = P.dma("act", FAC[:, :], consts[:, 640:704], s_msk)

        xsrc = A["xT"].rearrange("(k p) t -> p k t", p=128)
        x_t = [P.dma("sp", XT[:, 4 * i:4 * i + 4, :], xsrc[:, 4 * i:4 * i + 4, :], s_x[i]) for i in range(2)]
        st.fetch()
        M1 = newcols(24)
        M2 = newcols(48)
        MC = newcols(16)
        accf = [[], []]
        mod_t = {}
        acc_prev = [None, None]
        deferred = []

        def defer(n, fn):
            deferred.append([n, fn])

        def run_deferred(every=False):
            for d in deferred:
                d[0] -= 1
            for d in [d for d in deferred if every or d[0] <= 0]:
                deferred.remove(d)
                d[1]()

        cc_t = [act(CC[:, 0:8], col("c", 0, 8), ACTF.Silu, par_t),
                act(CC[:, 8:24], col("c_2", 0, 16), ACTF.Silu, par_t)]
        cbank = [None]
        acc_full = [False, False]

        def ada_item(it, raw, tok, ks=(0, 1, 2, 3)):
            _, (name, *_), g, half = it
            w = raw[:, :].rearrange("p (k n) -> p k n", n=512)
            vecs = [0] if name == "ada_w" else [8, 16] if g < 4 else [8]
            first = name == "ada_w" and g < 4
            ai = [0, 1] if len(vecs) == 2 else [g // 2 if first else g % 2]
            on_pe = first and g % 2 == 0
            if half == 0 and ks[0] == 0:
                if first:
                    cbank[0] = auxr.take()
                elif any(acc_full[i] for i in ai):
                    run_deferred(True)
            last, pt_ = None, None
            for k in ks:
                kk = 4 * half + k
                if on_pe and k < 1:
                    b, bk, bf = cbank[0]
                    for j in range(4):
                        pt_ = mm(bk[:, j:j + 1], w[:, k, j * 128:(j + 1) * 128], CC[:, kk:kk + 1], kk == 0 and j == 0,
                                 False, tok, cc_t, bf, skip=True)
                    if half == 1:
                        run_deferred()
                    continue
                for vi, cb in zip(ai, vecs):
                    a, cs = ACC[:, vi, :], CC[:, cb + kk:cb + kk + 1]
                    if kk == (1 if on_pe else 0):
                        last = ts(V, a, w[:, k, :], cs, None, MUL, None, tok, cc_t, accf[vi])
                    else:
                        last = stt(a, w[:, k, :], cs, a, MUL, ADD, tok, acc_prev[vi])
                    acc_prev[vi] = last
            if half == 1 and ks[-1] == 3:
                def sums():
                    for n, vi in enumerate(ai):
                        if name == "ada_w":
                            dst, bias = M1, "ada_b"
                        else:
                            dst, bias = (M2, MC)[n], "b_ada_2"
                        acc_full[vi] = False
                        t, v = cols_of_acc(dst[:, 4 * g:4 * g + 4], ACC[:, vi, :], 4, col(bias, 4 * g, 4),
                                           acc_prev[vi], on_t)
                        accf[vi] = [t]
                        key = "1s" if name == "ada_w" and g < 4 else "1g" if name == "ada_w" else "2"
                        mod_t[key] = [mod_t.get(key), v]
                if first:
                    def sums(cb=cbank[0]):
                        b, bk, bf = cb
                        for j in range(4):
                            t = mm(bk[:, j:j + 1], ACC[:, ai[0], j * 128:(j + 1) * 128], ONES[:, 0:1],
                                   not on_pe and j == 0, j == 3, last, on_t, bf, skip=True)
                        accf[ai[0]] = [t]
                        v = tt(V, M1[:, 4 * g:4 * g + 4], bk[:, 0:4], col("ada_b", 4 * g, 4), ADD, t)
                        auxr.give(b, v)
                        mod_t[g % 2] = [mod_t.get(g % 2), v]
                    if g == 3:
                        run_deferred(True)
                        sums()
                    elif g == 2:
                        sums()
                    else:
                        defer(0, sums)
                else:
                    for i in ai:
                        acc_full[i] = True
                    defer(6 if len(ai) == 1 else 4, sums)
            return [last, pt_]

        LB, LT, OML = newcols(8), newcols(8), newcols(8)
        hlb = col("hgrn_lower_bounds", 0, 8)
        v1 = tt(V, LT, hlb, hlb, SUB, par_t)
        v2 = act(LT, LT, ACTF.Exp, v1)
        v3 = V(lambda e: e.reciprocal(OML, LT), v2)
        v4 = tt(V, LT, LT, OML, MUL, v3)
        v5 = tt(V, LB, LT, LT, SUB, v4)
        lb_t = ts(V, OML, LB, -1.0, 1.0, MUL, ADD, v5)
        st.pump(3)
        xb, xbk, xbf = auxr.take()
        pa = None
        for k in range(8):
            xi, x, xf = xr.take() if k else (None, Q0[:, :], None)
            a = act(x, XT[:, k, :], ACTF.Square, x_t[k // 4], xf)
            if k:
                pa = tt(G, Q0[:, :], Q0[:, :], x, ADD, a, pa or a0)
                xr.give(xi, pa)
            else:
                a0 = a
        for j in range(4):
            t = mm(xbk[:, j:j + 1], Q0[:, j * 128:(j + 1) * 128], ONES[:, 0:1], True, True, pa, on_t, xbf)
        si, sc, sf = sct.take()
        BX = newcols(4)
        ts(V, BX, xbk[:, 0:4], 1.0 / D, EPS2, MUL, ADD, t)
        v = ts(V, sc[:, 0:4], xbk[:, 0:4], 1.0 / D, EPS1, MUL, ADD, t)
        auxr.give(xb, v)
        g_ = G(lambda e: e.tensor_tensor(sc[:, 4:8], sc[:, 0:4], NPOW[:, 0:4], ALU.pow), v, np_t)
        mk_t = cp(G, MK[:, :], HB[:, 0:2, :].rearrange("p a n -> p (a n)")[:, 0:896], m_dma)
        pad_t = None
        for u in UP:
            pad_t = G(lambda e, u=u: e.memset(u[:, 0:16], 0.0))
        st.pump(4)
        b, rb, t = diag_bcast(sc[:, 4:8], 4, None, g_, on_t, c_dma)
        dgf[0] = t
        sct.give(si, t)
        rt_ = act(Q0[:, :], rb, ACTF.Copy, t)
        auxr.give(b, rt_)
        n_toks = [tt(G, XT[:, k, :], XT[:, k, :], Q0[:, :], MUL, rt_, a) for k in range(8)]
        A1, G1 = newcols(8), newcols(8)

        def split_later(dh, dl, src, q, *w):
            a = act(dh, src, ACTF.Copy, w)
            r = [a]
            q.append(lambda: r.append(tt(V, dl, src, dh.bitcast(F32), SUB, a, w)))
            if len(q) > 1:
                q.pop(0)()
            return r

        def flush(q):
            while q:
                q.pop(0)()

        h_toks, lq = [], []

        def h_tiles(hf):
            ks = slice(4 * hf, 4 * hf + 4)
            v = ts(V, A1[:, ks], M1[:, 8 + 4 * hf:12 + 4 * hf], 1.0, None, ADD, None, mod_t[hf])
            a1_t = tt(V, A1[:, ks], A1[:, ks], col("norm_pre_w", 4 * hf, 4), MUL, v)
            for k in range(4 * hf, 4 * hf + 4):
                v = ts(V, XT[:, k, :], XT[:, k, :], A1[:, k:k + 1], M1[:, k:k + 1], MUL, ADD, a1_t, n_toks[k])
                h_toks.append(split_later(HH[:, k, :], HL[:, k, :], XT[:, k, :], lq, v))
            flush(lq)

        st.pump(5)
        h_tiles(0)
        st.pump(6)
        ws4 = [st.next() for _ in range(4)]
        bs4 = [mainr.take() for _ in range(4)]
        for k in range(4):
            for i in (0, 1):
                mm3(bs4[i][1], ws4[i][1][:, k * 128:k * 128 + 128], ws4[i][2][:, k * 128:k * 128 + 128],
                    HH[:, k, :], HL[:, k, :], k == 0, False, ws4[i][3], h_toks[k])
        for k in range(4):
            for i in (2, 3):
                mm3(bs4[i][1], ws4[i][1][:, k * 128:k * 128 + 128], ws4[i][2][:, k * 128:k * 128 + 128],
                    HH[:, k, :], HL[:, k, :], k == 0, False, ws4[i][3], h_toks[k])
        st.pump(10)
        h_tiles(1)
        st.pump()
        for k in range(4, 8):
            for i in range(4):
                t = mm3(bs4[i][1], ws4[i][1][:, k * 128:k * 128 + 128], ws4[i][2][:, k * 128:k * 128 + 128],
                        HH[:, k, :], HL[:, k, :], False, k == 7, ws4[i][3], h_toks[k])
                ws4[i] += (t,)
        four = [(b, bk, w[-1]) for (b, bk, _), w in zip(bs4, ws4)]
        for w in ws4:
            st.done(w[0], w[-1])
        xt_free = h_toks[-1]

        ticks = []
        side = []

        def side_tick(n):
            for _ in range(n):
                if side:
                    try:
                        next(side[0])
                    except StopIteration:
                        side.pop(0)

        hold = [None]

        def tick():
            run_deferred()
            if st.chunks and not hold[0]:
                st.chunk()
            hold[0] = None
            if side:
                side_tick(1)
            if ticks:
                try:
                    hold[0] = next(ticks[0])
                except StopIteration:
                    ticks.pop(0)

        def block(bk, wh, wl, xh, xl, nk, wtoks, xtoks, bf, tk=(), first=True, last=True):
            t = None
            for k in range(nk):
                t = mm3(bk, wh(k), wl(k), xh(k), xl(k), first and k == 0, last and k == nk - 1,
                        wtoks, xtoks[k] if xtoks else None, bf)
                if k in tk:
                    tick()
            return t

        def wk(w, m=128, c0=0):
            return lambda k: w[:, c0 + k * m:c0 + k * m + m]

        def block1(xh_, xl_, nk, xtoks, tk=(), n=S, first=True, last=True, bnk=None):
            w, wh, wl, wt = st.next()
            b, bk, bf = bnk or mainr.take()
            t = block(bk[:, 0:n], wk(wh), wk(wl), xh_, xl_, nk, wt, xtoks, bf, tk, first, last)
            st.done(w, t)
            return b, bk, t

        def blocks3(xh_, xl_, xtoks, n=3, order=(0, 1, 2, 3, 4, 5, 6, 7)):
            ws = [st.next() for _ in range(n)]
            bs = [mainr.take() for _ in range(n)]
            t = [None] * n
            for k in order:
                for i in range(n):
                    (_, wh, wl, wt), (_, bk, bf) = ws[i], bs[i]
                    t[i] = mm3(bk, wk(wh)(k), wk(wl)(k), xh_(k), xl_(k), k == order[0], k == order[7], wt, xtoks[k], bf)
            for i in range(n):
                st.done(ws[i][0], t[i])
            return [(bs[i][0], bs[i][1], t[i]) for i in range(n)]

        hh = lambda k: HH[:, k, :]
        hl = lambda k: HL[:, k, :]

        MKv = MK[:, :].rearrange("p (l n) -> p l n", n=128)
        buf = {"AT": None, "KDT": None, "E0": None, "Q0": None, "SS": None}
        hfree = [dict(v=mk_t, k=mk_t), dict()]
        buf["Q0"] = n_toks[-1]
        oh_t = {}

        def zhead(h):
            p = h % 2
            Vb, Kb, Bb, Qb, Gb = (HB[:, 5 * p + i, :] for i in range(5))
            fr = hfree[p]
            r = {}
            TK = (1, 3, 5, 7)
            b, bk, t = four.pop(0) if four else block1(hh, hl, 8, None, TK)
            r["v"] = act(Vb, bk, ACTF.Copy, t, fr.get("v"))
            mainr.give(b, r["v"])
            b, bk, t = four.pop(0) if four else block1(hh, hl, 8, None, TK)
            xi, x, xf = xr.take()
            s_ = act(Kb, bk, ACTF.Sigmoid, t, fr.get("k"))
            mainr.give(b, s_)
            f_ = ts(V, Kb, Kb, OML[:, h:h + 1], LB[:, h:h + 1], MUL, ADD, s_, lb_t)
            l_ = act(x, Kb, ACTF.Ln, f_, xf)
            r["k"] = ts(V, Kb, Kb, -1.0, 1.0, MUL, ADD, l_)
            r["b"] = V(lambda e: e.tensor_tensor_scan(Bb, SM[:, :], x, 0.0, MUL, ADD), l_, m_dma, fr.get("b"))
            xr.give(xi, r["b"])
            b, bk, t = four.pop(0) if four else block1(hh, hl, 8, None, TK)
            r["q"] = act(Qb, bk, ACTF.Copy, t, fr.get("q"))
            mainr.give(b, r["q"])
            b, bk, t = four.pop(0) if four else block1(hh, hl, 8, None, TK)
            r["g"] = act(Gb, bk, ACTF.Silu, t, fr.get("g"))
            mainr.give(b, r["g"])
            return r

        def hgrn(h, r):
            p = h % 2
            Vb, Kb, Bb, Qb, Gb = (HB[:, 5 * p + i, :] for i in range(5))
            ats = G(lambda e: e.memset(AT[:, :], 0.0), buf["AT"])
            last_cp = [ats]
            pend = []

            def ew(l):
                half, blk = 1 << (l - 1), 1 << l
                Bv, Kv, Qv = (z.rearrange("p (n b) -> p n b", b=blk) for z in (Bb, Kb, Qb))
                xi, x, xf = xr.take()
                Xv = x.rearrange("p (n b) -> p n b", b=blk)
                ref = Bv[:, :, half - 1:half].broadcast_to([128, 512 // blk, half])
                g1 = tt(G, Xv[:, :, half:blk], Bv[:, :, half:blk], ref, SUB, r["b"], xf)
                g2 = tt(G, Xv[:, :, 0:half], ref, Bv[:, :, 0:half], SUB, r["b"], xf)
                a = act(x, x, ACTF.Exp, g1, g2)
                v1 = tt(V, Xv[:, :, half:blk], Xv[:, :, half:blk], Qv[:, :, half:blk], MUL, a, r["q"])
                v2 = tt(V, Xv[:, :, 0:half], Xv[:, :, 0:half], Kv[:, :, 0:half], MUL, a, r["k"])
                pend.append((l, xi, x, [v1, v2]))

            def sc(l, xi, x, toks):
                b, bk, bf = auxr.take()
                for j in range(4):
                    js = slice(j * 128, (j + 1) * 128)
                    lo = Kb[:, js] if l == 0 else x[:, js]
                    ro = Qb[:, js] if l == 0 else x[:, js]
                    t = mm(bk[:, js], lo, ro, True, True, toks, bf)
                if xi is not None:
                    xr.give(xi, t)
                half, blk = (0, 128) if l == 0 else (1 << (l - 1), 1 << l)
                o, d = (z.rearrange("p (j n b) -> p j n b", n=128 // blk, b=blk)[:, :, :, half:blk]
                        for z in (AT[:, :], bk))
                m = MKv[:, l, :].rearrange("p (j n b) -> p j n b", j=1, b=blk)[:, :, :, half:blk]\
                    .broadcast_to([128, 4, 128 // blk, blk - half])
                last_cp[0] = V(lambda e: e.copy_predicated(o, m, d), t, last_cp[0], mk_t)
                auxr.give(b, last_cp[0])
                return t

            ew(1)
            b, bk, bf = auxr.take()
            for j in range(4):
                js = slice(j * 128, (j + 1) * 128)
                t = tr(bk[:, js], Vb[:, js], IDN[:, :], r["v"], bf)
            v_t = act(Vb, bk, ACTF.Copy, t)
            auxr.give(b, v_t)
            yield
            ew(2)
            sc(0, None, None, [r["k"], r["q"]])
            yield
            for l in range(3, 7):
                ew(l)
                sc(*pend.pop(0))
                yield
            a = act(E0[:, :], Bb, ACTF.Exp, r["b"], buf["E0"])
            q0 = tt(V, Q0[:, :], E0[:, :], Qb, MUL, a, r["q"], buf["Q0"])
            e0_t = a
            sc(*pend.pop(0))
            xi, x, xf = xr.take()
            Bv = Bb.rearrange("p (n b) -> p n b", b=64)
            Xv = x.rearrange("p (n b) -> p n b", b=64)
            g = tt(G, Xv, Bv[:, :, 63:64].broadcast_to([128, 8, 64]), Bv, SUB, r["b"], xf)
            a = act(x, x, ACTF.Exp, g)
            kd = tt(V, x, x, Kb, MUL, a, r["k"])
            yield
            sc(*pend.pop(0))
            hfree[p]["b"] = [a, e0_t]
            hfree[p]["k"] = kd
            b, bk, bf = auxr.take()
            for j in range(4):
                js = slice(j * 128, (j + 1) * 128)
                t = tr(bk[:, js], x[:, js], IDN[:, :], kd, bf)
            xr.give(xi, t)
            hfree[p]["k"] = [kd, t]
            kt = act(KDT[:, :], bk, ACTF.Copy, t, buf["KDT"])
            auxr.give(b, kt)
            yield
            ob, obk, obf = auxr.take()
            for j in range(4):
                js = slice(j * 128, (j + 1) * 128)
                mm(obk[:, js], Vb[:, js], AT[:, js], j == 0, False, last_cp[0], v_t, obf, skip=True)
            prev = None
            kb_ = [auxr.take() for _ in range(2)]
            kt_ = [None, None]
            for c in range(7):
                rs = slice((c % 2) * 64, (c % 2) * 64 + 64)
                js = slice((c // 2) * 128, (c // 2) * 128 + 128)
                kt_[c % 2] = mm(kb_[c % 2][1][:, js], KDT[rs, js], Vb[rs, js], True, True, kt, v_t, kb_[c % 2][2])
            yield "hold"
            for c in range(7):
                kv = kb_[c % 2][1][:, (c // 2) * 128:(c // 2) * 128 + 128]
                if c == 0:
                    prev = cp(V, SS[:, 0, :], kv, kt_, buf["SS"])
                else:
                    prev = stt(SS[:, c, :], SS[:, c - 1, :], E0[:, 64 * c + 63:64 * c + 64], kv, MUL, ADD,
                               prev, e0_t)
            auxr.give(kb_[0][0], prev)
            auxr.give(kb_[1][0], prev)
            t = kt_
            yield "hold"
            yield "hold"
            yield
            buf["KDT"] = t
            buf["E0"] = [prev, q0]
            b, bk = ob, obk
            for c in range(1, 8):
                t = mm(bk[:, c * 64:c * 64 + 64], SS[:, c - 1, :], Q0[:, c * 64:c * 64 + 64], False, c == 7,
                       prev, q0, skip=True)
            buf["AT"] = buf["SS"] = buf["Q0"] = t
            hfree[p]["v"] = t
            hfree[p]["q"] = t
            xi, x, xf = xr.take()
            o = act(XT[:, h, :], bk, ACTF.Copy, t, xt_free)
            sq = act(x, bk, ACTF.Square, t, xf)
            auxr.give(b, sq)
            yield
            b, bk, t = stat_cols([x], 4, sq)
            xr.give(xi, t)
            si, sc_, sf = sct.take()
            v = ts(V, sc_[:, 0:4], bk[:, 0:4], 1.0 / 128, EPS1, MUL, ADD, t, sf)
            auxr.give(b, v)
            g = G(lambda e: e.tensor_tensor(sc_[:, 4:8], sc_[:, 0:4], NPOW[:, 0:4], ALU.pow), v, np_t)
            yield
            rb_, rbk, rt = diag_bcast(sc_[:, 4:8], 4, dgf[0], g)
            dgf[0] = rt
            sct.give(si, rt)
            yield
            v = stt(XT[:, h, :], XT[:, h, :], col("hgrn_norm_w"), rbk, MUL, MUL, rt, o)
            auxr.give(rb_, v)
            oh_t[h] = tt(G, XT[:, h, :], XT[:, h, :], Gb, MUL, v, r["g"])
            hfree[p]["g"] = oh_t[h]

        for h in range(8):
            while len(ticks) > 1:
                tick()
            r = zhead(h)
            ticks.append(hgrn(h, r))

        mix_t = {}
        while len(ticks) > 1:
            tick()
        GPS = [GP[:, :, :], HB[:, 0:2, :]]
        gp_free, d_free = [None, list(hfree[0].values())], [None]
        upf = [[], [], []]

        def mix_at(kk):
            if 2 <= kk < 10:
                return MPH[:, kk - 2, :], MPL[:, kk - 2, :]
            return HH[:, (kk - 10) % 16, :], HL[:, (kk - 10) % 16, :]

        def pool_u(g):
            dt_ = []
            for m in range(2):
                b, bk, t = block1(hh, hl, 8, None, (1, 3, 5, 7))
                u, s0, s1 = UP[0], UP[1], UP[2]
                a = act(u[:, 16:], bk, ACTF.Copy, t, upf[0])
                mainr.give(b, a)
                src, prev = u, a
                for i in range(g + 1):
                    d = 1 << i
                    dst = (s0, s1)[i % 2]
                    prev = tt(G, dst[:, 16:], src[:, 16:], src[:, 16 - d:528 - d], ADD, prev, pad_t, upf[1 + i % 2])
                    src = dst
                def tail(src=src, prev=prev, m=m, u=u):
                    wd = 2 << g
                    prev = tt(V, src[:, 16:16 + wd], src[:, 16:16 + wd], FAC[:, 16 * g:16 * g + wd], MUL, prev, m_dma)
                    prev = stt(src[:, 16:], src[:, 16:], 1.0 / wd, u[:, 16:], MUL, SUB, prev)
                    a = act(DH[:, m, :], src[:, 16:], ACTF.Copy, prev, d_free[0])
                    v = tt(V, DL[:, m, :], src[:, 16:], DH[:, m, :].bitcast(F32), SUB, a)
                    upf[:] = [[prev], [v], [v]]
                    dt_.append([a, v])

                defer(4 if g > 1 else 3, tail)
            return t, dt_

        def pool_mix(g, dt_, gp_t, last_z):
            for m in range(2):
                b, bk, t = block1(lambda k: DH[:, k, :], lambda k: DL[:, k, :], 2, dt_)
                assert len(dt_) == 2
                kk = 2 * g + m
                x = GPS[g % 2][:, m, :]
                v = stt(x, bk, col("pool_scale", kk), x, MUL, MUL, t, gp_t[m])
                mainr.give(b, v)
                mh_, ml_ = mix_at(kk)
                a = act(mh_, x, ACTF.Copy, v, last_z)
                v = tt(V, ml_, x, mh_.bitcast(F32), SUB, a, last_z)
                gp_free[g % 2] = v
                mix_t[kk] = [a, v]
            d_free[0] = t

        for h in range(2):
            mh_, ml_ = mix_at(8 + h)
            mix_t[8 + h] = split_later(mh_, ml_, XT[:, h, :], lq, oh_t[h])
        flush(lq)
        waiting = None
        for g in (3, 2, 1, 0):
            gp_t = []
            for m in range(2):
                b, bk, t = block1(hh, hl, 8, None, (1, 3, 5, 7))
                a = act(GPS[g % 2][:, m, :], bk, ACTF.Silu, t, gp_free[g % 2])
                mainr.give(b, a)
                gp_t.append(a)
            if waiting:
                pool_mix(*waiting, None)
            last_z, dt_ = pool_u(g)
            waiting = (g, dt_, gp_t)
        while ticks:
            tick()
        for h in range(2, 8):
            mh_, ml_ = mix_at(8 + h)
            mix_t[8 + h] = split_later(mh_, ml_, XT[:, h, :], lq, oh_t[h], last_z)
        flush(lq)
        XT2 = HB[:, 0:8, :]
        x2_t = [P.dma("sp", XT2[:, 4 * i:4 * i + 4, :], xsrc[:, 4 * i:4 * i + 4, :], s_x[2 + i], oh_t[6], oh_t[7], gp_free[1],
                      list(hfree[0].values()), list(hfree[1].values())) for i in range(2)]
        xt_free = [mix_t[8 + h] for h in range(8)]

        def acc_stats(src, m, s1, s2, sq, stt_, toks):
            a = act(sq[1], src, ACTF.Square, toks, sq[2])
            if m == 0:
                t2 = cp(G, s2, sq[1], a, stt_.get("free"))
                t1 = cp(G, s1, src, toks, stt_.get("free")) if s1 is not None else None
            else:
                t2 = tt(G, s2, s2, sq[1], ADD, a, stt_["s2"])
                t1 = tt(G, s1, s1, src, ADD, toks, stt_["s1"]) if s1 is not None else None
            stt_["s1"], stt_["s2"] = t1, t2
            return [a, t2]

        g1_t = tt(V, G1, M1[:, 16:24], col("norm_post_w", 0, 8), MUL, mod_t["1g"])
        SY, SG, SX, SD, SE = Q0[:, :], AT[:, :], E0[:, :], KDT[:, :], GP[:, 0, :]
        sfree_ = [buf[n] for n in ("Q0", "AT", "E0", "KDT")] + [list(gp_free)]
        gy_t, ch = [], {}
        for kk in range(8):
            bnk = mainr.take()
            block1(lambda k: MPH[:, k, :], lambda k: MPL[:, k, :], 8, [mix_t[k] for k in range(2, 10)], (1, 3, 5, 7),
                   last=False, bnk=bnk)
            if kk == 0:
                pool_mix(*waiting, last_z)
            b, bk, t = block1(hh, hl, 8, [mix_t[(10 + k) % 16] for k in range(8)], (1, 3, 5, 7), first=False, bnk=bnk)
            y_end = t
            gk = G1[:, kk:kk + 1]
            (i1, x1, f1), (i2, x2, f2), (i3, x3, f3) = \
                [xr.take() if kk else (None, s_, sfree_) for s_ in (SY, SD, SE)]
            a = act(XT[:, kk, :], bk, ACTF.Identity, t, xt_free, g1_t, scale=gk)
            sq = act(x1, bk, ACTF.Square, t, f1)
            se = act(x3, bk, ACTF.Square, t, f3, scale=gk)
            mainr.give(b, se)
            gy_t.append(a)
            xg = tt(V, x2, XT[:, kk, :], XT2[:, kk, :], MUL, a, x2_t, f2)
            if kk == 0:
                ch = {"y": sq, "d": xg, "e": se}
                continue
            if kk == 1:
                ch["g"] = tt(G, SG, XT[:, 0, :], XT[:, 1, :], ADD, a, gy_t, sfree_)
                ch["x"] = tt(G, SX, XT2[:, 0, :], XT2[:, 1, :], ADD, x2_t, sfree_)
            elif kk < 7:
                ch["g"] = tt(G, SG, SG, XT[:, kk, :], ADD, a, ch["g"])
            if kk > 1:
                ch["x"] = tt(G, SX, SX, XT2[:, kk, :], ADD, x2_t, ch["x"])
            if kk < 7:
                ch["y"] = tt(G, SY, SY, x1, ADD, sq, ch["y"])
                ch["d"] = tt(V, SD, SD, x2, ADD, xg, ch["d"])
                ch["e"] = tt(V, SE, SE, x3, ADD, se, ch["e"])
                for i, u in ((i1, ch["y"]), (i2, ch["d"]), (i3, ch["e"])):
                    xr.give(i, u)
        while st.chunks:
            st.chunk()
        run_deferred(True)
        b, bk, bf = auxr.take()
        first = True
        for a_, src, w_ in ((2, SX, ch["x"]), (0, SY, ch["y"]), (1, SG, ch["g"]), (3, SD, ch["d"]), (4, SE, ch["e"]),
                            (0, x1, sq), (1, XT[:, 7, :], a), (3, x2, xg), (4, x3, se)):
            for j in range(4):
                t = mm(bk[:, 4 * a_ + j:4 * a_ + j + 1], src[:, j * 128:(j + 1) * 128], ONES[:, 0:1], first, a_ == 4,
                       w_, bf, skip=True)
                first = False
        for i in (i1, i2, i3):
            xr.give(i, t)
        FS = newcols(44)
        vy, ry, mg, mx, md, me, ex, m_, rr, r2, r3 = (FS[:, 4 * i:4 * i + 4] for i in range(11))
        v1 = ts(V, vy, bk[:, 0:4], 1.0 / D, EPS1, MUL, ADD, t)
        v2 = ts(V, FS[:, 8:24], bk[:, 4:20], 1.0 / D, None, MUL, None, t)
        auxr.give(b, v2)
        g = G(lambda e: e.tensor_tensor(ry, vy, NPOW[:, 0:4], ALU.pow), v1, np_t)
        v = tt(V, m_, mg, ry, MUL, v2, g)
        v = tt(V, m_, m_, mx, ADD, v)
        u = tt(V, ex, me, ry, MUL, g)
        u = stt(ex, md, 2.0, ex, MUL, ADD, u)
        u = tt(V, ex, ex, ry, MUL, u)
        u = tt(V, ex, ex, BX, ADD, u)
        w_ = tt(V, vy, m_, m_, MUL, v)
        u = tt(V, ex, ex, vy, SUB, u, w_)
        g = G(lambda e: e.tensor_tensor(rr, ex, NPOW[:, 0:4], ALU.pow), u)
        b1, rb1, t1 = diag_bcast(rr, 4, dgf[0], g)
        v = tt(V, r2, ry, rr, MUL, g)
        b2, rb2, t2 = diag_bcast(r2, 4, buf["AT"], v, dg=SM[:, :])
        v = stt(r3, m_, -1.0, rr, MUL, MUL, g)
        b3, rb3, t3 = diag_bcast(r3, 4, None, v, t, dg=SG)
        dgf[0] = t1
        R1, R3 = SX, SD
        c1_ = act(R1, rb1, ACTF.Copy, t1, t)
        c3_ = act(R3, rb3, ACTF.Copy, t3, t)
        auxr.give(b1, c1_)
        auxr.give(b3, c3_)
        MH, ML = HH, HL
        SC1, SC2, SC1C = newcols(8), newcols(8), newcols(8)
        e1 = ts(V, SC1, M2[:, 8:16], 1.0, None, ADD, None, mod_t["2"])
        e2 = ts(V, SC2, M2[:, 32:40], 1.0, None, ADD, None, mod_t["2"])
        e3 = ts(V, SC1C, MC[:, 8:16], 1.0, None, ADD, None, mod_t["2"])
        PT = [PTA[:, 768 * i:768 * i + 768] for i in range(2)]
        xw = Ring([x[:, 0:512] for x in PT])
        xw.free = [flat(xr.free[0:3]) for _ in PT]
        xl_t, h2_t = [], []
        for k in range(8):
            u = tt(G, XT2[:, k, :], XT2[:, k, :], R1, MUL, c1_, ch["x"], t, x2_t, xg)
            if k % 2:
                u = tt(G, XT2[:, k, :], XT2[:, k, :], R3, ADD, c3_, u)
            v = tt(V, XL[:, k, :], XL[:, k, :], rb2, MUL, t2, gy_t[k], ch["g"], xg, t)
            if k % 2 == 0:
                v = tt(V, XL[:, k, :], XL[:, k, :], R3, ADD, c3_, v)
            v = tt(V, XL[:, k, :], XL[:, k, :], XT2[:, k, :], ADD, v, u)
            xl_t.append(v)
            si, x, sf = xw.take()
            v = act(x, XL[:, k, :], ACTF.Identity, v, e1, sf, bias=M2[:, k:k + 1], scale=SC1[:, k:k + 1])
            h2_t.append(split_later(MH[:, k, :], ML[:, k, :], x, lq, v, y_end))
            xw.give(si)
            xw.free[si] = h2_t[-1]
        flush(lq)
        v = xl_t[-1]
        auxr.give(b2, v)
        st_t = t3
        end1 = [v, t3, u]
        c1.close()
        assert not ticks

        c2 = ExitStack()
        CH = sb("CH", [128, 6, 512], F32R, c2)
        CL = sb("CL", [128, 6, 512], F32R, c2)
        QG = sb("QG", [128, 4, S], F32, c2)
        KG = sb("KG", [128, 4, NKEY], F32, c2)
        VG = sb("VG", [128, 6, 256], F32, c2)
        KR = sb("KR", [128, NKEY], F32, c2)
        VP = sb("VP", [128, 4, S + 30], F32, c2)
        CV = sb("CV", [128, 4, S], F32, c2)
        OTm = sb("OTm", [128, 4, 512], F32, c2)
        PM = [sb(f"PM{i}", [128, NKEY], F32, c2) for i in range(2)]
        CS = sb("CS", [128, NKEY], F32, c2)
        TMP = sb("TMP", [128, 1024], F32, c2)
        XC = KG[:, :, :].rearrange("p a n -> p (a n)")[:, 0:2048].rearrange("p (k n) -> p k n", n=NCTX)
        HCH = CH[:, 0:4, :].rearrange("p a n -> p (a n)").rearrange("p (k n) -> p k n", n=NCTX)
        HCL = CL[:, 0:4, :].rearrange("p a n -> p (a n)").rearrange("p (k n) -> p k n", n=NCTX)
        CQ = QG[:, 0:3, :]
        CKV = KG[:, 0:2, :]
        CKH, CKL = (z[:, 3:6, :].rearrange("p a n -> p (a n)").rearrange("p (k n) -> p k n", n=NKEY)
                    for z in (CH, CL))
        cs_t = P.dma("act", CS[:, :], consts[:, 704:704 + NKEY], s_msk, end1, st_t, *[xl_t])
        vp_t = [G(lambda e, a=a: e.memset(VP[:, :, a:a + 15], 0.0), end1, oh_t[7]) for a in (0, S + 15)]

        csrc = A["ctxT"].rearrange("(k p) t -> p k t", p=128)
        xc_t = P.dma("sp", XC, csrc, s_c, end1)

        def split(dh, dl, src, *w):
            a = act(dh, src, ACTF.Copy, w)
            return [a, tt(V, dl, src, dh.bitcast(F32), SUB, a, w)]

        hc_t = []

        def ctx_norm():
            CS1, CS2, CSQ = PM[0][:, 0:NCTX], PM[1][:, 0:NCTX], PM[0][:, NCTX:2 * NCTX]
            a = act(CS2, XC[:, 0, :], ACTF.Square, xc_t, end1)
            c2_ = a
            c1_ = cp(G, CS1, XC[:, 0, :], xc_t, end1)
            for k in range(1, 8):
                a = act(CSQ, XC[:, k, :], ACTF.Square, c2_)
                c2_ = tt(G, CS2, CS2, CSQ, ADD, a)
                c1_ = tt(G, CS1, CS1, XC[:, k, :], ADD, c1_)
                yield
                yield
            yield
            yield
            yield
            yield
            b, bk, t = stat_cols([CS1, CS2], 2, c1_, c2_)
            stc = newcols(8)
            v1 = ts(V, stc[:, 0:2], bk[:, 0:2], 1.0 / D, None, MUL, None, t)
            v2 = ts(V, stc[:, 2:4], bk[:, 4:6], 1.0 / D, EPS2, MUL, ADD, t)
            auxr.give(b, v2)
            v3 = tt(V, stc[:, 4:6], stc[:, 0:2], stc[:, 0:2], MUL, v1)
            v4 = tt(V, stc[:, 2:4], stc[:, 2:4], stc[:, 4:6], SUB, v2, v3)
            g = G(lambda e: e.tensor_tensor(stc[:, 4:6], stc[:, 2:4], NPOW[:, 0:2], ALU.pow), v4)
            v5 = stt(stc[:, 6:8], stc[:, 0:2], -1.0, stc[:, 4:6], MUL, MUL, g)
            yield
            yield
            yield
            yield
            b1, rb, t1 = diag_bcast(stc[:, 4:6], 2, dgf[0], g)
            yield
            b2, mb, t2 = diag_bcast(stc[:, 6:8], 2, t1, v5)
            dgf[0] = t2
            for k in range(8):
                x = XC[:, k, :]
                v = tt(V, x, x, rb[:, 0:NCTX], MUL, t1, xc_t, c1_, a)
                v = tt(V, x, x, mb[:, 0:NCTX], ADD, v, t2)
                vl = v
                v = ts(V, x, x, SC1C[:, k:k + 1], MC[:, k:k + 1], MUL, ADD, v, e3)
                hc_t.append(split(HCH[:, k, :], HCL[:, k, :], x, v, end1))
                yield
            auxr.give(b1, vl)
            auxr.give(b2, vl)

        ticks.append(ctx_norm())
        mh = lambda k: MH[:, k, :]
        ml = lambda k: ML[:, k, :]

        def drain(n=10 ** 6):
            while ticks and n:
                tick()
                n -= 1

        va_t, conv_t = [], {}

        def conv_side(j, tmp):
            v = act(CV[:, j, :], VP[:, j, 0:S], ACTF.Identity, va_t[j], vp_t,
                    bias=col("conv_dw_b_2", j), scale=col("conv_dw_w_2", j))
            for k in range(1, 31):
                xi, x, xf = tmp.take()
                a = act(x, VP[:, j, k:k + S], ACTF.Identity, xf, scale=col("conv_dw_w_2", 4 * k + j))
                v = tt(G, CV[:, j, :], CV[:, j, :], x, ADD, a, v)
                tmp.give(xi, v)
                yield
            conv_t[j] = v

        def conv(j):
            v = ts(V, CV[:, j, :], VP[:, j, 0:S], col("conv_dw_w_2", j), col("conv_dw_b_2", j), MUL, ADD, va_t[j], vp_t)
            for k in range(1, 31):
                v = stt(CV[:, j, :], VP[:, j, k:k + S], col("conv_dw_w_2", 4 * k + j), CV[:, j, :], MUL, ADD, v)
                yield
            conv_t[j] = v

        cn = {}

        def conv_norm():
            while len(conv_t) < 4:
                yield
            S1_, S2_, SQa, SQb = (VP[:, i, 0:512] for i in range(4))
            done = list(conv_t.values())
            c1_ = c2_ = None
            sqf = [None, None]
            for j in range(4):
                sq = (SQa, SQb)[j % 2]
                a = act(sq, CV[:, j, :], ACTF.Square, done, sqf[j % 2])
                if j == 0:
                    c1_ = cp(G, S1_, CV[:, j, :], done)
                    c2_ = cp(G, S2_, sq, a)
                else:
                    c1_ = tt(G, S1_, S1_, CV[:, j, :], ADD, c1_)
                    c2_ = tt(G, S2_, S2_, sq, ADD, a, c2_)
                sqf[j % 2] = c2_
                yield
                yield
            auxr.even()
            b, bk, bf = auxr.take()
            for a_, acc, w_ in ((0, S1_, c1_), (1, S2_, c2_)):
                for j in range(4):
                    t = mm(bk[:, 4 * a_ + j:4 * a_ + j + 1], acc[:, j * 128:(j + 1) * 128], ONES[:, 0:1], True, True,
                           w_, bf)
            stc = newcols(16)
            m, v, r, q = (stc[:, 4 * i:4 * i + 4] for i in range(4))
            a1 = ts(V, m, bk[:, 0:4], 1.0 / 512, None, MUL, None, t)
            a2 = ts(V, v, bk[:, 4:8], 1.0 / 512, EPS2, MUL, ADD, t)
            auxr.give(b, a2)
            auxr.even()
            a3 = tt(V, q, m, m, MUL, a1)
            a4 = tt(V, v, v, q, SUB, a3, a2)
            g = tt(G, r, v, NPOW[:, 0:4], ALU.pow, a4, np_t)
            yield
            yield
            yield
            yield
            b1, bk1, t1 = diag_bcast(r, 4, dgf[0], g)
            a5 = stt(q, m, -1.0, r, MUL, MUL, g)
            b2, bk2, t2 = diag_bcast(q, 4, c2_, a5, dg=SQa)
            dgf[0] = t1
            r1 = act(S1_, bk1, ACTF.Copy, t1, t)
            r2 = act(S2_, bk2, ACTF.Copy, t2, t)
            auxr.give(b1, r1)
            auxr.give(b2, r2)
            yield
            cn["t"] = []
            for j in range(4):
                x = CV[:, j, :]
                v_ = tt(V, x, x, S1_, MUL, r1, c1_, a)
                yield
                cn["t"].append(tt(V, x, x, S2_, ADD, r2, v_))
                yield
            cn["done"] = t2

        TK8 = (0, 1, 2, 3, 4, 5, 6, 7)
        three = blocks3(mh, ml, h2_t)
        for j in range(4):
            b, bk, t = three.pop(0) if three else block1(mh, ml, 8, h2_t, TK8 if len(hc_t) < 8 else (1, 4, 7))
            b2, bk2, t2 = three.pop(0) if three else block1(mh, ml, 8, h2_t, TK8 if len(hc_t) < 8 else (1, 4, 7))
            a = act(VP[:, j, 15:15 + S], bk2, ACTF.Sigmoid, t2, end1)
            mainr.give(b2, a)
            v = tt(V, VP[:, j, 15:15 + S], VP[:, j, 15:15 + S], bk, MUL, a, t)
            mainr.give(b, v)
            va_t.append(v)
            if j < 2:
                ticks.append(conv(j))

        while len(hc_t) < 8:
            tick()
        tmp = Ring([TMP[:, 512 * i:512 * i + 512] for i in range(2)])
        tmp.free = [[end1] for _ in range(2)]
        side += [conv_side(2, tmp), conv_side(3, tmp), conv_norm()]
        x_free = [hc_t[-1]]
        cq_t, ckv_t = [], []
        norms = {"q": [], "kv": []}
        sfree = [[hc_t[-1], dgf[0]]]

        def rms_small(src, nb, cols, n, toks, name, dst):
            chn = None
            SAv, SQv = PM[1][:, 0:cols], PM[0][:, 0:cols]
            for m in range(nb):
                if m == 0:
                    chn = act(SAv, src[:, m, :], ACTF.Square, toks[m], sfree[0])
                else:
                    a = act(SQv, src[:, m, :], ACTF.Square, toks[m], sfree[0], chn if m > 1 else None)
                    chn = tt(V, SAv, SAv, SQv, ADD, a, chn)
            yield
            yield
            res = []
            for at in range(0, cols, 512):
                k = min(4, (cols - at) // 128)
                b, bk, t = stat_cols([SAv[:, at:at + k * 128]], k, chn)
                stt_ = t
                si, sc, sf = sct.take()
                v = ts(V, sc[:, 0:k], bk[:, 0:k], 1.0 / n, EPS2, MUL, ADD, t, sf)
                auxr.give(b, v)
                g = tt(G, sc[:, 4:4 + k], sc[:, 0:k], NPOW[:, 0:k], ALU.pow, v, np_t)
                yield
                yield
                yield
                b, bk, t = diag_bcast(sc[:, 4:4 + k], k, dgf[0], g)
                dgf[0] = t
                sct.give(si, t)
                yield
                for m in range(nb):
                    cs = slice(at, at + k * 128)
                    v = stt(src[:, m, cs], src[:, m, cs], col(name, m), bk[:, 0:k * 128], MUL, MUL, t, toks[m])
                auxr.give(b, v)
                res.append(v)
                yield
            sfree[0] = [stt_, chn]
            dst += res
        hch, hcl = (lambda k: HCH[:, k, :]), (lambda k: HCL[:, k, :])

        def ctxb(w):
            b, bk, bf = mainr.take()
            t = block(bk[:, 0:NCTX], wk(w[1]), wk(w[2]), hch, hcl, 8, w[3], hc_t, bf, (3, 7))
            return b, bk[:, 0:NCTX], t

        def both(w):
            b, bk, bf = mainr.take()
            t = block(bk, wk(w[1]), wk(w[2]), mh, ml, 8, w[3], h2_t, bf, (1, 3, 5, 7))
            yield b, bk, t
            yield ctxb(w)

        for m in range(3):
            b, bk, t = block1(mh, ml, 8, h2_t, (1, 4, 7))
            a = act(CQ[:, m, :], bk, ACTF.Copy, t, end1)
            mainr.give(b, a)
            cq_t.append(a)
        ticks.insert(0, rms_small(CQ, 3, S, 384, cq_t, "q_norm_g_2", norms["q"]))
        for m in range(2):
            w = st.next()
            ts_ = []
            for (b, bk, t), cs in zip(both(w), (slice(NCTX, NKEY), slice(0, NCTX))):
                a = act(CKV[:, m, cs], bk, ACTF.Copy, t, x_free)
                mainr.give(b, a)
                ts_.append(a)
            st.done(w[0], t)
            ckv_t.append(ts_)
        while not norms["q"]:
            tick()
        ticks.insert(0, rms_small(CKV, 2, NKEY, 256, ckv_t, "kv_norm_g_2", norms["kv"]))
        kr_t = []
        w = st.next()
        for (b, bk, t), cs in zip(both(w), (slice(NCTX, NKEY), slice(0, NCTX))):
            si, x, sf = xw.take()
            n = cs.stop - cs.start
            v1 = tt(V, x[64:96, 0:n], bk[96:128, 0:n], CS[96:128, cs], MUL, t, cs_t, sf)
            v2 = tt(V, KR[64:96, cs], bk[64:96, 0:n], CS[64:96, cs], MUL, t, cs_t)
            mainr.give(b, v2)
            v = tt(V, KR[64:96, cs], KR[64:96, cs], x[64:96, 0:n], ADD, v1, v2)
            xw.give(si, v)
            kr_t.append(v)
        st.done(w[0], t)
        h2_free = t

        def halves(src, nb, cols, vt, dh, dl):
            return [[split(dh[:, m, a:b], dl[:, m, a:b], src[:, m, a:b], v, h2_free) for m in range(nb)]
                    for (a, b), v in zip(cols, vt)]

        while ticks and not norms["kv"]:
            tick()
        cqn_k = halves(CQ, 3, [(0, S)], norms["q"], CH[:, 0:3, :], CL[:, 0:3, :])[0]
        cqn = cqn_k
        ckn = halves(CKV, 2, [(0, 512), (512, NKEY)], norms["kv"], CKH, CKL)

        pmr = Ring([x[:, :] for x in PM])
        ptr = Ring([x[:, :] for x in PT])
        pmr.free = [list(sfree[0]), list(sfree[0])]
        ptr.free = [list(flat(xw.free[0])), list(flat(xw.free[1]))]
        NM = newcols(12)
        nmr = Ring([NM[:, 3 * i:3 * i + 3] for i in range(4)])
        qg_free, kg_free, vg_free = [cqn, None], [ckn, None], [None]
        o_t = []
        CT = 2
        mo_t, cm_t = [], []

        def attn_out(f):
            b, bk, bf = mainr.take()
            for j in range(4):
                t = tr(bk[:, j * 128:(j + 1) * 128], OTm[:, j, f * 128:(f + 1) * 128], IDN[:, :], o_t[-1], o_t, bf)
            a = act(MH[:, 4 + f, :], bk, ACTF.Copy, t, h2_free)
            v = tt(V, ML[:, 4 + f, :], bk, MH[:, 4 + f, :].bitcast(F32), SUB, a)
            mainr.give(b, v)
            mo_t.append([a, v, t])

        for g in range(2):
            q_t = []
            for h in range(4):
                b, bk, t = block1(lambda k: CH[:, k, :], lambda k: CL[:, k, :], 3, cqn_k, (0,))
                a = act(QG[0:64, h, :], bk[0:64, :], ACTF.Copy, t, qg_free)
                si, x, sf = ptr.take()
                v1 = tt(V, x[64:96, 0:S], bk[96:128, :], CS[96:128, NCTX:NKEY], MUL, t, sf)
                v2 = tt(V, QG[64:96, h, :], bk[64:96, :], CS[64:96, NCTX:NKEY], MUL, t, qg_free)
                mainr.give(b, a, v2)
                v = tt(V, QG[64:96, h, :], QG[64:96, h, :], x[64:96, 0:S], ADD, v1, v2)
                ptr.give(si, v)
                q_t.append([a, v])
            if g:
                attn_out(0)
                attn_out(1)
            k_t = [[] for _ in range(4)]
            for h in range(4):
                if h % 2:
                    k_t[h].append(cp(V, KG[64:96, h, :], KR[64:96, :], kr_t, kg_free))
                else:
                    k_t[h].append(act(KG[64:96, h, :], KR[64:96, :], ACTF.Copy, kr_t, kg_free))
            for pr in range(2):
                w, wh, wl, wt = st.next()
                for cs in (slice(NCTX, NKEY), slice(0, NCTX)):
                    n = cs.stop - cs.start
                    b, bk, bf = mainr.take()
                    t = block(bk[:, 0:n], wk(wh), wk(wl), lambda k: CKH[:, k, cs], lambda k: CKL[:, k, cs], 2,
                              [wt, ckn], None, bf, (0,))
                    for i in range(2):
                        a = act(KG[0:64, 2 * pr + i, cs], bk[64 * i:64 * i + 64, 0:n], ACTF.Copy, t, kg_free)
                        k_t[2 * pr + i].append(a)
                    mainr.give(b, a)
                st.done(w, t)
            v_t = []
            w, wh, wl, wt = st.next()
            for t6 in range(6):
                b, bk, bf = mainr.take()
                ks = slice(t6 * 128, t6 * 128 + 128)
                t = block(bk[:, 0:256], lambda k: CKH[:, k, ks], lambda k: CKL[:, k, ks],
                          wk(wh, 256), wk(wl, 256), 2, [wt, ckn], None, bf)
                a = act(VG[:, t6, :], bk[:, 0:256], ACTF.Copy, t, vg_free)
                mainr.give(b, a)
                v_t.append(a)
            st.done(w, t)
            c_free = t

            seq = [(h, j) for h in range(4) for j in range(4)]
            stage = {}

            def scores(i):
                h, j = seq[i]
                i0, _, f0 = auxr.take()
                i1, _, f1 = auxr.take()
                bp = PB[2 + i0 // 2]
                assert i0 % 2 == 0
                js = slice(j * 128, (j + 1) * 128)
                mm(bp[:, 0:512], QG[0:96, h, js], KG[0:96, h, 0:512], True, True, q_t[h], k_t[h], f0, f1)
                t = mm(bp[:, 512:768], QG[0:96, h, js], KG[0:96, h, 512:768], True, True)
                ni, nm, nf = nmr.take()
                v = V(lambda e: e.tensor_reduce(nm[:, 0:1], bp[:, 0:NKEY], AX.X, ALU.max, negate=True), t, nf)
                v = ts(V, nm[:, 0:1], nm[:, 0:1], SCALE, None, MUL, None, v)
                pi, pm, pf = pmr.take()
                a = act(pm, bp[:, 0:NKEY], ACTF.Exp, v, pf, bias=nm[:, 0:1], scale=SCALE, acc=nm[:, 1:2])
                auxr.give(i0, a)
                auxr.give(i1, a)
                v = V(lambda e: e.reciprocal(nm[:, 2:3], nm[:, 1:2]), a)
                stage[i] = [t, pi, pm, a, ni, nm, v]

            def turn(i):
                t, pi, pm, a, ni, nm, v = stage[i]
                f0, f1 = tfree[0]
                mp = PB[0]
                for k in range(6):
                    t = tr(mp[:, k * 128:(k + 1) * 128], pm[:, k * 128:(k + 1) * 128], IDN[:, :], a, f0, f1)
                pmr.give(pi, t)
                qi, pt, qf = ptr.take()
                c = act(pt[:, 0:512], mp[:, 0:512], ACTF.Copy, t, qf)
                c2_ = cp(V, pt[:, 512:768], mp[:, 512:768], t, qf)
                tfree[0] = [c, c2_]
                stage[i] += [qi, pt, [c, c2_]]

            def values(i):
                h, j = seq[i]
                ni, nm, v, qi, pt, ct = stage[i][4:]
                bk = bank[2 + i % 2][:, 0:64]
                f0, f1 = ofree[i % 2], None
                for k in range(6):
                    t = mm(bk, pt[:, k * 128:(k + 1) * 128], VG[:, k, h * 64:h * 64 + 64], k == 0, k == 5, ct, v_t, f0, f1)
                ptr.give(qi, t)
                hg = 4 * g + h
                v = ts(V, OTm[:, j, hg * 64:hg * 64 + 64], bk, nm[:, 2:3], None, MUL, None, t, v)
                ofree[i % 2] = v
                nmr.give(ni, v)
                o_t.append(v)
                return t

            auxr.even()
            mainr.even()
            mb_ = [mainr.take() for _ in range(4)]
            mb_.sort(key=lambda z: z[0])
            tfree, ofree = [[mb_[0][2], mb_[1][2]]], [mb_[2][2], mb_[3][2]]
            scores(0)
            for i in range(17):
                if i + 1 < 16:
                    scores(i + 1)
                if i < 16:
                    turn(i)
                if i:
                    t = values(i - 1)
                for _ in range(CT):
                    if ticks:
                        tick()
                side_tick(1)
            for i, f in enumerate((tfree[0][0], tfree[0][1], ofree[0], ofree[1])):
                mainr.give(i, f)
            qg_free, kg_free, vg_free = [t], [t], [t]

        attn_out(2)
        attn_out(3)
        ot_free = mo_t[-1][2]
        while ticks:
            tick()
        side_tick(100)
        for j in range(4):
            x = CV[:, j, :]
            a = act(x, x, ACTF.Silu, cn["t"][j], bias=col("conv_ln_b_2", j), scale=col("conv_ln_g_2", j))
            cm_t.append(split_later(MH[:, j, :], ML[:, j, :], x, lq, a, h2_free))
        flush(lq)
        m_t = cm_t + [z[0:2] for z in mo_t]

        def residual(bk, k, bias, gate, t, *w):
            si, x, sf = wr.take()
            v = ts(V, x, bk, bias, gate, ADD, MUL, t, sf)
            v2 = stt(XL[:, k, :], XL[:, k, :], ALPHA, x, MUL, ADD, v, w)
            wr.give(si, v2)
            return v, v2

        def stats_of(k, toks, s1, s2, chain):
            si, x, sf = wr.take()
            if k == 7:
                a = act(x, XL[:, k, :], ACTF.Square, toks, sf)
                chain["last"] = (XL[:, k, :], x, [toks, a])
                return
            u = acc_stats(XL[:, k, :], k, s1, s2, (si, x, sf), chain, toks)
            wr.give(si, u)

        wr = Ring([OTm[:, i, :] for i in range(4)])
        wr.free = [[ot_free] for _ in range(4)]
        S1, S2 = CV[:, 0, :], CV[:, 1, :]
        chain = {"free": [m_t[0], m_t[1]]}
        r_t = []
        three = blocks3(mh, ml, m_t, order=(4, 5, 6, 7, 0, 1, 2, 3))
        for kk in range(8):
            b, bk, t = three.pop(0) if three else block1(mh, ml, 8, m_t)
            v, v2 = residual(bk, kk, col("b_o_2", kk), M2[:, 16 + kk:17 + kk], t, h2_t[kk])
            mainr.give(b, v)
            r_t.append(v2)
            stats_of(kk, v2, S1, S2, chain)
        mo_free = t
        (b1, rb, t1), (b2, mb, t2), st1 = ln_bcast(S1, S2, 4, D, EPS2, chain["s1"], chain["s2"], last=chain["last"],
                                                   dg=CV[:, 2, :], dgf2=m_t[2])
        A2, B2 = newcols(8), newcols(8)
        v = tt(V, A2, SC2, col("ln1_g_2", 0, 8), MUL, e2)
        v_ = tt(V, B2, SC2, col("ln1_b_2", 0, 8), MUL, e2)
        v_ = tt(V, B2, B2, M2[:, 24:32], ADD, v_)
        wr.free = [f if f is not None else [st1] for f in wr.free]
        h3_t, xm_t = [], []
        for k in range(8):
            x = XL[:, k, :]
            v1 = tt(V, x, x, rb, MUL, t1, chain["s1"], chain["s2"], r_t[k], st1)
            v1 = tt(V, x, x, mb, ADD, v1, t2)
            si, y, sf = wr.take()
            v2 = act(y, x, ACTF.Identity, v1, v, v_, sf, bias=B2[:, k:k + 1], scale=A2[:, k:k + 1])
            h3_t.append(split_later(MH[:, k, :], ML[:, k, :], y, lq, v2, mo_free))
            wr.give(si)
            wr.free[si] = h3_t[-1]
            xm_t.append(ts(G, x, x, col("ln1_g_2", k), col("ln1_b_2", k), MUL, ADD, v1, v2))
        flush(lq)
        auxr.give(b1, v1)
        auxr.give(b2, v1)
        end2 = [h3_t[-1], st1, t2]
        c2.close()

        c3 = ExitStack()
        AH = sb("AH", [128, 22, S], F32R, c3)
        AL = sb("AL", [128, 22, S], F32R, c3)
        YG = [PTA[:, 512 * i:512 * i + 512] for i in range(3)] + [sb("YG3", [128, S], F32, c3)[:, :]]
        ygr = Ring([y[:, :] for y in YG])

        def tap(i, blk_):
            return col("ffn_dw_w_2", 44 * i + blk_)

        a_t = []
        three = blocks3(mh, ml, h3_t)
        for j in range(22):
            ys = []
            for m in range(2):
                b, bk, t = three.pop(0) if three else block1(mh, ml, 8, h3_t)
                blk_ = 22 * m + j
                yi, y, yf = ygr.take()
                a = act(y, bk, ACTF.Identity, t, yf, end2, bias=col("ffn_dw_b_2", blk_), scale=tap(1, blk_))
                v = stt(y[:, 1:S], bk[:, 0:S - 1], tap(0, blk_), y[:, 1:S], MUL, ADD, a)
                v = stt(y[:, 0:S - 1], bk[:, 1:S], tap(2, blk_), y[:, 0:S - 1], MUL, ADD, v)
                mainr.give(b, v)
                ys.append((yi, y, v))
            (gi, yg, gt), (vi, yv, vt) = ys
            a = act(yg, yg, ACTF.Silu, gt)
            v = tt(V, yg, yg, yv, MUL, a, vt)
            s_ = split(AH[:, j, :], AL[:, j, :], yg, v, end2)
            ygr.give(gi, s_)
            ygr.give(vi, v)
            a_t.append(s_)
        up_end = t
        S1, S2 = YG[2][:, :], YG[3][:, :]
        wr = Ring([YG[0][:, :], YG[1][:, :]])
        wr.free = [[s_, v], [s_, v]]
        chain = {"free": [s_, v]}
        r_t = []
        for cpair in range(4):
            bs = [mainr.take() for _ in range(2)]
            for q, (r0, nk) in enumerate(((0, 8), (8, 7), (15, 7))):
                for m in range(2):
                    kk = 2 * cpair + m
                    b, bk, t = block1(lambda k: AH[:, r0 + k, :], lambda k: AL[:, r0 + k, :], nk,
                                      [a_t[r0 + k] for k in range(nk)], first=q == 0, last=q == 2, bnk=bs[m])
                    if q == 2:
                        v, v2 = residual(bk, kk, col("b_down_2", kk), M2[:, 40 + kk:41 + kk], t, xm_t[kk])
                        mainr.give(b, v)
                        r_t.append(v2)
                        stats_of(kk, v2, S1, S2, chain)
        (b1, rb, t1), (b2, mb, t2), st1 = ln_bcast(S1, S2, 4, D, EPS2, chain["s1"], chain["s2"], last=chain["last"],
                                                   dg=RAW[0][:, 0:512], dgf2=st.rfree)
        f_t = []
        for k in range(8):
            x = XL[:, k, :]
            v1 = tt(V, x, x, rb, MUL, t1, chain["s1"], chain["s2"], r_t[k], st1)
            v1 = tt(V, x, x, mb, ADD, v1, t2)
            f = act(x, x, ACTF.Identity, v1, bias=col("ln2_b_2", k), scale=col("ln2_g_2", k))
            f_t.append(P.dma("sp", out[k * 128:(k + 1) * 128, :], x, s_out, f))
        P.q["sp"].append([[f_t[-1]], None, None])
        c3.close()
        run_blocks(nc, ctx, P)


def run_blocks(nc, ctx, P):
    P.number()
    blk = ctx.enter_context(nc.Block())

    @blk.sync
    def _(e):
        P.emit("sp", e)

    @blk.gpsimd
    def _(e):
        P.emit("pool", e)

    @blk.scalar
    def _(e):
        P.emit("act", e)

    @blk.tensor
    def _(e):
        P.emit("pe", e)

    @blk.vector
    def _(e):
        P.emit("dve", e)


def shape_constants():
    f = np.float32
    con = np.zeros((128, 704 + 768), f)
    con[:, 0:128] = np.eye(128, dtype=f)
    con[:, 128:640] = (np.arange(512) % 64 != 0).astype(f)
    for g in range(4):
        w = 2 << g
        con[:, 640 + 16 * g:640 + 16 * g + w] = f(w) / np.arange(1, w + 1, dtype=f)
    tok = np.arange(S)
    inv = (f(10000.0) ** (-np.arange(8, dtype=f) / f(8))).astype(f)
    ang = np.concatenate([(tok // 64).astype(f)[:, None] * inv, (tok % 64).astype(f)[:, None] * inv], -1).astype(f)
    co, si = np.cos(ang).T.astype(f), np.sin(ang).T.astype(f)
    con[64:96, 704:960] = 1.0
    con[64:96, 960:1472] = np.concatenate([co, co])
    con[96:128, 960:1472] = np.concatenate([-si, si])
    s_, t_ = np.arange(128)[:, None], np.arange(128)[None, :]
    mk = np.zeros((128, 7, 128), f)
    mk[:, 0] = s_ == t_
    for lv in range(1, 7):
        h, b = 1 << (lv - 1), 1 << lv
        mk[:, lv] = ((s_ // b == t_ // b) & (s_ % b < h) & (t_ % b >= h))
    return con, mk.reshape(128, 7 * 128)


def host_layout(np, inputs):
    cols = []
    for name, n in PARAMS:
        a = np.ascontiguousarray(inputs[name]).reshape(n, 128)
        cols.append(a.T)
    parts = []
    for it in stream_layout():
        blocks = it[1] if it[0] == "w" else [it[1]]
        views = []
        for name, at, r0, nk, sets in blocks:
            a = np.asarray(inputs[name])
            a = a[at[0]][at[1]] if isinstance(at, tuple) else a[at]
            rows = a[r0 * 128:(r0 + nk) * 128]
            if r0 + nk > a.shape[0] // 128:
                rows = np.concatenate([rows, a[:(r0 + nk) * 128 - a.shape[0]]], axis=0)
            b = np.concatenate([rows[:, c:c + n] for c, n in sets], axis=1)
            views.append(b.reshape(nk, 128, -1).transpose(1, 0, 2).reshape(128, -1))
        parts.append(np.concatenate(views, axis=1).reshape(-1))
    return {
        "params": np.concatenate(cols, axis=1),
        "xT": np.asarray(inputs["x"])[0].T,
        "ctxT": np.asarray(inputs["ctx_2"])[0].T,
        "wstream": np.concatenate(parts),
    }


def kernel(**inputs):
    import numpy as _np
    import concourse.bacc as _bacc
    from concourse import mybir as _mybir
    from concourse.bass_utils import run_bass_kernel_spmd as _run

    nc = _bacc.Bacc("TRN2", target_bir_lowering=False, num_devices=1)
    arrays, args = {}, {}
    con, mk = shape_constants()
    packed = host_layout(_np, inputs)
    for name, a in list(packed.items()) + [("consts", con), ("masks", mk)]:
        a = _np.ascontiguousarray(a)
        arrays[f"in_{name}"] = a
        args[name] = nc.dram_tensor(f"in_{name}", a.shape, _mybir.dt.from_np(a.dtype), kind="ExternalInput").ap()
    out = nc.dram_tensor("out_0", (D, S), _mybir.dt.float32, kind="ExternalOutput").ap()
    build(nc, args, out, args.pop("consts"), args.pop("masks"))
    r = _run(nc, [arrays], core_ids=[0])
    return _np.ascontiguousarray(r.results[0]["out_0"].T).reshape(1, S, D)
```
